# Optimizing a Trainium2 kernel written in Bass

```python
import math
import jax, jax.numpy as jnp
from jax import lax
import numpy as np

D_MODEL = 1024
BATCH = 1
SEQ = 256
DEPTH = 1

N_META = 16
S5_WIDTH = D_MODEL // 2
S5_GROUP = 16
S5_GROUPS = S5_WIDTH // S5_GROUP
S5_STATE = 64
DT_MIN = 1e-3
DT_MAX = 1e-1
M_HEADS = 4
M_DK = D_MODEL // 8
M_DV = D_MODEL // 4
M_QK_WIDTH = M_HEADS * M_DK
M_V_WIDTH = M_HEADS * M_DV
M_CHUNK = 64
CONV_WIDTH = 4
D_FF = 4 * D_MODEL
ALPHA = (2.0 * DEPTH) ** 0.25
BETA = (8.0 * DEPTH) ** -0.25
LN_EPS = 1e-5
IN_SIZES = (S5_WIDTH, M_QK_WIDTH, M_QK_WIDTH, M_V_WIDTH, M_V_WIDTH, M_HEADS, M_HEADS, D_MODEL, D_MODEL)
IN_WIDTH = sum(IN_SIZES)
F_GATE_OFFSET = S5_WIDTH + 2 * M_QK_WIDTH + 2 * M_V_WIDTH + M_HEADS


def _layer_norm(x, g, b):
    xf = x.astype(jnp.float32)
    mu = jnp.mean(xf, axis=-1, keepdims=True)
    var = jnp.mean(jnp.square(xf - mu), axis=-1, keepdims=True)
    y = (xf - mu) * lax.rsqrt(var + LN_EPS)
    return (y * g.astype(jnp.float32) + b.astype(jnp.float32)).astype(x.dtype)

def _head_norm(h, g):
    hf = h.astype(jnp.float32)
    mu = jnp.mean(hf, axis=-1, keepdims=True)
    var = jnp.mean(jnp.square(hf - mu), axis=-1, keepdims=True)
    return (hf - mu) * lax.rsqrt(var + LN_EPS) * g.astype(jnp.float32).reshape(M_HEADS, M_DV)

def _split_columns(p):
    parts, start = [], 0
    for size in IN_SIZES:
        parts.append(p[..., start:start + size])
        start += size
    return parts

def _causal_depthwise_conv(x, w, b):
    c = x.shape[-1]
    y = lax.conv_general_dilated(
        x, w[:, None, :].astype(x.dtype), window_strides=(1,),
        padding=((CONV_WIDTH - 1, 0),), dimension_numbers=("NWC", "WIO", "NWC"),
        feature_group_count=c)
    return y + b

def _linear_recurrence_combine(left, right):
    a_l, b_l = left
    a_r, b_r = right
    return a_l * a_r, a_r * b_l + b_r

def _s5_mixer(u, lam_re, lam_im, log_dt, b_re, b_im, c_re, c_im, d_skip):
    f32 = jnp.float32
    bsz, length, _ = u.shape
    uf = u.astype(f32).reshape(bsz, length, S5_GROUPS, S5_GROUP)
    lam = lax.complex(lam_re.astype(f32), lam_im.astype(f32))
    dt = jnp.exp(log_dt.astype(f32))[:, None]
    lam_bar = jnp.exp(lam * dt)
    b_mat = lax.complex(b_re.astype(f32), b_im.astype(f32))
    b_bar = ((lam_bar - 1.0) / lam)[..., None] * b_mat
    bu = jnp.einsum("gph,blgh->blgp", b_bar, uf.astype(jnp.complex64))
    a = jnp.broadcast_to(lam_bar, (1, length, S5_GROUPS, S5_STATE))
    _, state = lax.associative_scan(_linear_recurrence_combine, (a, bu), axis=1)
    c_mat = lax.complex(c_re.astype(f32), c_im.astype(f32))
    y = jnp.real(jnp.einsum("ghp,blgp->blgh", c_mat, state))
    y = y + d_skip.astype(f32).reshape(S5_GROUPS, S5_GROUP) * uf
    return y.reshape(bsz, length, S5_WIDTH)

def _mlstm_mixer(q, k, v, i_pre, f_pre):
    f32 = jnp.float32
    bsz, length = q.shape[:2]
    n_pad = M_CHUNK - N_META
    n_chunks = (length + n_pad) // M_CHUNK

    def to_chunks(t, fill):
        t = t.astype(f32)
        t = jnp.pad(t, ((0, 0), (n_pad, 0)) + ((0, 0),) * (t.ndim - 2), constant_values=fill)
        t = t.reshape((bsz, n_chunks, M_CHUNK) + t.shape[2:])
        return jnp.moveaxis(t, (1, 3), (0, 2))

    qc = to_chunks(q, 0.0)
    kc = to_chunks(k * (M_DK ** -0.5), 0.0)
    vc = to_chunks(v, 0.0)
    log_i = to_chunks(i_pre, -jnp.inf)
    log_f = to_chunks(jax.nn.log_sigmoid(f_pre.astype(f32)), 0.0)
    causal = jnp.tril(jnp.ones((M_CHUNK, M_CHUNK), dtype=bool))

    def chunk_step(carry, inp):
        c_st, n_st, m_st = carry
        q_c, k_c, v_c, li_c, lf_c = inp
        b = jnp.cumsum(lf_c, axis=-1)
        d_mat = jnp.where(causal, b[..., :, None] - b[..., None, :] + li_c[..., None, :], -jnp.inf)
        m_inter = b + m_st[..., None]
        m_row = jnp.maximum(m_inter, jnp.max(d_mat, axis=-1))
        w_intra = jnp.exp(d_mat - m_row[..., None])
        w_inter = jnp.exp(m_inter - m_row)
        s = jnp.einsum("bhsd,bhjd->bhsj", q_c, k_c) * w_intra
        num = (jnp.einsum("bhsj,bhje->bhse", s, v_c)
               + w_inter[..., None] * jnp.einsum("bhsd,bhde->bhse", q_c, c_st))
        den = jnp.sum(s, axis=-1) + w_inter * jnp.einsum("bhsd,bhd->bhs", q_c, n_st)
        h_c = num / jnp.maximum(jnp.abs(den), jnp.exp(-m_row))[..., None]
        b_last = b[..., -1]
        g_log = b_last[..., None] - b + li_c
        m_new = jnp.maximum(b_last + m_st, jnp.max(g_log, axis=-1))
        w_k = jnp.exp(g_log - m_new[..., None])
        decay = jnp.exp(b_last + m_st - m_new)
        c_new = decay[..., None, None] * c_st + jnp.einsum("bhj,bhjd,bhje->bhde", w_k, k_c, v_c)
        n_new = decay[..., None] * n_st + jnp.einsum("bhj,bhjd->bhd", w_k, k_c)
        return (c_new, n_new, m_new), h_c

    init = (jnp.zeros((bsz, M_HEADS, M_DK, M_DV), f32),
            jnp.zeros((bsz, M_HEADS, M_DK), f32),
            jnp.zeros((bsz, M_HEADS), f32))
    _, h = lax.scan(chunk_step, init, (qc, kc, vc, log_i, log_f))
    h = jnp.moveaxis(h, (0, 2), (1, 3)).reshape(bsz, n_chunks * M_CHUNK, M_HEADS, M_DV)
    return h[:, n_pad:]

def first_inputs(seed: int = 0) -> dict:
    key = jax.random.key(seed)
    ks = jax.random.split(key, 27)
    f32 = jnp.float32

    def nrm(k, shape, scale):
        return scale * jax.random.normal(k, shape, f32)

    b_in = nrm(ks[5], (DEPTH, IN_WIDTH), 0.02)
    b_in = b_in.at[:, F_GATE_OFFSET:F_GATE_OFFSET + M_HEADS].add(jnp.linspace(3.0, 6.0, M_HEADS))
    s5_lambda_re = -0.5 + nrm(ks[8], (DEPTH, S5_GROUPS, S5_STATE), 0.01)
    s5_lambda_im = jnp.pi * jnp.arange(S5_STATE, dtype=f32) + nrm(ks[9], (DEPTH, S5_GROUPS, S5_STATE), 0.01)
    s5_log_dt = jax.random.uniform(ks[10], (DEPTH, S5_GROUPS), f32, math.log(DT_MIN), math.log(DT_MAX))
    return {
        "x": nrm(ks[0], (BATCH, SEQ, D_MODEL), 1.0),
        "meta_tokens": nrm(ks[1], (N_META, D_MODEL), 1.0),
        "ln0_g": 1.0 + nrm(ks[2], (D_MODEL,), 0.05),
        "ln0_b": nrm(ks[3], (D_MODEL,), 0.02),
        "w_in": nrm(ks[4], (DEPTH, D_MODEL, IN_WIDTH), D_MODEL ** -0.5),
        "b_in": b_in,
        "qk_conv_w": nrm(ks[6], (DEPTH, CONV_WIDTH, 2 * M_QK_WIDTH), CONV_WIDTH ** -0.5),
        "qk_conv_b": nrm(ks[7], (DEPTH, 2 * M_QK_WIDTH), 0.02),
        "s5_lambda_re": s5_lambda_re,
        "s5_lambda_im": s5_lambda_im,
        "s5_log_dt": s5_log_dt,
        "s5_b_re": nrm(ks[11], (DEPTH, S5_GROUPS, S5_STATE, S5_GROUP), (2.0 * S5_GROUP) ** -0.5),
        "s5_b_im": nrm(ks[12], (DEPTH, S5_GROUPS, S5_STATE, S5_GROUP), (2.0 * S5_GROUP) ** -0.5),
        "s5_c_re": nrm(ks[13], (DEPTH, S5_GROUPS, S5_GROUP, S5_STATE), S5_STATE ** -0.5),
        "s5_c_im": nrm(ks[14], (DEPTH, S5_GROUPS, S5_GROUP, S5_STATE), S5_STATE ** -0.5),
        "s5_d": nrm(ks[15], (DEPTH, S5_WIDTH), 1.0),
        "s5_w_glu": nrm(ks[16], (DEPTH, S5_WIDTH, 2 * D_MODEL), S5_WIDTH ** -0.5),
        "m_norm_g": 1.0 + nrm(ks[17], (DEPTH, M_V_WIDTH), 0.05),
        "m_w_out": nrm(ks[18], (DEPTH, M_V_WIDTH, D_MODEL), M_V_WIDTH ** -0.5),
        "w_o": nrm(ks[19], (DEPTH, D_MODEL, D_MODEL), BETA * D_MODEL ** -0.5),
        "ln1_g": 1.0 + nrm(ks[20], (DEPTH, D_MODEL), 0.05),
        "ln1_b": nrm(ks[21], (DEPTH, D_MODEL), 0.02),
        "w_up": nrm(ks[22], (DEPTH, D_MODEL, D_FF), D_MODEL ** -0.5),
        "b_up": nrm(ks[23], (DEPTH, D_FF), 0.02),
        "w_down": nrm(ks[24], (DEPTH, D_FF, D_MODEL), BETA * D_FF ** -0.5),
        "ln2_g": 1.0 + nrm(ks[25], (DEPTH, D_MODEL), 0.05),
        "ln2_b": nrm(ks[26], (DEPTH, D_MODEL), 0.02),
    }

def first_block(x, meta_tokens, ln0_g, ln0_b, w_in, b_in, qk_conv_w, qk_conv_b,
              s5_lambda_re, s5_lambda_im, s5_log_dt, s5_b_re, s5_b_im, s5_c_re, s5_c_im,
              s5_d, s5_w_glu, m_norm_g, m_w_out, w_o, ln1_g, ln1_b, w_up, b_up, w_down,
              ln2_g, ln2_b):
    bsz = x.shape[0]
    meta = jnp.broadcast_to(meta_tokens[None].astype(x.dtype), (bsz, N_META, D_MODEL))
    h = _layer_norm(jnp.concatenate([meta, x], axis=1), ln0_g, ln0_b)
    length = h.shape[1]
    for layer in range(DEPTH):
        p = h @ w_in[layer] + b_in[layer]
        u_s5, q, k, v, o_pre, i_pre, f_pre, g_s5, g_m = _split_columns(p)
        y_s5 = _s5_mixer(u_s5, s5_lambda_re[layer], s5_lambda_im[layer], s5_log_dt[layer],
                         s5_b_re[layer], s5_b_im[layer], s5_c_re[layer], s5_c_im[layer], s5_d[layer])
        z = jax.nn.gelu(y_s5).astype(h.dtype) @ s5_w_glu[layer]
        y_s5 = z[..., :D_MODEL] * jax.nn.sigmoid(z[..., D_MODEL:])
        qk = jax.nn.silu(_causal_depthwise_conv(jnp.concatenate([q, k], axis=-1),
                                                qk_conv_w[layer], qk_conv_b[layer]))
        q_h = qk[..., :M_QK_WIDTH].reshape(bsz, length, M_HEADS, M_DK)
        k_h = qk[..., M_QK_WIDTH:].reshape(bsz, length, M_HEADS, M_DK)
        v_h = v.reshape(bsz, length, M_HEADS, M_DV)
        hm = _mlstm_mixer(q_h, k_h, v_h, i_pre, f_pre)
        hm = _head_norm(hm, m_norm_g[layer]).reshape(bsz, length, M_V_WIDTH).astype(h.dtype)
        y_m = (jax.nn.sigmoid(o_pre) * hm) @ m_w_out[layer]
        mix = jax.nn.sigmoid(g_s5) * y_s5 + jax.nn.sigmoid(g_m) * y_m
        h = _layer_norm(ALPHA * h + mix @ w_o[layer], ln1_g[layer], ln1_b[layer])
        ff = jnp.square(jax.nn.relu(h @ w_up[layer] + b_up[layer])) @ w_down[layer]
        h = _layer_norm(ALPHA * h + ff, ln2_g[layer], ln2_b[layer])
    return h[:, N_META:]


MIX_WIDTH = D_MODEL
HEAD_DIM = 64
ATTN_WIDTH = MIX_WIDTH // 2
N_Q_HEADS = ATTN_WIDTH // HEAD_DIM
N_KV_HEADS = 2
KV_WIDTH = N_KV_HEADS * HEAD_DIM
TOK_WIDTH = MIX_WIDTH - ATTN_WIDTH
N_TOK_HEADS = TOK_WIDTH // HEAD_DIM
N_IN = ATTN_WIDTH + 2 * KV_WIDTH + 2 * TOK_WIDTH
CHUNK = 128
Q_BLOCK = 128
GRID_W = 64
ROPE_THETA = 10000.0
D_FF_2 = 2816
CONV_W = 3
N_MOD = 6
EPS = 1e-6


def rmsnorm(x, g):
    xf = x.astype(jnp.float32)
    y = xf * lax.rsqrt(jnp.mean(xf * xf, axis=-1, keepdims=True) + EPS)
    return (y * g.astype(jnp.float32)).astype(x.dtype)

def axial_rope_tables(seq_len):
    rows = seq_len // GRID_W
    row_id = jnp.broadcast_to(jnp.arange(rows)[:, None], (rows, GRID_W)).reshape(-1).astype(jnp.float32)
    col_id = jnp.broadcast_to(jnp.arange(GRID_W)[None, :], (rows, GRID_W)).reshape(-1).astype(jnp.float32)
    axis_dim = HEAD_DIM // 2
    inv_freq = jnp.power(jnp.float32(ROPE_THETA), -jnp.arange(0, axis_dim, 2, dtype=jnp.float32) / axis_dim)
    ang_r = row_id[:, None] * inv_freq[None, :]
    ang_c = col_id[:, None] * inv_freq[None, :]
    ang = jnp.concatenate([ang_r, ang_r, ang_c, ang_c], axis=-1)
    return jnp.cos(ang), jnp.sin(ang)

def rotate_half(a):
    a1, a2 = jnp.split(a, 2, axis=-1)
    return jnp.concatenate([-a2, a1], axis=-1)

def apply_axial_rope(x, cos, sin):
    xr, xc = jnp.split(x, 2, axis=-1)
    rot = jnp.concatenate([rotate_half(xr), rotate_half(xc)], axis=-1)
    return x * cos + rot * sin

def block_attention(q, k, v):
    B, S = q.shape[0], q.shape[1]
    groups = N_Q_HEADS // N_KV_HEADS
    nb = S // Q_BLOCK
    qb = q.reshape(B, nb, Q_BLOCK, N_KV_HEADS, groups, HEAD_DIM).transpose(1, 0, 2, 3, 4, 5)
    scale = jnp.float32(HEAD_DIM ** -0.5)

    def one_block(qi):
        s = jnp.einsum('bqkgd,bskd->bkgqs', qi, k, preferred_element_type=jnp.float32) * scale
        p = jax.nn.softmax(s, axis=-1)
        return jnp.einsum('bkgqs,bskd->bqkgd', p.astype(v.dtype), v)

    ob = lax.map(one_block, qb)
    return ob.transpose(1, 0, 2, 3, 4, 5).reshape(B, S, ATTN_WIDTH)

def chunked_token_mlp(z, g_v, w_s, b_s):
    B, S = z.shape[0], z.shape[1]
    nc = S // CHUNK
    z = jax.nn.gelu(z)
    u, v = jnp.split(z, 2, axis=-1)
    v = rmsnorm(v.reshape(B, S, N_TOK_HEADS, HEAD_DIM), g_v)
    v = v.reshape(B, nc, CHUNK, N_TOK_HEADS, HEAD_DIM)
    mixed = jnp.einsum('hpq,bcqhd->bcphd', w_s, v) + b_s.T[None, None, :, :, None]
    out = u.reshape(B, nc, CHUNK, N_TOK_HEADS, HEAD_DIM) * mixed
    return out.reshape(B, S, TOK_WIDTH)

def conv_glu_ffn(h, w_up, w_conv, b_conv, w_down):
    z = h @ w_up
    zp = jnp.pad(z, ((0, 0), (1, 1), (0, 0)))
    z = zp[:, :-2] * w_conv[0] + zp[:, 1:-1] * w_conv[1] + zp[:, 2:] * w_conv[2] + b_conv
    a, b = jnp.split(z, 2, axis=-1)
    return (jax.nn.silu(a) * b) @ w_down

def second_inputs(seed: int = 0) -> dict:
    key = jax.random.key(seed)
    ks = jax.random.split(key, 24)
    f32 = jnp.float32
    L, D = DEPTH, D_MODEL

    def nrm(k, shape, scale):
        return jax.random.normal(k, shape, f32) * scale

    def gain(k, shape):
        return 1.0 + 0.05 * jax.random.normal(k, shape, f32)

    return {
        "x": nrm(ks[0], (BATCH, SEQ, D), 1.0),
        "c": nrm(ks[1], (BATCH, D), 1.0),
        "w_ada": nrm(ks[2], (L, D, N_MOD * D), 0.5 * D ** -0.5),
        "b_ada": nrm(ks[3], (L, N_MOD * D), 0.01),
        "g_norm1": gain(ks[4], (L, D)),
        "w_in": nrm(ks[5], (L, D, N_IN), D ** -0.5),
        "g_q": gain(ks[6], (L, HEAD_DIM)),
        "g_k": gain(ks[7], (L, HEAD_DIM)),
        "g_tok_v": gain(ks[8], (L, HEAD_DIM)),
        "w_s": nrm(ks[9], (L, N_TOK_HEADS, CHUNK, CHUNK), CHUNK ** -0.5),
        "b_s": 1.0 + nrm(ks[10], (L, N_TOK_HEADS, CHUNK), 0.01),
        "g_attn_out": gain(ks[11], (L, ATTN_WIDTH)),
        "g_tok_out": gain(ks[12], (L, TOK_WIDTH)),
        "w_out": nrm(ks[13], (L, MIX_WIDTH, D), MIX_WIDTH ** -0.5),
        "g_norm2": gain(ks[14], (L, D)),
        "w_up": nrm(ks[15], (L, D, 2 * D_FF_2), D ** -0.5),
        "w_conv": nrm(ks[16], (L, CONV_W, 2 * D_FF_2), CONV_W ** -0.5),
        "b_conv": nrm(ks[17], (L, 2 * D_FF_2), 0.01),
        "w_down": nrm(ks[18], (L, D_FF_2, D), D_FF_2 ** -0.5),
        "g_final": gain(ks[19], (D,)),
    }

def second_block(x, c, w_ada, b_ada, g_norm1, w_in, g_q, g_k, g_tok_v, w_s, b_s,
              g_attn_out, g_tok_out, w_out, g_norm2, w_up, w_conv, b_conv, w_down, g_final):
    B, S, _ = x.shape
    cos, sin = axial_rope_tables(S)
    cos = cos.astype(x.dtype)[None, :, None, :]
    sin = sin.astype(x.dtype)[None, :, None, :]
    mod_all = jnp.einsum('bd,ldm->lbm', jax.nn.silu(c), w_ada) + b_ada[:, None, :]

    for l in range(DEPTH):
        sh1, sc1, gt1, sh2, sc2, gt2 = jnp.split(mod_all[l][:, None, :], N_MOD, axis=-1)

        h = rmsnorm(x, g_norm1[l]) * (1.0 + sc1) + sh1
        proj = h @ w_in[l]
        q, k, v, z = jnp.split(
            proj, [ATTN_WIDTH, ATTN_WIDTH + KV_WIDTH, ATTN_WIDTH + 2 * KV_WIDTH], axis=-1)
        q = rmsnorm(q.reshape(B, S, N_Q_HEADS, HEAD_DIM), g_q[l])
        k = rmsnorm(k.reshape(B, S, N_KV_HEADS, HEAD_DIM), g_k[l])
        q = apply_axial_rope(q, cos, sin)
        k = apply_axial_rope(k, cos, sin)
        v = v.reshape(B, S, N_KV_HEADS, HEAD_DIM)
        attn = block_attention(q, k, v)
        tok = chunked_token_mlp(z, g_tok_v[l], w_s[l], b_s[l])
        mixed = jnp.concatenate(
            [rmsnorm(attn, g_attn_out[l]), rmsnorm(tok, g_tok_out[l])], axis=-1)
        x = x + gt1 * (mixed @ w_out[l])

        h = rmsnorm(x, g_norm2[l]) * (1.0 + sc2) + sh2
        x = x + gt2 * conv_glu_ffn(h, w_up[l], w_conv[l], b_conv[l], w_down[l])

    return rmsnorm(x, g_final)


def setup_inputs(seed=0):
    out = dict(first_inputs(seed))
    for name, value in second_inputs(seed + 1).items():
        if name != "x":
            out[name + "_2"] = value
    return out


def reference(
    x, meta_tokens, ln0_g, ln0_b, w_in, b_in, qk_conv_w, qk_conv_b, s5_lambda_re, s5_lambda_im,
    s5_log_dt, s5_b_re, s5_b_im, s5_c_re, s5_c_im, s5_d, s5_w_glu, m_norm_g, m_w_out, w_o,
    ln1_g, ln1_b, w_up, b_up, w_down, ln2_g, ln2_b, c_2, w_ada_2, b_ada_2, g_norm1_2, w_in_2,
    g_q_2, g_k_2, g_tok_v_2, w_s_2, b_s_2, g_attn_out_2, g_tok_out_2, w_out_2, g_norm2_2,
    w_up_2, w_conv_2, b_conv_2, w_down_2, g_final_2,
):
    x = first_block(
        x, meta_tokens, ln0_g, ln0_b, w_in, b_in, qk_conv_w, qk_conv_b, s5_lambda_re,
        s5_lambda_im, s5_log_dt, s5_b_re, s5_b_im, s5_c_re, s5_c_im, s5_d, s5_w_glu, m_norm_g,
        m_w_out, w_o, ln1_g, ln1_b, w_up, b_up, w_down, ln2_g, ln2_b,
    )
    return second_block(
        x, c_2, w_ada_2, b_ada_2, g_norm1_2, w_in_2, g_q_2, g_k_2, g_tok_v_2, w_s_2, b_s_2,
        g_attn_out_2, g_tok_out_2, w_out_2, g_norm2_2, w_up_2, w_conv_2, b_conv_2, w_down_2,
        g_final_2,
    )


_drawn_inputs = setup_inputs


def setup_inputs(seed=0):
    import zlib

    import numpy as np

    out = dict(_drawn_inputs(seed))
    spreads = {}
    factors = {'qk_conv_b': 8.0,
     's5_lambda_re': 64.0,
     's5_lambda_im': 59.976,
     's5_log_dt': 61.296,
     's5_b_re': 64.0,
     's5_b_im': 64.0,
     's5_c_re': 64.0,
     's5_c_im': 64.0,
     'm_norm_g': 7.538,
     'b_up': 4.402,
     'b_ada_2': 3.815,
     'g_norm1_2': 3.943,
     'g_q_2': 8.0,
     'g_k_2': 8.0,
     'g_tok_v_2': 7.664,
     'b_s_2': 64.0,
     'g_attn_out_2': 5.027,
     'g_tok_out_2': 5.008,
     'g_norm2_2': 3.797,
     'b_conv_2': 8.0}
    for name, (base, spread) in spreads.items():
        noise = np.random.default_rng([zlib.crc32(name.encode()), seed]).standard_normal(out[name].shape)
        drawn = base * np.exp(spread * noise) if base else spread * noise
        out[name] = __import__('jax').numpy.asarray(drawn.astype(out[name].dtype))
    for name, factor in factors.items():
        out[name] = (out[name] * factor).astype(out[name].dtype)
    return out
```

```python
from contextlib import ExitStack

import concourse.bass as bass
from concourse import mybir

F32 = mybir.dt.float32
F32R = mybir.dt.float32r
ACT = mybir.ActivationFunctionType
ALU = mybir.AluOpType
AX = mybir.AxisListType

P = 128
D = 1024
KD = D // P
SEQ = 256
META = 16
TOK = SEQ + META
NT = SEQ // P
S5W, S5G, S5H, S5P = 512, 32, 16, 64
NS5 = S5G * S5P // P
CH = S5W // P
HEADS, DK, DV = 4, 128, 256
DFF = 4 * D
KF = DFF // P
DFF2 = 2816
KF2 = DFF2 // P
QT = 4
AH = 8
HD = 64
NMOD = 6
ALPHA = 2.0 ** 0.25
LN_EPS = 1e-5
RMS_EPS = 1e-6
TWO_PI = 6.283185307179586
HALF_TURN = 3.1415925
ROUND = 12582912.0
PI_A, PI_B, PI_C = 6.28125, 0.0019353071693331003, 1.0253131677018246e-11

RING = 4
AHEAD = 3
B_U, B_Q, B_K, B_V = 0, 4, 8, 12
B_GS, B_O, B_GM = 20, 28, 36
B_GLU, B_MOUT, B_WO = 44, 52, 60
B_F1 = 68
B_IN2 = B_F1 + 2 * KF
B_OUT2 = B_IN2 + 14
B_F2 = B_OUT2 + KD
NBLK = B_F2 + 3 * KF2
N_POOL = B_MOUT
LOOP1_PAIR = 8
ADA_RING = 4
ADA_SHARE = (3, 2, 2, 3, 2, 2, 2, 0)
SP_LOOP = B_F1 + 20
B_ZV, B_ZU, B_K2, B_V2, B_Q2 = B_IN2, B_IN2 + 4, B_IN2 + 8, B_IN2 + 9, B_IN2 + 10
LOOP2_TRIPLE = 2
M_SH1, M_SC1, M_GT1, M_SH2, M_SC2, M_GT2 = (n * KD for n in range(NMOD))

COLS = {}


def _layout_cols():
    at = 0
    for name, n in (("b_in", 44), ("conv_w", 32), ("conv_b", 8), ("s5_d", 4), ("ln0_g", 8), ("ln0_b", 8),
                    ("ln1_g", 8), ("ln1_b", 8), ("b_up", 32), ("ln2_g", 8), ("ln2_b", 8), ("m_norm_g", 8),
                    ("lam_re", 16), ("lam_im", 16), ("log_dt", 16), ("b_ada", 48), ("g_norm1", 8), ("g_q", 1),
                    ("g_k", 1), ("g_tok_v", 1), ("g_attn", 4), ("g_tok", 4), ("g_norm2", 8), ("conv2_w", 132),
                    ("conv2_b", 44), ("g_final", 8), ("c", 8)):
        COLS[name] = (at, n)
        at += n
    return at


NCOL = _layout_cols()
C_ID, C_ONE, C_BLK, C_ROT, C_SWAP, C_MASK, C_T = 0, 128, 256, 384, 512, 640, 768
C_ONE_ = C_T + TOK
NCONST = C_ONE_ + 1


class Steps:

    def __init__(self, eng, sem):
        self.eng, self.sem, self.n, self.at = eng, sem, 0, None

    def __call__(self, ins):
        ins.then_inc(self.sem, 1)
        self.n += 1
        self.eng.wait_ge(self.sem, self.n if self.at is None else self.at + self.n)

    def enter(self, i, per):
        self.base, self.per, self.at, self.n = self.n, per, i * per + self.n, 0

    def leave(self, turns):
        assert self.n == self.per, (self.n, self.per)
        self.n, self.at = self.base + turns * self.per, None


def two_blocks(nc: bass.Bass, A: dict, out: bass.AP):
    with ExitStack() as ctx:
        def sb(name, shape, dt=F32, scope=None):
            return (scope or ctx).enter_context(nc.sbuf_tensor(name, shape, dt))

        def sem(name):
            return ctx.enter_context(nc.semaphore(name))

        raw = sb("raw", [P, RING, 1024])
        wh = sb("wh", [P, RING, 1024], F32R)
        wl = sb("wl", [P, RING, 1024], F32R)
        xh = sb("xh", [P, KD, TOK], F32R)
        xl = sb("xl", [P, KD, TOK], F32R)
        res = sb("res", [P, KD, TOK])
        cols = sb("cols", [P, NCOL])
        cst = sb("cst", [P, NCONST])
        hb = sb("hb", [P, 52])
        mod = sb("mod", [P, NMOD * KD])
        eps = sb("eps", [P, 3])
        std = sb("std", [P, SEQ])
        rstd2 = sb("rstd2", [P, SEQ])
        rstd = sb("rstd", [P, SEQ])

        tabs = ExitStack()
        tab = sb("tab", [P, NS5, 2, TOK], F32, tabs)
        tabs.close()
        gh = sb("gh", [P, 4, SEQ], F32R)
        gl = sb("gl", [P, 4, SEQ], F32R)
        tg_m = sb("tg_m", [P, KD, SEQ])
        mh = sb("mh", [P, KD, SEQ], F32R)
        ml = sb("ml", [P, KD, SEQ], F32R)
        rest_of_tab = sb("rest_of_tab", [P, NS5 * 2 * TOK - 2 * 4 * SEQ - 3 * KD * SEQ])

        ph1 = ExitStack()
        tg_s = sb("tg_s", [P, KD, SEQ], F32, ph1)
        tg_o = sb("tg_o", [P, KD, SEQ], F32, ph1)
        vtk = sb("vtk", [P, 3, HEADS, DV + 1], F32, ph1)
        qkT = sb("qkT", [P, 8, TOK + 3], F32, ph1)
        uT = sb("uT", [P, CH, TOK], F32, ph1)
        hraw = sb("hraw", [P, NT, HEADS, DV + 1], F32, ph1)
        swork = sb("swork", [P, 4, TOK], F32, ph1)
        sA, sB = swork[:, 0:2, :], swork[:, 2:4, :]
        zz = sb("zz", [P, 2, TOK], F32, ph1)
        sP = sb("sP", [P, 2, SEQ], F32, ph1)
        sQ = sb("sQ", [P, 2, SEQ], F32, ph1)
        xst = sb("xst", [P, 2, 2, SEQ], F32, ph1)
        cv = sb("cv", [P, 2, TOK], F32, ph1)
        vr = sb("vr", [P, 2, TOK], F32, ph1)
        ee = sb("ee", [P, 640], F32, ph1)
        pp = sb("pp", [P, 640], F32, ph1)
        rows = sb("rows", [HEADS, 4, TOK], F32, ph1)
        wg = sb("wg", [P, KD, 8], F32, ph1)
        bg = sb("bg", [HEADS, 2], F32, ph1)
        sel = sb("sel", [HEADS, HEADS, P], F32, ph1)
        aT = sb("aT", [P, 3, HEADS], F32, ph1)
        floor = sb("floor", [P, NT, HEADS], F32, ph1)
        hst = sb("hst", [P, 6], F32, ph1)
        hmv = sb("hmv", [P, NT, HEADS, 2], F32, ph1)
        hsm = sb("hsm", [P, 4, NT, HEADS], F32, ph1)
        early = hraw[:, :, :, :].rearrange("p t h e -> p (t h e)")
        s5m = early[:, 0:1024].rearrange("p (n s h) -> p n s h", n=4, s=NS5)
        zre = early[:, 1024:1536].rearrange("p (s h) -> p s h", s=NS5)
        zim = early[:, 1536:2048].rearrange("p (s h) -> p s h", s=NS5)
        btr = sb("btr", [P, CH, P], F32, ph1)
        bti = sb("bti", [P, CH, P], F32, ph1)
        cbr = sb("cbr", [P, NS5, 2 * S5H], F32, ph1)
        cbi = sb("cbi", [P, NS5, 2 * S5H], F32, ph1)
        sv = sb("sv", [P, 20, NS5], F32, ph1)
        xt = [vtk[:, :, :, :].rearrange("p a b c -> p (a b c)")[:, n * D:(n + 1) * D] for n in range(3)]
        lnst = sb("lnst", [P, 3, 2, 6], F32, ph1)
        lnmv = sb("lnmv", [P, 3, 2], F32, ph1)
        lnr = sb("lnr", [P, 3, 2], F32, ph1)
        swork_flat = swork[:, :, :].rearrange("p a t -> p (a t)")
        tz = swork_flat[:, 0:2 * SEQ].rearrange("p (a t) -> p a t", a=2)
        tw = swork_flat[:, 2 * SEQ:4 * SEQ].rearrange("p (a t) -> p a t", a=2)

        ph1.close()

        mods = ExitStack()
        ada_w = sb("ada_w", [P, ADA_RING, D], F32, mods)
        mods.close()
        prob = sb("prob", [P, 2, NT, SEQ])
        probt = sb("probt", [P, 2, NT, SEQ])
        ob = sb("ob", [P, NT, D])
        ada_acc = sb("ada_acc", [P, 2, D])
        sc = sb("silu_c", [P, KD])
        relu = sb("relu", [P, 2, SEQ])
        relu2 = sb("relu2", [P, 2, SEQ])
        sq = sb("sq", [P, KD, SEQ])
        gain = sb("gain", [P, 2, KD])
        rope = sb("rope", [P, 2, SEQ])
        zv = sb("zv", [P, QT, SEQ])
        zu = sb("zu", [P, QT, SEQ])
        zst = sb("zst", [P, QT, SEQ])
        zvt = sb("zvt", [P, NT, QT * P])
        ws = sb("ws", [P, AH, P])
        wst = sb("wst", [P, AH, P])
        bs = sb("bs", [P, QT, P])
        qs = sb("qs", [P, 2, SEQ])
        qg = sb("qg", [P, 2, SEQ])
        qstd = sb("qstd", [P, 2, SEQ])
        qrot = sb("qrot", [P, SEQ])
        qf = sb("qf", [P, QT, SEQ])
        kf = sb("kf", [P, 2, SEQ])
        vv = sb("vv", [P, SEQ])
        vtok = sb("vtok", [P, NT, P])
        smax = sb("smax", [P, AH, 2, NT])
        ssum = sb("ssum", [P, AH, NT])
        ao = sb("ao", [P, QT, SEQ])
        ca = sb("ca", [P, 2, SEQ])
        cb = sb("cb", [P, 2, SEQ])
        cg = sb("cg", [P, 2, SEQ])

        ps = ctx.enter_context(nc.psum_tensor("ps", [P, 8, 512], F32))

        landed = [sem(f"block_landed_{r}") for r in range(RING)]
        hi_done, lo_pool, lo_dve, blk_done = sem("hi_done"), sem("lo_by_pool"), sem("lo_by_dve"), sem("block_done")
        act_step, dve_step, pool_step = sem("act_step"), sem("dve_step"), sem("pool_step")
        S = {n: sem(n) for n in (
            "x_landed", "x2_landed", "meta_landed", "cols_landed", "consts_landed", "gates_landed", "s5m_landed",
            "stored",
            "cleared", "ln0_var", "ln0_std", "ln0_norm", "ln0_turned", "ln0_h", "ln0_hi", "ln0_lo",
            "dt_done", "half_done", "phase_done", "tables_done", "z_done", "z_turned", "bt_done",
            "c_done", "gate_mm", "gate_ev", "abs_f", "ln_done", "rows_done", "a_turned", "a_copied", "floor_done",
            "u_ev", "qk_ev", "conv_done", "silu_done", "v_ev", "v_turned", "v_copied", "gs_ev", "o_ev", "gm_ev",
            "s5_in", "s5_free", "s5_x", "s5_y", "y_sum", "y_hi", "y_act", "y_lo",
            "cs_done", "e_done", "p_done", "num_done", "num_copied", "hvar", "hstd", "hnorm",
            "h_turned", "h_gated", "hm_f", "hm_hi", "hm_lo",
            "glu_t", "glu_ev", "mout_ev", "mix_hi", "mix_lo", "wo_ev",
            "ada_used", "mod_mm", "mod_done", "silu_c", "f_relu", "f_hi", "f_lo", "f1_res",
            "mixing_landed", "ws_turned", "ws_copied",
            "zv_ev", "zv_sq", "zv_ms", "zv_std", "zv_n", "zv_turned", "zv_copied", "zu_ev", "mixed", "tok_pre", "tok_done",
            "q_ev", "q_stat", "q_std", "b3_full", "b3_free", "v2_ev", "qk_ready",
            "s_done", "max_done", "exp_done", "prob_done", "pt_done", "pt_copied", "o_done", "ao_done",
            "tok_sq", "att_sq", "branch_ms", "branch_std", "branch_f", "branch_hi", "branch_lo",
            "out2_ev", "ff2_a", "ff2_b", "ff2_ca", "ff2_cb", "ff2_silu", "ff2_g", "ff2_hi", "ff2_lo", "f2_res",
            "fin_sq", "fin_ms", "fin_std", "fin_f", "fin_turned", "fin_copied",
        )}

        NORM_BASE = {"mean": (0, 1), "d": (0, 4), "sq": (0, 4, 8, 12), "var": (0, 1, 2, 3), "std": (0, 1, 2, 3),
                     "h": (0, 8, 16, 24), "hi": (0, 4, 4, 8), "lo": (0, 4, 4, 8)}
        NORM = {what: sem(f"norm_{what}") for what in NORM_BASE}

        def norm(tag, what, n=1):
            return NORM[what], NORM_BASE[what][("n1", "n2", "r1", "r2").index(tag)] + n

        ada_landed = [sem(f"ada_landed_{r}") for r in range(ADA_RING)]

        def col(name, n=0, rows_=P):
            return cols[0:rows_, COLS[name][0] + n:COLS[name][0] + n + 1]

        def span(name):
            return cols[:, COLS[name][0]:COLS[name][0] + COLS[name][1]]

        ident = cst[:, C_ID:C_ID + P]
        ones = cst[:, C_ONE:C_ONE + P]

        J = ((0, META), (META, META + P), (META + P, TOK))

        def y_s(c):
            return uT[:, c, META:TOK]

        block = ctx.enter_context(nc.Block())

        @block.sync
        def _(sp):
            sp.dma_start(xt[1], A["x"][0, 0:P, :]).then_inc(S["x_landed"], 16)
            sp.dma_start(xt[2], A["x"][0, P:2 * P, :]).then_inc(S["x2_landed"], 16)
            for b in range(RING):
                sp.dma_start(raw[:, b], A["w_stream"][b]).then_inc(landed[b], 16)
            with sp.Fori(0, N_POOL // RING) as i:
                for r in range(RING):
                    sp.wait_ge(lo_pool, i * RING + (r + 1))
                    sp.dma_start(raw[:, r], A["w_stream"][i * RING + (RING + r)]).then_inc(landed[r], 16)

            def block_in(b, t=0):
                sp.wait_ge(lo_dve, t + (b - RING - N_POOL + 1))
                sp.dma_start(raw[:, b % RING], A["w_stream"][t + b]).then_inc(landed[b % RING], 16)

            def ada_in(n, t=0):
                if n >= ADA_RING:
                    sp.wait_ge(S["ada_used"], t + (n - ADA_RING + 1))
                sp.dma_start(ada_w[:, n % ADA_RING], A["w_ada"][t + n]).then_inc(ada_landed[n % ADA_RING], 16)

            FIRST = N_POOL + RING
            with sp.Fori(0, (SP_LOOP - FIRST) // RING) as i:
                for r in range(RING):
                    block_in(FIRST + r, i * RING)
            for n in range(ADA_RING):
                ada_in(n)
            def ffn_turn(t, last):
                n = ADA_RING
                for q in range(8):
                    block_in(SP_LOOP + 2 * q, t)
                    block_in(SP_LOOP + 2 * q + 1, t)
                    for _ in range(ADA_SHARE[q]):
                        if not last or n < 16:
                            ada_in(n, t)
                        n += 1

            with sp.Fori(0, 2) as i:
                ffn_turn(i * 16, False)
            ffn_turn(32, True)
            REST = SP_LOOP + 48
            with sp.Fori(0, (NBLK - REST) // RING) as i:
                for r in range(RING):
                    block_in(REST + r, i * RING)
            for n in range(4):
                t, half = n // 2, n % 2
                sp.wait_ge(S["fin_copied"], n + 1)
                sp.dma_start(out[0, t * P:(t + 1) * P, half * 512:(half + 1) * 512], ob[:, t, half * 512:(half + 1) * 512])\
                    .then_inc(S["stored"], 16)
            sp.wait_ge(S["stored"], 64)

        @block.tensor
        def _(pe):
            def evacuated(b):
                if b < 2:
                    return
                c = b - 2
                for first, n, name in ((B_WO, 8, "wo_ev"), (B_MOUT, 8, "mout_ev"), (B_GLU, 8, "glu_ev"),
                                       (B_GM, 8, "gm_ev"), (B_O, 8, "o_ev"), (B_GS, 8, "gs_ev"),
                                       (B_V, 8, "v_ev"), (B_Q, 8, "qk_ev"), (B_U, 4, "u_ev")):
                    if c >= first:
                        pe.wait_ge(S[name], c - first + 1)
                        return

            def split_ready(b):
                if b < N_POOL:
                    pe.wait_ge(lo_pool, b + 1)
                else:
                    pe.wait_ge(lo_dve, b + 1 - N_POOL)

            def product(bank, n, slot, pieces, done=True):
                k = 0
                for tile, ah, al in pieces:
                    w_hi, w_lo = (w[:, slot, tile * P:(tile + 1) * P] for w in (wh, wl))
                    for w, a in ((w_hi, ah), (w_hi, al), (w_lo, ah)):
                        mm = nc.tensor.matmul(bank[:, 0:n], w, a, start=(k == 0), stop=(k == 3 * len(pieces) - 1))
                        k += 1
                return mm

            def stream(b, first_token, h=xh, l=xl, n=KD):
                evacuated(b)
                split_ready(b)
                product(ps[:, b % 2], TOK - first_token, b % RING,
                        [(k, h[:, k, first_token:TOK], l[:, k, first_token:TOK]) for k in range(n)]).then_inc(blk_done, 1)

            pe.wait_ge(S["consts_landed"], 16)
            pe.wait_ge(S["ln0_norm"], 3)
            for k in range(KD):
                if k >= 2:
                    pe.wait_ge(S["ln0_hi"], k - 1)
                for n, (a, z) in enumerate(J):
                    mm = nc.tensor.transpose(ps[:, 2 + k % 2, a:z], xt[n][0:z - a, k * P:(k + 1) * P], ident[0:z - a, 0:z - a])
                mm.then_inc(S["ln0_turned"], 1)
            pe.wait_ge(S["ln0_lo"], KD)
            for b in range(B_U, B_Q):
                stream(b, 0)
            pe.wait_ge(S["gates_landed"], 48)
            for g in range(2):
                for k in range(KD):
                    mm = nc.tensor.matmul(ps[0:HEADS, 6 + g, 0:TOK], wg[:, k, 4 * g:4 * g + 4], res[:, k, :],
                                          start=(k == 0), stop=(k == KD - 1))
                mm.then_inc(S["gate_mm"], 1)
            pe.wait_ge(S["z_done"], 1)
            for n, z in enumerate((zre, zim)):
                for c in range(CH):
                    mm = nc.tensor.transpose(ps[:, 2 + n, c * P:(c + 1) * P],
                                             z[:, 4 * c:4 * c + 4, :].rearrange("p s h -> p (s h)"), ident)
                mm.then_inc(S["z_turned"], 1)

            def s5_in(s):
                if s == 0:
                    pe.wait_ge(S["bt_done"], 2)
                    pe.wait_ge(S["u_ev"], CH)
                else:
                    pe.wait_ge(S["s5_free"], s)
                r, c = 32 * (s % 4), s // 4
                for n, bt in enumerate((btr, bti)):
                    mm = nc.tensor.matmul(ps[:, 2 + n, 0:TOK], bt[r:r + 32, c, :], uT[r:r + 32, c, :], start=True, stop=True,
                                          tile_position=(r, 0))
                mm.then_inc(S["s5_in"], 1)

            def s5_out(s):
                r = 32 * (s % 4)
                if s == 0:
                    pe.wait_ge(S["c_done"], 1)
                if s % 4 == 0 and s:
                    pe.wait_ge(S["y_sum"], s // 4)
                pe.wait_ge(S["s5_x"], s + 1)
                nc.tensor.matmul(ps[r:r + 32, 4, 0:SEQ], cbr[:, s, :], xst[:, s % 2, 0, :], start=True, stop=False)
                nc.tensor.matmul(ps[r:r + 32, 4, 0:SEQ], cbi[:, s, :], xst[:, s % 2, 1, :], start=False, stop=True)\
                    .then_inc(S["s5_y"], 1)

            def turn_gates():
                pe.wait_ge(S["rows_done"], 1)
                for n, (a, z) in enumerate(J):
                    nc.tensor.transpose(ps[0:z - a, 6, 4 * n:4 * n + 4], rows[:, 0, a:z], ident[0:HEADS, 0:HEADS])
                for n in range(NT):
                    a, z = J[1 + n]
                    mm = nc.tensor.transpose(ps[:, 6, 12 + 4 * n:16 + 4 * n], rows[:, 3, a:z], ident[0:HEADS, 0:HEADS])
                mm.then_inc(S["a_turned"], 1)

            def turn_v(e):
                pe.wait_ge(S["v_ev"], e + 1)
                if e == 0:
                    pe.wait_ge(S["gate_ev"], 2)
                else:
                    pe.wait_ge(S["v_copied"], e)
                for n, (a, z) in enumerate(J):
                    mm = nc.tensor.transpose(ps[0:z - a, 7, n * P:(n + 1) * P], vr[:, e % 2, a:z], ident)
                mm.then_inc(S["v_turned"], 1)

            def scores(h):
                if h == 0:
                    pe.wait_ge(S["a_copied"], 1)
                    pe.wait_ge(S["v_copied"], 8)
                else:
                    pe.wait_ge(S["e_done"], h)
                    pe.wait_ge(S["num_copied"], NT * h)
                pe.wait_ge(S["silu_done"], 5 + h)
                for n, (tile, masked) in enumerate(((1, True), (2, False), (1, False), (2, True))):
                    a, z = J[tile]
                    o = ps[:, 5, n * P:(n + 1) * P]
                    nc.tensor.matmul(o, sel[:, h, :], rows[:, 2, a:z], start=True, stop=not masked)
                    if masked:
                        nc.tensor.matmul(o, ident, cst[:, C_MASK:C_MASK + P], start=False, stop=True)
                q, k = qkT[:, h], qkT[:, HEADS + h]
                nc.tensor.matmul(ps[:, 6, 0:SEQ], k[:, META:META + P], q[:, META:TOK], start=True, stop=True)
                nc.tensor.matmul(ps[:, 6, SEQ:SEQ + P], k[:, META + P:TOK], q[:, META + P:TOK], start=True, stop=True)
                nc.tensor.matmul(ps[0:META, 7, 0:SEQ], k[:, 0:META], q[:, META:TOK], start=True, stop=True)\
                    .then_inc(S["cs_done"], 1)

            def numerators(h, t):
                pe.wait_ge(S["p_done"], h + 1)
                if h == 0:
                    pe.wait_ge(pool_step, 1)
                if h or t:
                    pe.wait_ge(S["num_copied"], NT * h + t)
                o = ps[:, 7, 0:DV + 1]
                nc.tensor.matmul(o, pp[0:META, 384 + t * P:384 + (t + 1) * P], vtk[0:META, 0, h, :], start=True, stop=False)
                mm = nc.tensor.matmul(o, pp[:, t * P:(t + 1) * P], vtk[:, 1, h, :], start=False, stop=(t == 0))
                if t:
                    mm = nc.tensor.matmul(o, pp[:, 256:384], vtk[:, 2, h, :], start=False, stop=True)
                mm.then_inc(S["num_done"], 1)

            for b in range(B_Q, B_GLU):
                stream(b, 0 if b < B_GS else META)
                s = (b - 4) // 2
                if b % 2 == 0 and s < NS5:
                    s5_in(s)
                    if s:
                        s5_out(s - 1)
                if b == 36:
                    s5_out(NS5 - 1)
                if b == 8:
                    turn_gates()
                if 13 <= b < 21:
                    turn_v(b - 13)
                if b in (23, 27, 31, 35):
                    scores((b - 23) // 4)
                if b in (25, 29, 33, 37):
                    numerators((b - 25) // 4, 0)
                if b in (26, 30, 34, 38):
                    numerators((b - 26) // 4, 1)

            for m in range(KD):
                h, half = m // 2, m % 2
                if m == 0:
                    pe.wait_ge(S["hnorm"], NT * HEADS)
                if m >= 2:
                    pe.wait_ge(S["h_gated"], m - 1)
                for t in range(NT):
                    mm = nc.tensor.transpose(ps[:, 5 + m % 2, t * P:(t + 1) * P], hraw[:, t, h, half * P:(half + 1) * P], ident)
                mm.then_inc(S["h_turned"], 1)

            pe.wait_ge(S["y_lo"], CH)
            for b in range(B_GLU, B_MOUT):
                evacuated(b)
                split_ready(b)
                for half in range(2):
                    mm = product(ps[:, b % 2, half * SEQ:(half + 1) * SEQ], SEQ, b % RING,
                                 [(4 * half + k, gh[:, k, :], gl[:, k, :]) for k in range(CH)])
                mm.then_inc(blk_done, 1)
            pe.wait_ge(S["hm_lo"], KD)
            for b in range(B_MOUT, B_WO):
                stream(b, META)
            pe.wait_ge(S["mix_lo"], KD)
            def mean_of(m):
                pe.wait_ge(S["wo_ev"], m + 1)
                mm = nc.tensor.matmul(ps[:, 6, 0:SEQ], ones, res[:, m, META:TOK], start=(m == 0), stop=(m == KD - 1))
                if m == KD - 1:
                    mm.then_inc(NORM["mean"], 1)

            for b in range(B_WO, B_F1):
                evacuated(b)
                split_ready(b)
                product(ps[:, b % 2], SEQ, b % RING, [(k, mh[:, k, :], ml[:, k, :]) for k in range(KD)]).then_inc(blk_done, 1)
                if b > B_WO:
                    mean_of(b - B_WO - 1)
            mean_of(KD - 1)

            def sum_squares(tag, bank, n=KD, per=1):
                for m in range(n):
                    pe.wait_ge(*norm(tag, "sq", m // per + 1))
                    mm = nc.tensor.matmul(ps[:, bank, 0:SEQ], ones, sq[:, m, :], start=(m == 0), stop=(m == n - 1))
                mm.then_inc(NORM["var"], 1)

            def block(b, bank, name, value, t=0, h=xh, l=xl, first=META, order=range(KD), ready=None):
                if name:
                    pe.wait_ge(S[name], value)
                pe.wait_ge(lo_dve, t + (b + 1 - N_POOL))
                k = 0
                for n in order:
                    if ready:
                        pe.wait_ge(*ready(n))
                    a, z = h[:, n, first:first + SEQ], l[:, n, first:first + SEQ]
                    w_hi, w_lo = (w[:, b % RING, n * P:(n + 1) * P] for w in (wh, wl))
                    for w, x in ((w_hi, a), (w_hi, z), (w_lo, a)):
                        mm = nc.tensor.matmul(ps[:, bank, 0:SEQ], w, x, start=(k == 0), stop=(k == 3 * KD - 1))
                        k += 1
                mm.then_inc(blk_done, 1)

            def down(b, j, name, value, t=0, first=False, last=False):
                pe.wait_ge(lo_dve, t + (b + 1 - N_POOL))
                pe.wait_ge(S[name], value)
                for m in range(KD):
                    o = ps[:, 2 + m // 2, (m % 2) * SEQ:(m % 2 + 1) * SEQ]
                    w_hi, w_lo = (w[:, b % RING, m * P:(m + 1) * P] for w in (wh, wl))
                    for n, (w, x) in enumerate(((w_hi, gh), (w_hi, gl), (w_lo, gh))):
                        mm = nc.tensor.matmul(o, w, x[:, j % 4, :], start=(first and m % 2 == 0 and n == 0),
                                              stop=(last and n == 2), skip_group_check=True)
                mm.then_inc(blk_done, 1)

            def modulation(p_, i=0):
                pe.wait_ge(S["ada_used"], i * 16 + (p_ + 1) * 8)
                if p_:
                    pe.wait_ge(S["mod_done"], i * 2 + p_)
                for m in range(KD):
                    mm = nc.tensor.matmul(ps[:, 7, m:m + 1], ada_acc[:, p_, m * P:(m + 1) * P], cst[:, C_ONE_:C_ONE_ + 1],
                                          start=True, stop=True)
                mm.then_inc(S["mod_mm"], 1)

            sum_squares("n1", 7, per=2)
            pe.wait_ge(S["wo_ev"], KD)
            block(B_F1, 0, None, 0, ready=lambda n: norm("n1", "lo", n // 2 + 1))

            def pair(j, i=0):
                if j >= 2:
                    block(B_F1 - 1 + 2 * j, j % 2, "f_relu", i * 8 + (j - 1), i * 16)
                else:
                    block(B_F1 - 1 + 2 * j, j % 2, None, 0, i * 16)
                down(B_F1 + 2 * j, j - 1, "f_lo", i * 8 + j, i * 16, first=(j == 1))

            for j in range(1, LOOP1_PAIR):
                pair(j)
            with pe.Fori(0, 3) as i:
                for q in range(8):
                    pair(LOOP1_PAIR + q, i)
                    if q == 5:
                        modulation(0, i)
                    if q == 7:
                        modulation(1, i)
            down(B_F1 + 2 * KF - 1, KF - 1, "f_lo", KF, last=True)

            for g in range(4):
                pe.wait_ge(S["f1_res"], g + 1)
                for m in (2 * g, 2 * g + 1):
                    mm = nc.tensor.matmul(ps[:, 6, 0:SEQ], ones, res[:, m, META:TOK], start=(m == 0), stop=(m == KD - 1))
            mm.then_inc(NORM["mean"], 1)
            sum_squares("n2", 7, per=2)
            pe.wait_ge(S["mixing_landed"], 64)
            for n in range(2):
                for q in range(4):
                    mm = nc.tensor.transpose(ps[:, 2 + n, q * P:(q + 1) * P], ws[:, 4 * n + q, :], ident)
                mm.then_inc(S["ws_turned"], 1)
            sum_squares("r1", 6, per=2)

            def zv_stat(m):
                pe.wait_ge(S["zv_sq"], m + 1)
                if m == 0:
                    pe.wait_ge(*norm("r1", "std"))
                nc.tensor.matmul(ps[:, 6 + m // 2, (m % 2) * SEQ:(m % 2 + 1) * SEQ], cst[:, C_BLK:C_BLK + P], sq[:, m, :],
                                 start=True, stop=True).then_inc(S["zv_ms"], 1)

            def q_stat(t):
                pe.wait_ge(S["q_ev"], t + 1)
                if t:
                    pe.wait_ge(S["q_std"], t)
                else:
                    pe.wait_ge(S["ws_copied"], 2)
                nc.tensor.matmul(ps[:, 2, 0:SEQ], cst[:, C_BLK:C_BLK + P], qs[:, t % 2, :], start=True, stop=True)\
                    .then_inc(S["q_stat"], 1)
                bank3(lambda: nc.tensor.matmul(ps[:, 3, 0:SEQ], cst[:, C_ROT:C_ROT + P], qg[:, t % 2, :], start=True, stop=True))

            uses = [0]

            def bank3(make):
                if uses[0]:
                    pe.wait_ge(S["b3_free"], uses[0])
                make().then_inc(S["b3_full"], 1)
                uses[0] += 1

            def turn_zv():
                pe.wait_ge(S["zv_n"], 1)
                for c in range(NT):
                    for m in range(QT):
                        mm = nc.tensor.transpose(ps[:, 4 + c, m * P:(m + 1) * P], zv[:, m, c * P:(c + 1) * P], ident)
                    mm.then_inc(S["zv_turned"], 1)

            def turn_v2():
                pe.wait_ge(S["v2_ev"], 1)

                def make():
                    for c in range(NT):
                        mm = nc.tensor.transpose(ps[:, 3, c * P:(c + 1) * P], vv[:, c * P:(c + 1) * P], ident)
                    return mm
                bank3(make)

            def swap_k():
                pe.wait_ge(S["qk_ready"], 1)
                bank3(lambda: nc.tensor.matmul(ps[:, 3, 0:SEQ], cst[:, C_SWAP:C_SWAP + P], kf[:, 0, :], start=True, stop=True))

            def mix_tokens():
                pe.wait_ge(S["zv_copied"], NT)
                for m in range(QT):
                    for c in range(NT):
                        for g in range(2):
                            o = ps[64 * g:64 * g + 64, 6 + m // 2, (m % 2) * SEQ + c * P:(m % 2) * SEQ + (c + 1) * P]
                            mm = nc.tensor.matmul(o, zvt[:, c, m * P + 64 * g:m * P + 64 * g + 64], wst[:, 2 * m + g, :],
                                                  start=True, stop=True)
                mm.then_inc(S["mixed"], 1)

            for b in range(B_IN2, B_OUT2):
                n = b - B_IN2
                if n < 2:
                    pe.wait_ge(*norm("n2", "d", 4))
                    block(b, b % 2, None, 0, ready=(lambda q: norm("r1", "lo", q // 2 + 1)) if n == 0 else None)
                elif n < 10:
                    block(b, b % 2, *(("zv_sq", n - 1) if n < 6 else ("zu_ev", n - 5)))
                elif n == 10:
                    block(b, b % 2, "q_ev", 1)
                elif n == 11:
                    block(b, b % 2, "v2_ev", 1)
                else:
                    block(b, b % 2, "q_ev", n - 10)
                if 1 <= n < 5:
                    zv_stat(n - 1)
                if n == 9:
                    q_stat(0)
                if n == 10:
                    turn_zv()
                    turn_v2()
                if n == 11:
                    swap_k()
                    q_stat(1)
                if n == 12:
                    mix_tokens()
                    q_stat(2)
                if n == 13:
                    q_stat(3)
            q_stat(4)

            def scores2(h):
                r, qt = 64 * (h % 2), h // 2
                pe.wait_ge(S["qk_ready"], 2 + qt)
                if h == 0:
                    pe.wait_ge(S["b3_free"], 3)
                if h < 2:
                    pe.wait_ge(S["tok_pre"], 1)
                else:
                    pe.wait_ge(S["exp_done"], h - 1)
                k = kf[r:r + 64, 0 if h // 4 == h % 2 else 1, :]
                for t in range(NT):
                    mm = nc.tensor.matmul(ps[:, 6 + h % 2, t * SEQ:(t + 1) * SEQ], qf[r:r + 64, qt, t * P:(t + 1) * P], k,
                                          start=True, stop=True)
                mm.then_inc(S["s_done"], 1)

            def turn_probs(h):
                pe.wait_ge(S["prob_done"], h + 1)
                if h < 2:
                    pe.wait_ge(S["zv_copied"], NT)
                else:
                    pe.wait_ge(S["pt_copied"], h - 1)
                for s in range(NT):
                    for t in range(NT):
                        mm = nc.tensor.transpose(ps[:, 4 + h % 2, s * SEQ + t * P:s * SEQ + (t + 1) * P],
                                                 prob[:, h % 2, t, s * P:(s + 1) * P], ident)
                mm.then_inc(S["pt_done"], 1)

            def weigh_v(h):
                pe.wait_ge(S["pt_copied"], h + 1)
                r, qt, kv = 64 * (h % 2), h // 2, h // 4
                if h % 2 == 0:
                    if qt >= 2:
                        pe.wait_ge(S["ao_done"], qt - 1)
                    else:
                        pe.wait_ge(S["q_ev"], 4 + qt)
                for s in range(NT):
                    mm = nc.tensor.matmul(ps[r:r + 64, qt % 2, 0:SEQ], vtok[:, s, 64 * kv:64 * kv + 64],
                                          probt[:, h % 2, s, :], start=(s == 0), stop=(s == NT - 1))
                mm.then_inc(S["o_done"], 1)

            for h in range(AH + 2):
                if h < AH:
                    scores2(h)
                if 1 <= h <= AH:
                    turn_probs(h - 1)
                if h >= 2:
                    weigh_v(h - 2)
                if h == 4:
                    for m in range(QT):
                        pe.wait_ge(S["tok_sq"], 1)
                        mm = nc.tensor.matmul(ps[:, 3, 0:SEQ], ones, sq[:, 4 + m, :], start=(m == 0), stop=(m == QT - 1))
                    mm.then_inc(S["branch_ms"], 1)
            for m in range(QT):
                pe.wait_ge(S["att_sq"], m + 1)
                mm = nc.tensor.matmul(ps[:, 2, 0:SEQ], ones, sq[:, m, :], start=(m == 0), stop=(m == QT - 1))
            mm.then_inc(S["branch_ms"], 1)

            for b in range(B_OUT2, B_F2):
                n = b - B_OUT2
                ready = (lambda q: (S["branch_lo"], q - 3 if q >= QT else QT + q + 1)) if n == 0 else None
                block(b, b % 2, *(("ao_done", QT) if n < 2 else ("out2_ev", n - 1)), h=mh, l=ml, first=0,
                      order=(4, 5, 6, 7, 0, 1, 2, 3), ready=ready)
            sum_squares("r2", 6)

            def up2(j, i=0, ready=None):
                t = i * 12
                b = B_F2 + (0 if j == 0 else 3 * j - 1)
                block(b, 0, *(("ff2_ca", i * 4 + j) if j else ("out2_ev", KD)), t, ready=ready)
                block(b + 1, 1, *(("ff2_cb", i * 4 + j) if j else ("out2_ev", KD)), t)

            def triple(j, i=0):
                up2(j, i)
                down(B_F2 + 3 * j + 1, j - 1, "ff2_lo", i * 4 + j, i * 12, first=(j == 1))

            up2(0, ready=lambda q: norm("r2", "lo", q // 2 + 1))
            for j in range(1, LOOP2_TRIPLE):
                triple(j)
            with pe.Fori(0, (KF2 - LOOP2_TRIPLE) // 4) as i:
                for q in range(4):
                    triple(LOOP2_TRIPLE + q, i)
            down(NBLK - 1, KF2 - 1, "ff2_lo", KF2, last=True)

            for m in range(KD):
                pe.wait_ge(S["fin_sq"], m + 1)
                mm = nc.tensor.matmul(ps[:, 6, 0:SEQ], ones, sq[:, m, :], start=(m == 0), stop=(m == KD - 1))
            mm.then_inc(S["fin_ms"], 1)
            for n in range(4):
                t, half = n // 2, n % 2
                for m in range(4 * half, 4 * half + 4):
                    pe.wait_ge(S["fin_f"], m + 1)
                    mm = nc.tensor.transpose(ps[:, 2 + n, (m % 4) * P:(m % 4 + 1) * P], tg_m[:, m, t * P:(t + 1) * P], ident)
                mm.then_inc(S["fin_turned"], 1)

        @block.scalar
        def _(act):
            step = Steps(act, act_step)
            act.dma_start(cols[:, :], A["cols"]).then_inc(S["cols_landed"], 16)
            act.dma_start(xt[0][0:META, :], A["meta_tokens"]).then_inc(S["meta_landed"], 16)
            act.dma_start(cst[:, :], A["consts"]).then_inc(S["consts_landed"], 16)
            act.dma_start(s5m[:, :, :, :], A["s5_mats"]).then_inc(S["s5m_landed"], 16)
            act.dma_start(wg[:, :, :], A["w_gates"]).then_inc(S["gates_landed"], 16)
            act.dma_start(bg[:, :], A["b_gates"]).then_inc(S["gates_landed"], 16)
            act.dma_start(sel[:, :, :], A["sel"]).then_inc(S["gates_landed"], 16)

            def hi(b, t=0):
                if isinstance(b, int) and isinstance(t, int) and b + t >= NBLK:
                    return
                act.wait_ge(landed[b % RING], t * (16 // RING) + 16 * (b // RING + 1))
                if b >= RING:
                    act.wait_ge(blk_done, t + (b - RING + 1))
                nc.scalar.activation(wh[:, b % RING], raw[:, b % RING], ACT.Identity).then_inc(hi_done, 1)

            act.wait_ge(S["cols_landed"], 16)
            nc.scalar.activation(sv[:, 0], span("log_dt"), ACT.Exp).then_inc(S["dt_done"], 1)
            act.wait_ge(S["phase_done"], 1)
            nc.scalar.activation(sv[:, 3], sv[:, 1], ACT.Tanh, scale=0.5).then_inc(S["half_done"], 1)
            hi(0)
            hi(1)
            act.wait_ge(S["ln0_var"], 1)
            nc.scalar.activation(lnr[:, :, 0], lnr[:, :, 1], ACT.Sqrt).then_inc(S["ln0_std"], 1)
            hi(2)
            for k in range(KD):
                act.wait_ge(S["ln0_turned"], k + 1)
                for dst, s_ in ((res, "ln0_h"), (xh, "ln0_hi")):
                    nc.scalar.activation(dst[:, k, :], ps[:, 2 + k % 2, 0:TOK], ACT.Identity, bias=col("ln0_b", k),
                                         scale=col("ln0_g", k)).then_inc(S[s_], 1)

            def tables():
                act.wait_ge(S["phase_done"], 2)
                nc.scalar.activation(sv[:, 6], sv[:, 5], ACT.Sin, scale=HALF_TURN).then_inc(S["half_done"], 1)
                for q in range(4):
                    act.wait_ge(S["phase_done"], 2 + q)
                    s = slice(4 * q, 4 * q + 4)
                    nc.scalar.activation(tab[:, s, 1, :], tab[:, s, 1, :], ACT.Sin, scale=2 * HALF_TURN).then_inc(S["tables_done"], 1)
                    nc.scalar.activation(tab[:, s, 0, :], tab[:, s, 0, :], ACT.Sin, bias=cst_half_pi, scale=-2 * HALF_TURN)\
                        .then_inc(S["tables_done"], 1)

            cst_half_pi = hb[:, 51:52]

            def gate_rows():
                act.wait_ge(S["gates_landed"], 48)
                for g in range(2):
                    act.wait_ge(S["gate_mm"], g + 1)
                    nc.scalar.activation(rows[:, g, :], ps[0:HEADS, 6 + g, 0:TOK], ACT.Identity, bias=bg[:, g:g + 1])\
                        .then_inc(S["gate_ev"], 1)
                act.wait_ge(S["abs_f"], 1)
                step(nc.scalar.activation(rows[:, 2, :], rows[:, 2, :], ACT.Exp, scale=-1.0))
                nc.scalar.activation(rows[:, 2, :], rows[:, 2, :], ACT.Ln, bias=1.0).then_inc(S["ln_done"], 1)

            def evac(b):
                if b >= B_GLU:
                    return
                act.wait_ge(blk_done, b + 1)
                p_ = ps[:, b % 2, 0:TOK]
                if b < B_Q:
                    nc.scalar.activation(uT[:, b, :], p_, ACT.Identity, bias=col("b_in", b)).then_inc(S["u_ev"], 1)
                elif b < B_V:
                    t = b - B_Q
                    if t == 0:
                        act.wait_ge(S["cleared"], 2)
                    nc.scalar.activation(qkT[:, t, 3:], p_, ACT.Identity, bias=col("b_in", b)).then_inc(S["qk_ev"], 1)
                elif b < B_GS:
                    e = b - B_V
                    if e >= 2:
                        act.wait_ge(S["v_turned"], e - 1)
                    nc.scalar.activation(vr[:, e % 2, :], p_, ACT.Identity, bias=col("b_in", b)).then_inc(S["v_ev"], 1)
                else:
                    first, dst, name = ((B_GS, tg_s, "gs_ev"), (B_O, tg_o, "o_ev"), (B_GM, tg_m, "gm_ev"))[(b - B_GS) // 8]
                    if b == B_GM:
                        act.wait_ge(S["s5_x"], NS5)
                    nc.scalar.activation(dst[:, b - first, :], ps[:, b % 2, 0:SEQ], ACT.Tanh, bias=hb[:, b - B_GS:b - B_GS + 1],
                                         scale=0.5).then_inc(S[name], 1)

            def silu(t):
                act.wait_ge(S["conv_done"], t + 1)
                nc.scalar.activation(qkT[:, t, 0:TOK], cv[:, t % 2, :], ACT.Silu).then_inc(S["silu_done"], 1)

            def v_copy(e):
                h, half = e // 2, e % 2
                act.wait_ge(S["v_turned"], e + 1)
                step(nc.scalar.copy(vtk[0:META, 0, h, half * P:(half + 1) * P], ps[0:META, 7, 0:P]))
                nc.scalar.copy(vtk[:, 1:3, h, half * P:(half + 1) * P],
                               ps[:, 7, P:3 * P].rearrange("p (j e) -> p j e", j=2)).then_inc(S["v_copied"], 1)

            def decay(h):
                act.wait_ge(S["cs_done"], h + 1)
                if h == 0:
                    act.wait_ge(S["a_copied"], 1)
                else:
                    act.wait_ge(S["p_done"], h)
                nc.scalar.activation(ee[:, 0:256], ps[:, 5, 0:256], ACT.Exp, bias=aT[:, 1, h:h + 1])
                nc.scalar.activation(ee[:, 256:384], ps[:, 5, 384:512], ACT.Exp, bias=aT[:, 2, h:h + 1])
                for t, a in ((0, 256), (1, 128)):
                    ins = nc.scalar.activation(ee[0:META, 384 + t * P:384 + (t + 1) * P], ps[0:META, 5, a:a + P], ACT.Exp,
                                               bias=aT[0:META, 0, h:h + 1])
                ins.then_inc(S["e_done"], 1)

            def num_copy(h, t):
                act.wait_ge(S["num_done"], NT * h + t + 1)
                nc.scalar.copy(hraw[:, t, h, :], ps[:, 7, 0:DV + 1]).then_inc(S["num_copied"], 1)

            for b in range(B_U, B_GLU):
                if b in (24, 28, 32, 36):
                    decay((b - 24) // 4)
                if b in (26, 30, 34, 38):
                    num_copy((b - 26) // 4, 0)
                if b in (27, 31, 35, 39):
                    num_copy((b - 27) // 4, 1)
                hi(b + AHEAD)
                evac(b)
                if b == 2:
                    tables()
                if b == 3:
                    gate_rows()
                    for n, bt in enumerate((btr, bti)):
                        act.wait_ge(S["z_turned"], n + 1)
                        nc.scalar.copy(bt[:, :, :].rearrange("p c q -> p (c q)"), ps[:, 2 + n, :]).then_inc(S["bt_done"], 1)
                if b == 9:
                    act.wait_ge(S["a_turned"], 1)
                    nc.scalar.activation(floor[:, :, :].rearrange("p t h -> p (t h)"), ps[:, 6, 12:20], ACT.Exp)\
                        .then_inc(S["floor_done"], 1)
                if b >= 10 and b % 2 == 0 and (b - 10) // 2 < 8:
                    silu((b - 10) // 2)
                if 14 <= b < 22:
                    v_copy(b - 14)

            act.wait_ge(S["hvar"], 1)
            nc.scalar.activation(hsm[:, 1], hsm[:, 1], ACT.Sqrt).then_inc(S["hstd"], 1)
            for c in range(CH):
                act.wait_ge(S["y_sum"], c + 1)
                nc.scalar.activation(gh[:, c, :], y_s(c), ACT.Gelu_apprx_tanh).then_inc(S["y_hi"], 1)
                act.wait_ge(S["y_hi"], c + 1)
                nc.scalar.activation(y_s(c), y_s(c), ACT.Gelu_apprx_tanh).then_inc(S["y_act"], 1)

            def gate_heads(m):
                act.wait_ge(S["h_gated"], m + 1)
                if m == 0:
                    act.wait_ge(blk_done, B_GLU)
                nc.scalar.activation(xh[:, m, META:TOK], tg_o[:, m, :], ACT.Identity, scale=col("m_norm_g", m)).then_inc(S["hm_hi"], 1)
                act.wait_ge(S["hm_hi"], m + 1)
                nc.scalar.activation(tg_o[:, m, :], tg_o[:, m, :], ACT.Identity, scale=col("m_norm_g", m)).then_inc(S["hm_f"], 1)

            for b in range(B_GLU, B_MOUT):
                hi(b + AHEAD)
                gate_heads(b - B_GLU)
                act.wait_ge(blk_done, b + 1)
                j = b - B_GLU
                if j >= 2:
                    act.wait_ge(S["glu_ev"], j - 1)
                nc.scalar.activation(tz[:, j % 2, :], ps[:, b % 2, SEQ:2 * SEQ], ACT.Tanh, scale=0.5).then_inc(S["glu_t"], 1)
            for b in range(B_MOUT, B_WO):
                hi(b + AHEAD)
                m = b - B_MOUT
                act.wait_ge(S["mout_ev"], m + 1)
                nc.scalar.activation(mh[:, m, :], tg_s[:, m, :], ACT.Identity).then_inc(S["mix_hi"], 1)
            for b in range(B_WO, B_F1):
                hi(b + AHEAD)

            act.wait_ge(blk_done, B_F1)
            act.wait_ge(S["wo_ev"], KD)
            act.wait_ge(S["mix_lo"], KD)
            act.dma_start(rope[:, :, :], A["rope"]).then_inc(S["mixing_landed"], 16)
            act.dma_start(ws[:, :, :], A["w_s"]).then_inc(S["mixing_landed"], 16)
            for g in range(2):
                act.dma_start(bs[64 * g:64 * g + 64, :, :],
                              A["b_s"][None, g::2, :].to_broadcast([64, QT, P])).then_inc(S["mixing_landed"], 16)
            nc.scalar.activation(sc[:, :], span("c"), ACT.Silu).then_inc(S["silu_c"], 1)

            def squares(tag, src, what):
                for g in range(4):
                    act.wait_ge(*norm(tag, what, g + 1))
                    nc.scalar.activation(sq[:, 2 * g:2 * (g + 1), :], src[:, 2 * g:2 * (g + 1), :], ACT.Square)\
                        .then_inc(NORM["sq"], 1)

            def deviation(tag, bank, eps_col, scale=1.0):
                act.wait_ge(*norm(tag, "var"))
                nc.scalar.activation(std[:, :], ps[:, bank, 0:SEQ], ACT.Sqrt, bias=eps_col, scale=scale)\
                    .then_inc(NORM["std"], 1)

            def high_parts(tag, src):
                for g in range(4):
                    act.wait_ge(*norm(tag, "h", 2 * g + 2))
                    nc.scalar.activation(xh[:, 2 * g:2 * g + 2, META:TOK], src[:, 2 * g:2 * g + 2, :], ACT.Identity)\
                        .then_inc(NORM["hi"], 1)

            y = res[:, :, META:TOK]
            squares("n1", y, "d")
            deviation("n1", 7, eps[:, 0:1])
            high_parts("n1", y)

            def relu_block(b, j, t=0, i=0):
                act.wait_ge(blk_done, t + (b + 1))
                if j >= 2:
                    act.wait_ge(S["f_lo"], i * 8 + (j - 1))
                bias = cols[:, bass.ds(i * 8 + (COLS["b_up"][0] + j), 1)]
                nc.scalar.activation(relu[:, j % 2, :], ps[:, j % 2, 0:SEQ], ACT.Relu, bias=bias).then_inc(S["f_relu"], 1)
                act.wait_ge(S["f_relu"], i * 8 + (j + 1))
                nc.scalar.activation(gh[:, j % 4, :], relu[:, j % 2, :], ACT.Square).then_inc(S["f_hi"], 1)

            hi(B_F1 + AHEAD)
            relu_block(B_F1, 0)

            def pair(j, i=0):
                b, t = B_F1 - 1 + 2 * j, i * 16
                hi(b + AHEAD, t)
                relu_block(b, j, t, i)
                hi(b + 1 + AHEAD, t)

            for j in range(1, LOOP1_PAIR):
                pair(j)
            with act.Fori(0, 3) as i:
                for q in range(8):
                    pair(LOOP1_PAIR + q, i)
            hi(B_F1 + 2 * KF - 1 + AHEAD)

            squares("n2", y, "d")
            deviation("n2", 7, eps[:, 1:2])
            for g in range(4):
                act.wait_ge(*norm("n2", "h", 2 * g + 2))
                if g == 0:
                    act.wait_ge(*norm("n2", "var"))
                nc.scalar.activation(sq[:, 2 * g:2 * g + 2, :], y[:, 2 * g:2 * g + 2, :], ACT.Square).then_inc(NORM["sq"], 1)
            for n in range(2):
                act.wait_ge(S["ws_turned"], n + 1)
                nc.scalar.copy(wst[:, 4 * n:4 * n + 4, :].rearrange("p h q -> p (h q)"), ps[:, 2 + n, :]).then_inc(S["ws_copied"], 1)
            deviation("r1", 6, eps[:, 2:3])
            high_parts("r1", tg_m)

            def q_post(t):
                act.wait_ge(S["q_stat"], t + 1)
                if t >= 2:
                    act.wait_ge(S["qk_ready"], t - 1)
                nc.scalar.activation(qstd[:, t % 2, :], ps[:, 2, 0:SEQ], ACT.Sqrt, bias=eps[:, 2:3]).then_inc(S["q_std"], 1)

            for b in range(B_IN2, B_OUT2):
                n = b - B_IN2
                hi(b + AHEAD)
                if n >= 12:
                    q_post(n - 11)
                act.wait_ge(blk_done, b + 1)
                p_ = ps[:, b % 2, 0:SEQ]
                if n < 4:
                    nc.scalar.activation(zv[:, n, :], p_, ACT.Gelu_apprx_tanh).then_inc(S["zv_ev"], 1)
                    act.wait_ge(S["zv_ev"], n + 1)
                    if n == 0:
                        act.wait_ge(*norm("r1", "var"))
                    nc.scalar.activation(sq[:, n, :], zv[:, n, :], ACT.Square).then_inc(S["zv_sq"], 1)
                elif n < 8:
                    nc.scalar.activation(zu[:, n - 4, :], p_, ACT.Gelu_apprx_tanh).then_inc(S["zu_ev"], 1)
                elif n == 9:
                    nc.scalar.copy(vv[:, :], p_).then_inc(S["v2_ev"], 1)
                else:
                    t = 0 if n == 8 else n - 9
                    if t >= 2:
                        act.wait_ge(S["qk_ready"], t - 1)
                        act.wait_ge(S["b3_full"], t + 1)
                    nc.scalar.activation(qs[:, t % 2, :], p_, ACT.Square)
                    nc.scalar.activation(qg[:, t % 2, :], p_, ACT.Identity, scale=col("g_q" if t else "g_k"))\
                        .then_inc(S["q_ev"], 1)
                if n == 8:
                    act.wait_ge(S["zv_ms"], QT)
                    nc.scalar.activation(zst[:, :, :].rearrange("p m t -> p (m t)"),
                                         ps[:, 6:8, :].rearrange("p a b -> p (a b)"), ACT.Sqrt, bias=eps[:, 2:3])\
                        .then_inc(S["zv_std"], 1)
                if n == 10:
                    q_post(0)
                if n == 11:
                    for c in range(NT):
                        act.wait_ge(S["zv_turned"], c + 1)
                        nc.scalar.copy(zvt[:, c, :], ps[:, 4 + c, :]).then_inc(S["zv_copied"], 1)
            q_post(3)
            q_post(4)
            act.wait_ge(S["tok_done"], 1)
            nc.scalar.activation(sq[:, 4:8, :], zu[:, :, :], ACT.Square).then_inc(S["tok_sq"], 1)

            def exps(h):
                act.wait_ge(S["max_done"], h + 1)
                if h >= 2:
                    act.wait_ge(S["pt_done"], h - 1)
                for t in range(NT):
                    nc.scalar.activation(prob[:, h % 2, t, :], ps[:, 6 + h % 2, t * SEQ:(t + 1) * SEQ], ACT.Exp,
                                         bias=smax[:, h, 1, t:t + 1], scale=HD ** -0.5,
                                         accum_out=ssum[:, h, t:t + 1]).then_inc(act_step, 1)
                    step.n += 1
                act.wait_ge(act_step, step.n)
                act.sem_inc(S["exp_done"], 1)

            def probt_copy(h):
                act.wait_ge(S["pt_done"], h + 1)
                if h >= 2:
                    act.wait_ge(S["o_done"], h - 1)
                nc.scalar.copy(probt[:, h % 2, :, :].rearrange("p s t -> p (s t)"), ps[:, 4 + h % 2, :]).then_inc(S["pt_copied"], 1)

            for h in range(AH + 1):
                if h < AH:
                    exps(h)
                if h >= 1:
                    probt_copy(h - 1)
            for m in range(QT):
                act.wait_ge(S["ao_done"], m + 1)
                nc.scalar.activation(sq[:, m, :], ao[:, m, :], ACT.Square).then_inc(S["att_sq"], 1)
            act.wait_ge(S["branch_ms"], 1)
            nc.scalar.activation(rstd2[:, :], ps[:, 3, 0:SEQ], ACT.Sqrt, bias=eps[:, 2:3], scale=2.0).then_inc(S["branch_std"], 1)
            act.wait_ge(S["branch_ms"], 2)
            nc.scalar.activation(std[:, :], ps[:, 2, 0:SEQ], ACT.Sqrt, bias=eps[:, 2:3], scale=2.0).then_inc(S["branch_std"], 1)
            for n, (src, base) in enumerate(((zu, QT), (ao, 0))):
                for m in range(QT):
                    act.wait_ge(S["branch_f"], n * QT + m + 1)
                    nc.scalar.activation(mh[:, base + m, :], src[:, m, :], ACT.Identity).then_inc(S["branch_hi"], 1)

            for b in range(B_OUT2, B_F2):
                hi(b + AHEAD)
                m = b - B_OUT2
                act.wait_ge(S["out2_ev"], m + 1)
                nc.scalar.activation(sq[:, m, :], y[:, m, :], ACT.Square).then_inc(NORM["sq"], 1)
            deviation("r2", 6, eps[:, 2:3])
            high_parts("r2", tg_m)

            def taps(j, i, which):
                dst, bank, off = ((ca, 0, 0), (cb, 1, KF2))[which]
                b = B_F2 + (0 if j == 0 else 3 * j - 1) + which
                act.wait_ge(blk_done, i * 12 + (b + 1))
                if j >= 2:
                    act.wait_ge(S["ff2_g"], i * 4 + (j - 1))
                w, bias = (cols[:, bass.ds(i * 4 + (COLS[n][0] + o + off + j), 1)] for n, o in (("conv2_w", 2 * KF2), ("conv2_b", 0)))
                nc.scalar.activation(dst[:, j % 2, :], ps[:, bank, 0:SEQ], ACT.Identity, bias=bias, scale=w)\
                    .then_inc(S["ff2_b" if which else "ff2_a"], 1)

            def silu2(j, i):
                act.wait_ge(S["ff2_ca"], i * 4 + (j + 1))
                nc.scalar.activation(ca[:, j % 2, :], ca[:, j % 2, :], ACT.Silu).then_inc(S["ff2_silu"], 1)

            def high2(j, i):
                act.wait_ge(S["ff2_g"], i * 4 + (j + 1))
                nc.scalar.activation(gh[:, j % 4, :], cg[:, j % 2, :], ACT.Identity).then_inc(S["ff2_hi"], 1)

            def triple(j, i=0):
                b, t = B_F2 + 3 * j - 1, i * 12
                hi(b + AHEAD, t)
                high2(j - 1, i)
                taps(j, i, 0)
                hi(b + 1 + AHEAD, t)
                taps(j, i, 1)
                silu2(j, i)
                hi(b + 2 + AHEAD, t)

            hi(B_F2 + AHEAD)
            taps(0, 0, 0)
            hi(B_F2 + 1 + AHEAD)
            taps(0, 0, 1)
            silu2(0, 0)
            for j in range(1, LOOP2_TRIPLE):
                triple(j)
            with act.Fori(0, (KF2 - LOOP2_TRIPLE) // 4 - 1) as i:
                for q in range(4):
                    triple(LOOP2_TRIPLE + q, i)
            for q in range(KF2 - 4, KF2):
                triple(q)
            high2(KF2 - 1, 0)

            for m in range(KD):
                act.wait_ge(S["f2_res"], m + 1)
                nc.scalar.activation(sq[:, m, :], y[:, m, :], ACT.Square).then_inc(S["fin_sq"], 1)
            act.wait_ge(S["fin_ms"], 1)
            nc.scalar.activation(std[:, :], ps[:, 6, 0:SEQ], ACT.Sqrt, bias=eps[:, 2:3]).then_inc(S["fin_std"], 1)
            for n in range(4):
                t, half = n // 2, n % 2
                act.wait_ge(S["fin_turned"], n + 1)
                nc.scalar.copy(ob[:, t, half * 512:(half + 1) * 512], ps[:, 2 + n, :]).then_inc(S["fin_copied"], 1)

        @block.vector
        def _(dve):
            step = Steps(dve, dve_step)
            V = nc.vector

            def lo(b, t=0):
                if isinstance(t, int) and b + t >= NBLK:
                    return
                dve.wait_ge(hi_done, t + (b + 1))
                V.tensor_tensor(wl[:, b % RING], raw[:, b % RING], wh[:, b % RING].bitcast(F32), ALU.subtract).then_inc(lo_dve, 1)

            dve.wait_ge(S["cols_landed"], 16)
            dve.wait_ge(S["dt_done"], 1)
            step(V.tensor_tensor(sv[:, 2], span("lam_im"), sv[:, 0], ALU.mult))
            V.tensor_tensor(sv[:, 1], span("lam_re"), sv[:, 0], ALU.mult).then_inc(S["phase_done"], 1)
            step(V.tensor_scalar(sv[:, 4], sv[:, 2], 1.0 / TWO_PI, ROUND, ALU.mult, ALU.add))
            step(V.tensor_scalar(sv[:, 4], sv[:, 4], ROUND, None, ALU.subtract))
            for part in (PI_A, PI_B, PI_C):
                step(V.scalar_tensor_tensor(sv[:, 2], sv[:, 4], -part, sv[:, 2], ALU.mult, ALU.add))
            step(V.tensor_scalar(sv[:, 5], sv[:, 2], 1.0 / TWO_PI, None, ALU.mult))
            V.tensor_scalar(hb[:, 0:24], cols[:, 20:44], 0.5, None, ALU.mult)
            V.memset(hb[:, 51:52], TWO_PI / 4)
            V.memset(eps[:, 0:1], 16 * LN_EPS)
            V.memset(eps[:, 1:2], LN_EPS)
            V.memset(eps[:, 2:3], RMS_EPS)
            step(V.memset(lnr[:, :, :], 1.0))

            for n, name in ((1, "x_landed"), (2, "x2_landed"), (0, "meta_landed")):
                r = META if n == 0 else P
                dve.wait_ge(S[name], 16)
                for q in range(2):
                    V.bn_stats(lnst[0:r, n, q, :], xt[n][0:r, q * 512:(q + 1) * 512]).then_inc(dve_step, 1)
                step.n += 2
                dve.wait_ge(dve_step, step.n)
                step(V.bn_aggr(lnmv[0:r, n, :], lnst[0:r, n, :, :].rearrange("p a b -> p (a b)")))
                ins = V.tensor_scalar(lnr[0:r, n, 1:2], lnmv[0:r, n, 1:2], LN_EPS, None, ALU.add)
            ins.then_inc(S["ln0_var"], 1)
            dve.wait_ge(S["ln0_std"], 1)
            step(V.reciprocal(lnr[:, :, 0], lnr[:, :, 0]))
            for n in (1, 2, 0):
                r = META if n == 0 else P
                V.tensor_scalar(xt[n][0:r, :], xt[n][0:r, :], lnmv[0:r, n, 0:1], lnr[0:r, n, 0:1], ALU.subtract, ALU.mult)\
                    .then_inc(S["ln0_norm"], 1)

            dve.wait_ge(S["consts_landed"], 16)
            for q in range(4):
                s = slice(4 * q, 4 * q + 4)
                u, f = tab[:, s, 0, :], tab[:, s, 1, :]
                tmp = swork[:, :, :]
                step(V.tensor_tensor(u, cst[:, None, C_T:C_T + TOK].to_broadcast([P, 4, TOK]),
                                     sv[:, 5, s, None].to_broadcast([P, 4, TOK]), ALU.mult))
                step(V.tensor_scalar(tmp, u, ROUND, ROUND, ALU.add, ALU.subtract))
                step(V.tensor_tensor(f, u, tmp, ALU.subtract))
                V.scalar_tensor_tensor(u, f, -1.0, f, ALU.mult, ALU.max).then_inc(S["phase_done"], 1)
                dve.wait_ge(S["phase_done"], q + 2)

            dve.wait_ge(S["half_done"], 1)
            step(V.tensor_scalar(sv[:, 7], sv[:, 3], -1.0, 1.0, ALU.mult, ALU.add))
            step(V.reciprocal(sv[:, 7], sv[:, 7]))
            step(V.scalar_tensor_tensor(sv[:, 8], sv[:, 3], 2.0, sv[:, 7], ALU.mult, ALU.mult))
            step(V.tensor_scalar(sv[:, 9], sv[:, 8], 1.0, None, ALU.add))
            dve.wait_ge(S["half_done"], 2)
            step(V.tensor_tensor(sv[:, 10], sv[:, 6], sv[:, 6], ALU.mult))
            dve.wait_ge(S["tables_done"], 8)
            step(V.tensor_tensor(sv[:, 11], sv[:, 8], tab[:, :, 0, 1], ALU.mult))
            step(V.scalar_tensor_tensor(sv[:, 11], sv[:, 10], -2.0, sv[:, 11], ALU.mult, ALU.add))
            step(V.tensor_tensor(sv[:, 12], sv[:, 9], tab[:, :, 1, 1], ALU.mult))
            lr, li = span("lam_re"), span("lam_im")
            step(V.tensor_tensor(sv[:, 13], lr, lr, ALU.mult))
            step(V.tensor_tensor(sv[:, 14], li, li, ALU.mult))
            step(V.tensor_tensor(sv[:, 13], sv[:, 13], sv[:, 14], ALU.add))
            step(V.reciprocal(sv[:, 13], sv[:, 13]))
            step(V.tensor_tensor(sv[:, 14], sv[:, 11], lr, ALU.mult))
            step(V.tensor_tensor(sv[:, 15], sv[:, 12], li, ALU.mult))
            step(V.tensor_tensor(sv[:, 14], sv[:, 14], sv[:, 15], ALU.add))
            step(V.tensor_tensor(sv[:, 14], sv[:, 14], sv[:, 13], ALU.mult))
            step(V.tensor_tensor(sv[:, 15], sv[:, 12], lr, ALU.mult))
            step(V.tensor_tensor(sv[:, 16], sv[:, 11], li, ALU.mult))
            step(V.tensor_tensor(sv[:, 15], sv[:, 15], sv[:, 16], ALU.subtract))
            step(V.tensor_tensor(sv[:, 15], sv[:, 15], sv[:, 13], ALU.mult))
            dve.wait_ge(S["s5m_landed"], 16)
            dve.wait_ge(S["cleared"], 1)
            fr, fi = (sv[:, n, :, None].to_broadcast([P, NS5, S5H]) for n in (14, 15))
            w = [sA.rearrange("p a t -> p (a t)")[:, 0:256].rearrange("p (s h) -> p s h", s=NS5),
                 sB.rearrange("p a t -> p (a t)")[:, 0:256].rearrange("p (s h) -> p s h", s=NS5)]
            for z, (x0, x1), op in ((zre, (fr, fi), ALU.subtract), (zim, (fi, fr), ALU.add)):
                step(V.tensor_tensor(w[0], s5m[:, 0], x0, ALU.mult))
                step(V.tensor_tensor(w[1], s5m[:, 1], x1, ALU.mult))
                for g in range(2):
                    ins = V.tensor_tensor(z[64 * g:64 * g + 64, :, S5H * g:S5H * (g + 1)], w[0][64 * g:64 * g + 64],
                                          w[1][64 * g:64 * g + 64], op)
                    if z is zre:
                        step(ins)
                    elif g:
                        ins.then_inc(S["z_done"], 1)
            for c_part, n in ((cbr, 2), (cbi, 3)):
                for g in range(2):
                    ins = V.tensor_copy(c_part[64 * g:64 * g + 64, :, S5H * g:S5H * (g + 1)], s5m[64 * g:64 * g + 64, n])
            ins.then_inc(S["c_done"], 1)

            def gate_rows():
                dve.wait_ge(S["gate_ev"], 2)
                V.scalar_tensor_tensor(rows[:, 2, :], rows[:, 1, :], -1.0, rows[:, 1, :], ALU.mult, ALU.max).then_inc(S["abs_f"], 1)
                step(V.tensor_scalar(rows[:, 1, :], rows[:, 1, :], 0.0, None, ALU.min))
                dve.wait_ge(S["ln_done"], 1)
                step(V.tensor_tensor(rows[:, 1, :], rows[:, 1, :], rows[:, 2, :], ALU.subtract))
                one = cst[0:HEADS, C_ONE_:C_ONE_ + 1].to_broadcast([HEADS, TOK])
                step(V.tensor_tensor_scan(rows[:, 3, :], one, rows[:, 1, :], 0.0, ALU.mult, ALU.add))
                step(V.tensor_tensor(rows[:, 0, :], rows[:, 0, :], rows[:, 3, :], ALU.subtract))
                step(V.tensor_tensor_scan(rows[:, 2, :], rows[:, 0, :], rows[:, 0, :], 0.0, ALU.max, ALU.max))
                step(V.scalar_tensor_tensor(rows[:, 3, :], rows[:, 3, :], -1.0, rows[:, 2, :], ALU.mult, ALU.subtract))
                V.tensor_scalar(rows[:, 2, :], rows[:, 2, :], -1.0, None, ALU.mult).then_inc(S["rows_done"], 1)

            def scan(s):
                dve.wait_ge(S["s5_in"], s + 1)
                bu, cs, sc = ps[:, 2:4, 0:TOK], tab[:, s, 0:2, :], tab[:, s, ::-1, :]
                V.tensor_tensor(sA, bu, cs, ALU.mult).then_inc(dve_step, 1)
                V.tensor_tensor(sB, bu, sc, ALU.mult).then_inc(S["s5_free"], 1)
                step.n += 1
                dve.wait_ge(dve_step, step.n)
                dve.wait_ge(S["s5_free"], s + 1)
                V.tensor_tensor(sA[:, 0, :], sA[:, 0, :], sA[:, 1, :], ALU.add).then_inc(dve_step, 1)
                V.tensor_tensor(sB[:, 0, :], sB[:, 1, :], sB[:, 0, :], ALU.subtract).then_inc(dve_step, 1)
                step.n += 2
                dve.wait_ge(dve_step, step.n)
                r = sv[:, 9, s:s + 1].to_broadcast([P, TOK])
                V.tensor_tensor_scan(zz[:, 0, :], r, sA[:, 0, :], 0.0, ALU.mult, ALU.add).then_inc(dve_step, 1)
                V.tensor_tensor_scan(zz[:, 1, :], r, sB[:, 0, :], 0.0, ALU.mult, ALU.add).then_inc(dve_step, 1)
                step.n += 2
                dve.wait_ge(dve_step, step.n)
                z = zz[:, :, META:TOK]
                V.tensor_tensor(sP[:, :, :], z, cs[:, :, META:TOK], ALU.mult).then_inc(dve_step, 1)
                V.tensor_tensor(sQ[:, :, :], z, sc[:, :, META:TOK], ALU.mult).then_inc(dve_step, 1)
                step.n += 2
                dve.wait_ge(dve_step, step.n)
                if s >= 2:
                    dve.wait_ge(S["s5_y"], s - 1)
                V.tensor_tensor(xst[:, s % 2, 0, :], sP[:, 0, :], sP[:, 1, :], ALU.subtract)
                V.scalar_tensor_tensor(xst[:, s % 2, 1, :], sQ[:, 0, :], -1.0, sQ[:, 1, :], ALU.mult, ALU.subtract)\
                    .then_inc(S["s5_x"], 1)

            def y_sum(c):
                dve.wait_ge(S["s5_y"], 4 * c + 4)
                V.scalar_tensor_tensor(y_s(c), y_s(c), col("s5_d", c), ps[:, 4, 0:SEQ], ALU.mult, ALU.add).then_inc(S["y_sum"], 1)

            def conv(t):
                dve.wait_ge(S["qk_ev"], t + 1)
                if t >= 2:
                    dve.wait_ge(S["silu_done"], t - 1)
                a = cv[:, t % 2, :]
                step(V.tensor_scalar(a, qkT[:, t, 3:3 + TOK], col("conv_w", 8 * 3 + t), col("conv_b", t), ALU.mult, ALU.add))
                for w_ in range(2, -1, -1):
                    ins = V.scalar_tensor_tensor(a, qkT[:, t, w_:w_ + TOK], col("conv_w", 8 * w_ + t), a, ALU.mult, ALU.add)
                    if w_:
                        step(ins)
                ins.then_inc(S["conv_done"], 1)

            def weigh(h):
                dve.wait_ge(S["e_done"], h + 1)
                if h:
                    dve.wait_ge(S["num_done"], NT * h)
                sc = DK ** -0.5
                V.scalar_tensor_tensor(pp[:, 0:384], ps[:, 6, 0:384], sc, ee[:, 0:384], ALU.mult, ALU.mult)
                V.scalar_tensor_tensor(pp[0:META, 384:640], ps[0:META, 7, 0:SEQ], sc, ee[0:META, 384:640], ALU.mult, ALU.mult)\
                    .then_inc(S["p_done"], 1)

            def head_stat(h):
                for t in range(NT):
                    dve.wait_ge(S["num_copied"], NT * h + t + 1)
                    step(V.bn_stats(hst[:, :], hraw[:, t, h, 0:DV]))
                    step(V.bn_aggr(hmv[:, t, h, :], hst[:, :]))

            gate_rows()
            for s in range(NS5):
                scan(s)
                if s % 4 == 0 and s:
                    y_sum(s // 4 - 1)
                if s == 3:
                    dve.wait_ge(S["floor_done"], 1)
                    V.tensor_copy(aT[0:META, 0, :], ps[0:META, 6, 0:4])
                    V.tensor_copy(aT[:, 1:3, :].rearrange("p j h -> p (j h)"), ps[:, 6, 4:12]).then_inc(S["a_copied"], 1)
                if 2 <= s < 10:
                    conv(s - 2)
                if s in (10, 12, 14):
                    head_stat((s - 10) // 2)
                if s in (9, 11, 13, 15):
                    weigh((s - 9) // 2)

            head_stat(HEADS - 1)
            dve.wait_ge(S["num_copied"], NT * HEADS)
            den, var = hraw[:, :, :, DV], hmv[:, :, :, 1]
            step(V.scalar_tensor_tensor(hsm[:, 0], den, -1.0, den, ALU.mult, ALU.max))
            dve.wait_ge(S["floor_done"], 1)
            step(V.tensor_tensor(hsm[:, 0], hsm[:, 0], floor[:, :, :], ALU.max))
            step(V.reciprocal(hsm[:, 0], hsm[:, 0]))
            step(V.tensor_tensor(hsm[:, 1], var, hsm[:, 0], ALU.mult))
            step(V.tensor_tensor(hsm[:, 1], hsm[:, 1], hsm[:, 0], ALU.mult))
            V.tensor_scalar(hsm[:, 1], hsm[:, 1], LN_EPS, None, ALU.add).then_inc(S["hvar"], 1)
            dve.wait_ge(S["hstd"], 1)
            step(V.reciprocal(hsm[:, 1], hsm[:, 1]))
            step(V.tensor_tensor(hsm[:, 1], hsm[:, 1], hsm[:, 0], ALU.mult))
            for h in range(HEADS):
                for t in range(NT):
                    V.tensor_scalar(hraw[:, t, h, 0:DV], hraw[:, t, h, 0:DV], hmv[:, t, h, 0:1], hsm[:, 1, t, h:h + 1],
                                    ALU.subtract, ALU.mult).then_inc(S["hnorm"], 1)
            y_sum(CH - 1)
            for m in range(KD):
                dve.wait_ge(S["h_turned"], m + 1)
                dve.wait_ge(S["o_ev"], m + 1)
                V.scalar_tensor_tensor(tg_o[:, m, :], tg_o[:, m, :], 1.0, ps[:, 5 + m % 2, 0:SEQ], ALU.add, ALU.mult)\
                    .then_inc(S["h_gated"], 1)

            for b in range(B_GLU, B_MOUT):
                if b + AHEAD >= N_POOL:
                    lo(b + AHEAD)
                j = b - B_GLU
                dve.wait_ge(S["glu_t"], j + 1)
                if j == 0:
                    dve.wait_ge(S["gs_ev"], KD)
                V.scalar_tensor_tensor(tw[:, j % 2, :], tz[:, j % 2, :], 1.0, ps[:, b % 2, 0:SEQ], ALU.add, ALU.mult)\
                    .then_inc(S["glu_ev"], 1)
                dve.wait_ge(S["glu_ev"], j + 1)
                step(V.scalar_tensor_tensor(tg_s[:, j, :], tg_s[:, j, :], 1.0, tw[:, j % 2, :], ALU.add, ALU.mult))
            for b in range(B_MOUT, B_WO):
                lo(b + AHEAD)
                m = b - B_MOUT
                dve.wait_ge(blk_done, b + 1)
                if m == 0:
                    dve.wait_ge(S["gm_ev"], KD)
                step(V.scalar_tensor_tensor(tw[:, m % 2, :], tg_m[:, m, :], 1.0, ps[:, b % 2, 0:SEQ], ALU.add, ALU.mult))
                V.tensor_tensor(tg_s[:, m, :], tg_s[:, m, :], tw[:, m % 2, :], ALU.add).then_inc(S["mout_ev"], 1)
            for b in range(B_WO, B_F1):
                lo(b + AHEAD)
                m = b - B_WO
                dve.wait_ge(blk_done, b + 1)
                V.scalar_tensor_tensor(res[:, m, META:TOK], res[:, m, META:TOK], 4 * ALPHA, ps[:, b % 2, 0:SEQ],
                                       ALU.mult, ALU.add).then_inc(S["wo_ev"], 1)

            y = res[:, :, META:TOK]

            def centre(tag):
                dve.wait_ge(*norm(tag, "mean"))
                for g in range(4):
                    V.tensor_tensor(y[:, 2 * g:2 * g + 2, :], y[:, 2 * g:2 * g + 2, :],
                                    ps[:, 6:7, 0:SEQ].to_broadcast([P, 2, SEQ]), ALU.subtract).then_inc(NORM["d"], 1)

            def scaled(tag, dst, g_of, b_of):
                dve.wait_ge(*norm(tag, "std"))
                step(V.reciprocal(rstd[:, :], std[:, :]))
                for m in range(KD):
                    step(V.tensor_tensor(dst[:, m, :], y[:, m, :], rstd[:, :], ALU.mult))
                    V.tensor_scalar(dst[:, m, :], dst[:, m, :], g_of(m), b_of(m), ALU.mult, ALU.add).then_inc(NORM["h"], 1)

            centre("n1")
            scaled("n1", y, lambda m: col("ln1_g", m), lambda m: col("ln1_b", m))

            def ada(n, t=0):
                k, acc = n % KD, ada_acc[:, n // KD, :]
                dve.wait_ge(ada_landed[n % ADA_RING], t * (16 // ADA_RING) + 16 * (n // ADA_RING + 1))
                if n and n % KD:
                    dve.wait_ge(S["ada_used"], t + n)
                w = ada_w[:, n % ADA_RING]
                if k == 0:
                    ins = V.tensor_scalar(acc, w, sc[:, 0:1], None, ALU.mult)
                else:
                    ins = V.scalar_tensor_tensor(acc, w, sc[:, k:k + 1], acc, ALU.mult, ALU.add)
                ins.then_inc(S["ada_used"], 1)

            def mod_out(p_, i):
                dve.wait_ge(S["mod_mm"], i * 2 + (p_ + 1))
                V.tensor_tensor(mod[:, bass.ds(i * 16 + p_ * KD, KD)], ps[:, 7, 0:KD],
                                cols[:, bass.ds(i * 16 + (COLS["b_ada"][0] + p_ * KD), KD)], ALU.add).then_inc(S["mod_done"], 1)

            lo(B_F1 + AHEAD)
            for j in range(1, LOOP1_PAIR):
                lo(B_F1 - 1 + 2 * j + AHEAD)
                lo(B_F1 + 2 * j + AHEAD)
            dve.wait_ge(S["silu_c"], 1)
            with dve.Fori(0, 3) as i:
                n = 0
                for q in range(8):
                    b = B_F1 - 1 + 2 * (LOOP1_PAIR + q)
                    lo(b + AHEAD, i * 16)
                    lo(b + 1 + AHEAD, i * 16)
                    for _ in range(ADA_SHARE[q]):
                        ada(n, i * 16)
                        n += 1
                    if q == 6:
                        mod_out(0, i)
                mod_out(1, i)
            lo(B_F1 + 2 * KF - 1 + AHEAD)
            dve.wait_ge(S["mod_done"], NMOD)
            for n, (at, name) in enumerate(((M_SC1, "g_norm1"), (M_SC2, "g_norm2"))):
                step(V.scalar_tensor_tensor(gain[:, n, :], mod[:, at:at + KD], 1.0, span(name), ALU.add, ALU.mult))

            dve.wait_ge(blk_done, B_IN2)
            for g in range(4):
                V.scalar_tensor_tensor(y[:, 2 * g:2 * g + 2, :], y[:, 2 * g:2 * g + 2, :], ALPHA,
                                       ps[:, 2 + g, :].rearrange("p (a t) -> p a t", a=2), ALU.mult, ALU.add)\
                    .then_inc(S["f1_res"], 1)
            dve.wait_ge(S["f1_res"], 4)
            centre("n2")
            scaled("n2", y, lambda m: col("ln2_g", m), lambda m: col("ln2_b", m))
            dve.wait_ge(*norm("n2", "h", KD))
            scaled("r1", tg_m, lambda m: gain[:, 0, m:m + 1], lambda m: mod[:, M_SH1 + m:M_SH1 + m + 1])

            reads = [0]

            def bank3_read(last):
                last.then_inc(S["b3_free"], 1)
                reads[0] += 1

            def q_finish(t):
                dst = qf[:, t - 1, :] if t else kf[:, 0, :]
                dve.wait_ge(S["b3_full"], reads[0] + 1)
                if t == 0:
                    dve.wait_ge(S["mixing_landed"], 64)
                bank3_read(V.tensor_tensor(qrot[:, :], ps[:, 3, 0:SEQ], rope[:, 1, :], ALU.mult))
                step(V.tensor_tensor(dst, qg[:, t % 2, :], rope[:, 0, :], ALU.mult))
                dve.wait_ge(S["b3_free"], reads[0])
                step(V.tensor_tensor(dst, dst, qrot[:, :], ALU.add))
                dve.wait_ge(S["q_std"], t + 1)
                step(V.reciprocal(qstd[:, t % 2, :], qstd[:, t % 2, :]))
                V.tensor_tensor(dst, dst, qstd[:, t % 2, :], ALU.mult).then_inc(S["qk_ready"], 1)

            for b in range(B_IN2, B_OUT2):
                n = b - B_IN2
                lo(b + AHEAD)
                if n == 9:
                    dve.wait_ge(S["zv_std"], 1)
                    step(V.reciprocal(zst[:, :, :], zst[:, :, :]))
                    V.scalar_tensor_tensor(zv[:, :, :], zv[:, :, :], col("g_tok_v"), zst[:, :, :], ALU.mult, ALU.mult)\
                        .then_inc(S["zv_n"], 1)
                if n == 10:
                    q_finish(0)
                if n == 11:
                    dve.wait_ge(S["b3_full"], reads[0] + 1)
                    bank3_read(V.tensor_copy(vtok[:, :, :].rearrange("p s e -> p (s e)"), ps[:, 3, 0:SEQ]))
                if n == 12:
                    dve.wait_ge(S["b3_full"], reads[0] + 1)
                    bank3_read(V.tensor_copy(kf[:, 1, :], ps[:, 3, 0:SEQ]))
                    q_finish(1)
                if n == 13:
                    q_finish(2)
            dve.wait_ge(S["mixed"], 1)
            dve.wait_ge(S["mixing_landed"], 64)
            for m in range(QT):
                ins = V.tensor_tensor(zv[:, m, :].rearrange("p (c t) -> p c t", c=NT),
                                      ps[:, 6 + m // 2, (m % 2) * SEQ:(m % 2 + 1) * SEQ].rearrange("p (c t) -> p c t", c=NT),
                                      bs[:, m:m + 1, :].to_broadcast([P, NT, P]), ALU.add)
            ins.then_inc(S["tok_pre"], 1)
            dve.wait_ge(S["tok_pre"], 1)
            V.tensor_tensor(zu[:, :, :], zu[:, :, :], zv[:, :, :], ALU.mult).then_inc(S["tok_done"], 1)
            q_finish(3)
            q_finish(4)

            def maxima(h):
                dve.wait_ge(S["s_done"], h + 1)
                step(V.tensor_reduce(smax[:, h, 0, :], ps[:, 6 + h % 2, :].rearrange("p (t s) -> p t s", t=NT), AX.X, ALU.max))
                V.tensor_scalar(smax[:, h, 1, :], smax[:, h, 0, :], -HD ** -0.5, None, ALU.mult).then_inc(S["max_done"], 1)

            def normed(h):
                dve.wait_ge(S["exp_done"], h + 1)
                step(V.reciprocal(ssum[:, h, :], ssum[:, h, :]))
                for t in range(NT):
                    ins = V.tensor_scalar(prob[:, h % 2, t, :], prob[:, h % 2, t, :], ssum[:, h, t:t + 1], None, ALU.mult)
                ins.then_inc(S["prob_done"], 1)

            def attended(m):
                dve.wait_ge(S["o_done"], 2 * m + 2)
                V.tensor_copy(ao[:, m, :], ps[:, m % 2, 0:SEQ]).then_inc(S["ao_done"], 1)

            for h in range(AH + 1):
                if h < AH:
                    maxima(h)
                if h:
                    normed(h - 1)
                if h >= 4 and h % 2 == 0:
                    attended(h // 2 - 2)
            attended(3)
            for n, (src, g_name, dev) in enumerate(((zu, "g_tok", rstd2), (ao, "g_attn", std))):
                dve.wait_ge(S["branch_std"], n + 1)
                step(V.reciprocal(dev[:, :], dev[:, :]))
                for m in range(QT):
                    V.scalar_tensor_tensor(src[:, m, :], src[:, m, :], col(g_name, m), dev[:, :], ALU.mult, ALU.mult)\
                        .then_inc(S["branch_f"], 1)

            for b in range(B_OUT2, B_F2):
                lo(b + AHEAD)
                m = b - B_OUT2
                dve.wait_ge(blk_done, b + 1)
                V.scalar_tensor_tensor(y[:, m, :], ps[:, b % 2, 0:SEQ], mod[:, M_GT1 + m:M_GT1 + m + 1], y[:, m, :],
                                       ALU.mult, ALU.add).then_inc(S["out2_ev"], 1)
            dve.wait_ge(S["out2_ev"], KD)
            scaled("r2", tg_m, lambda m: gain[:, 1, m:m + 1], lambda m: mod[:, M_SH2 + m:M_SH2 + m + 1])

            def outer_taps(j, i, which):
                dst, bank, off = ((ca, 0, 0), (cb, 1, KF2))[which]
                done = S["ff2_cb" if which else "ff2_ca"]
                dve.wait_ge(S["ff2_b" if which else "ff2_a"], i * 4 + (j + 1))
                w0, w2 = (cols[:, bass.ds(i * 4 + (COLS["conv2_w"][0] + o * 2 * KF2 + off + j), 1)] for o in (0, 2))
                step(V.scalar_tensor_tensor(dst[:, j % 2, 1:SEQ], ps[:, bank, 0:SEQ - 1], w0, dst[:, j % 2, 1:SEQ], ALU.mult, ALU.add))
                V.scalar_tensor_tensor(dst[:, j % 2, 0:SEQ - 1], ps[:, bank, 1:SEQ], w2, dst[:, j % 2, 0:SEQ - 1], ALU.mult, ALU.add)\
                    .then_inc(done, 1)

            def triple(j, i=0):
                b, t = B_F2 + 3 * j - 1, i * 12
                lo(b + AHEAD, t)
                outer_taps(j, i, 0)
                lo(b + 1 + AHEAD, t)
                outer_taps(j, i, 1)
                lo(b + 2 + AHEAD, t)

            lo(B_F2 + AHEAD)
            outer_taps(0, 0, 0)
            lo(B_F2 + 1 + AHEAD)
            outer_taps(0, 0, 1)
            for j in range(1, LOOP2_TRIPLE):
                triple(j)
            with dve.Fori(0, (KF2 - LOOP2_TRIPLE) // 4 - 1) as i:
                step.enter(i, 8)
                for q in range(4):
                    triple(LOOP2_TRIPLE + q, i)
            step.leave((KF2 - LOOP2_TRIPLE) // 4 - 1)
            for j in range(KF2 - 4, KF2):
                triple(j)

            dve.wait_ge(blk_done, NBLK)
            for m in range(KD):
                V.scalar_tensor_tensor(y[:, m, :], ps[:, 2 + m // 2, (m % 2) * SEQ:(m % 2 + 1) * SEQ],
                                       mod[:, M_GT2 + m:M_GT2 + m + 1], y[:, m, :], ALU.mult, ALU.add).then_inc(S["f2_res"], 1)
            dve.wait_ge(S["fin_std"], 1)
            step(V.reciprocal(rstd[:, :], std[:, :]))
            for m in range(KD):
                V.scalar_tensor_tensor(tg_m[:, m, :], y[:, m, :], col("g_final", m), rstd[:, :], ALU.mult, ALU.mult)\
                    .then_inc(S["fin_f"], 1)

        @block.gpsimd
        def _(pool):
            G = nc.gpsimd
            for n, z in enumerate((zre, zim, cbr, cbi)):
                ins = G.memset(z[:, :, :], 0.0)
            ins.then_inc(S["cleared"], 1)
            G.memset(qkT[:, :, 0:3], 0.0).then_inc(S["cleared"], 1)

            def lo(b):
                pool.wait_ge(hi_done, b + 1)
                G.tensor_tensor(wl[:, b % RING], raw[:, b % RING], wh[:, b % RING].bitcast(F32), ALU.subtract).then_inc(lo_pool, 1)

            def hm_lo(m):
                pool.wait_ge(S["hm_f"], m + 1)
                G.tensor_tensor(xl[:, m, META:TOK], tg_o[:, m, :], xh[:, m, META:TOK].bitcast(F32), ALU.subtract)\
                    .then_inc(S["hm_lo"], 1)

            lo(0)
            lo(1)
            lo(2)
            for k in range(KD):
                pool.wait_ge(S["ln0_h"], k + 1)
                pool.wait_ge(S["ln0_hi"], k + 1)
                G.tensor_tensor(xl[:, k, :], res[:, k, :], xh[:, k, :].bitcast(F32), ALU.subtract).then_inc(S["ln0_lo"], 1)
            for b in range(3, N_POOL):
                lo(b)
                if b == 8:
                    pool.wait_ge(S["ln0_hi"], KD)
                    pool.wait_ge(S["ln0_turned"], KD)
                    G.memset(vtk[:, :, :, DV:DV + 1], 1.0).then_inc(pool_step, 1)
                if b == 46:
                    for c in range(CH):
                        pool.wait_ge(S["y_hi"], c + 1)
                        pool.wait_ge(S["y_act"], c + 1)
                        G.tensor_tensor(gl[:, c, :], y_s(c), gh[:, c, :].bitcast(F32), ALU.subtract).then_inc(S["y_lo"], 1)
                if b > 46:
                    hm_lo(b - 47)
            for m in range(5, KD):
                hm_lo(m)
            for m in range(KD):
                pool.wait_ge(S["mix_hi"], m + 1)
                pool.wait_ge(S["mout_ev"], m + 1)
                G.tensor_tensor(ml[:, m, :], tg_s[:, m, :], mh[:, m, :].bitcast(F32), ALU.subtract).then_inc(S["mix_lo"], 1)

            def low_parts(tag, src):
                for g in range(4):
                    s = slice(2 * g, 2 * g + 2)
                    pool.wait_ge(*norm(tag, "hi", g + 1))
                    G.tensor_tensor(xl[:, s, META:TOK], src[:, s, :], xh[:, s, META:TOK].bitcast(F32), ALU.subtract)\
                        .then_inc(NORM["lo"], 1)

            y = res[:, :, META:TOK]
            low_parts("n1", y)

            def square_low(j, i=0):
                pool.wait_ge(S["f_relu"], i * 8 + (j + 1))
                G.tensor_tensor(relu2[:, j % 2, :], relu[:, j % 2, :], relu[:, j % 2, :], ALU.mult).then_inc(pool_step, 1)
                pool.wait_ge(pool_step, i * 8 + (j + 2))
                pool.wait_ge(S["f_hi"], i * 8 + (j + 1))
                G.tensor_tensor(gl[:, j % 4, :], relu2[:, j % 2, :], gh[:, j % 4, :].bitcast(F32), ALU.subtract).then_inc(S["f_lo"], 1)

            for j in range(LOOP1_PAIR):
                square_low(j)
            with pool.Fori(0, 3) as i:
                for q in range(8):
                    square_low(LOOP1_PAIR + q, i)
            low_parts("r1", tg_m)
            for n, (src, base) in enumerate(((zu, QT), (ao, 0))):
                for m in range(QT):
                    pool.wait_ge(S["branch_hi"], n * QT + m + 1)
                    G.tensor_tensor(ml[:, base + m, :], src[:, m, :], mh[:, base + m, :].bitcast(F32), ALU.subtract)\
                        .then_inc(S["branch_lo"], 1)
            low_parts("r2", tg_m)

            def gated(j, i=0):
                pool.wait_ge(S["ff2_silu"], i * 4 + (j + 1))
                pool.wait_ge(S["ff2_cb"], i * 4 + (j + 1))
                G.tensor_tensor(cg[:, j % 2, :], ca[:, j % 2, :], cb[:, j % 2, :], ALU.mult).then_inc(S["ff2_g"], 1)

            def gated_low(j, i=0):
                pool.wait_ge(S["ff2_hi"], i * 4 + (j + 1))
                G.tensor_tensor(gl[:, j % 4, :], cg[:, j % 2, :], gh[:, j % 4, :].bitcast(F32), ALU.subtract).then_inc(S["ff2_lo"], 1)

            for j in range(LOOP2_TRIPLE):
                gated(j)
                gated_low(j)
            with pool.Fori(0, (KF2 - LOOP2_TRIPLE) // 4) as i:
                for q in range(4):
                    gated(LOOP2_TRIPLE + q, i)
                    gated_low(LOOP2_TRIPLE + q, i)


def _tiles(w):
    k, n = w.shape
    return w.reshape(k // P, P, n // P, P).transpose(2, 1, 0, 3).reshape(n // P, P, k)


def _cols(v):
    return v.reshape(-1, P).T


def kernel(**inputs):
    import numpy as np
    import concourse.bacc as bacc
    from concourse.bass_utils import run_bass_kernel_spmd

    I = {k: np.asarray(v) for k, v in inputs.items()}
    f = np.float32

    w_in = I["w_in"][0]
    gates_at = S5W + 2 * HEADS * DK + 2 * HEADS * DV
    o_at = S5W + 2 * HEADS * DK + HEADS * DV
    w1, w2 = I["w_in_2"][0], I["w_up_2"][0]
    glu = _tiles(I["s5_w_glu"][0])
    up, down = _tiles(I["w_up"][0]), I["w_down"][0].reshape(KF, P, D)
    up2, down2 = _tiles(w2), I["w_down_2"][0].reshape(KF2, P, D)
    t2 = _tiles(w1)
    ffn1 = np.concatenate([up[:1], np.stack([up[1:], down[:-1]], 1).reshape(-1, P, D), down[-1:]])
    ffn2 = np.concatenate([up2[:1], up2[KF2:KF2 + 1],
                           np.stack([up2[1:KF2], up2[KF2 + 1:], down2[:-1]], 1).reshape(-1, P, D), down2[-1:]])
    stream = np.concatenate([
        _tiles(w_in[:, :o_at]),
        _tiles(w_in[:, gates_at + 8:gates_at + 8 + D]),
        _tiles(w_in[:, o_at:gates_at]),
        _tiles(w_in[:, gates_at + 8 + D:]),
        np.concatenate([glu[:KD], glu[KD:]], 2),
        _tiles(I["m_w_out"][0]), _tiles(I["w_o"][0]), ffn1,
        t2[10:14], t2[6:10], t2[4:5], t2[5:6], t2[0:4],
        _tiles(I["w_out_2"][0]), ffn2])
    assert stream.shape == (NBLK, P, D)

    b_in = I["b_in"][0]
    b_main = np.concatenate([b_in[:o_at], b_in[gates_at + 8:gates_at + 8 + D], b_in[o_at:gates_at], b_in[gates_at + 8 + D:]])

    def states(v):
        return v.reshape((NS5, P) + v.shape[2:]).swapaxes(0, 1)

    twice = lambda v: np.concatenate([v, v])[:, None]
    vectors = {
        "b_in": _cols(b_main),
        "conv_w": np.concatenate([_cols(I["qk_conv_w"][0, n]) for n in range(4)], 1),
        "conv_b": _cols(I["qk_conv_b"][0]), "s5_d": _cols(I["s5_d"][0]),
        "ln0_g": _cols(I["ln0_g"]), "ln0_b": _cols(I["ln0_b"]),
        "ln1_g": _cols(I["ln1_g"][0]), "ln1_b": _cols(I["ln1_b"][0]), "b_up": _cols(I["b_up"][0]),
        "ln2_g": _cols(I["ln2_g"][0]), "ln2_b": _cols(I["ln2_b"][0]), "m_norm_g": _cols(I["m_norm_g"][0]),
        "lam_re": states(I["s5_lambda_re"][0]), "lam_im": states(I["s5_lambda_im"][0]),
        "log_dt": states(np.repeat(I["s5_log_dt"][0][:, None], S5P, 1)),
        "b_ada": _cols(I["b_ada_2"][0]), "g_norm1": _cols(I["g_norm1_2"][0]),
        "g_q": twice(I["g_q_2"][0]), "g_k": twice(I["g_k_2"][0]), "g_tok_v": twice(I["g_tok_v_2"][0]),
        "g_attn": _cols(I["g_attn_out_2"][0]), "g_tok": _cols(I["g_tok_out_2"][0]), "g_norm2": _cols(I["g_norm2_2"][0]),
        "conv2_w": np.concatenate([_cols(I["w_conv_2"][0, n]) for n in range(3)], 1),
        "conv2_b": _cols(I["b_conv_2"][0]), "g_final": _cols(I["g_final_2"]), "c": _cols(I["c_2"][0]),
    }
    cols = np.concatenate([vectors[n] for n in COLS], 1)
    s5_mats = np.stack([states(I["s5_b_re"][0]), states(I["s5_b_im"][0]),
                        states(I["s5_c_re"][0].transpose(0, 2, 1)), states(I["s5_c_im"][0].transpose(0, 2, 1))], 1)

    consts = np.zeros((P, NCONST), f)
    consts[:, C_ID:C_ID + P] = np.eye(P)
    consts[:, C_ONE:C_ONE + P] = 1.0 / D
    for g in range(2):
        consts[64 * g:64 * g + 64, C_BLK + 64 * g:C_BLK + 64 * g + 64] = 1.0 / HD
    for o in range(P):
        a = o % 32
        src, sign = (o + 16, -1.0) if a < 16 else (o - 16, 1.0)
        consts[src, C_ROT + o] = sign
        consts[(o + 64) % P, C_SWAP + o] = 1.0
    consts[:, C_MASK:C_MASK + P] = np.where(np.arange(P)[:, None] <= np.arange(P)[None, :], 0.0, -1e30)
    consts[:, C_T:C_T + TOK] = np.arange(TOK)
    consts[:, C_ONE_] = 1.0
    sel = np.zeros((HEADS, HEADS, P), f)
    for h in range(HEADS):
        sel[h, h] = 1.0
    n = np.arange(SEQ)
    inv = np.power(f(10000.0), -np.arange(0, 32, 2, dtype=f) / f(32)).astype(f)
    ar, ac = ((n // 64).astype(f)[:, None] * inv, (n % 64).astype(f)[:, None] * inv)
    ang = np.concatenate([ar, ar, ac, ac], 1).T
    rope = np.stack([np.concatenate([np.cos(ang)] * 2), np.concatenate([np.sin(ang)] * 2)], 1).astype(f)

    arrays = {
        "x": I["x"], "meta_tokens": I["meta_tokens"], "w_stream": stream, "cols": cols, "consts": consts,
        "s5_mats": s5_mats, "sel": sel, "rope": rope,
        "w_gates": w_in[:, gates_at:gates_at + 8].reshape(KD, P, 8).transpose(1, 0, 2),
        "b_gates": b_in[gates_at:gates_at + 8].reshape(2, HEADS).T,
        "w_ada": I["w_ada_2"][0].reshape(KD, P, NMOD, D).transpose(2, 0, 1, 3).reshape(NMOD * KD, P, D),
        "w_s": I["w_s_2"][0].transpose(1, 0, 2),
        "b_s": I["b_s_2"][0],
    }
    arrays = {k: np.ascontiguousarray(v) for k, v in arrays.items()}
    nc = bacc.Bacc("TRN2", target_bir_lowering=False, num_devices=1)
    A = {k: nc.dram_tensor(f"in_{k}", v.shape, mybir.dt.from_np(v.dtype), kind="ExternalInput").ap() for k, v in arrays.items()}
    out = nc.dram_tensor("out_0", (1, SEQ, D), F32, kind="ExternalOutput").ap()
    two_blocks(nc, A, out)
    r = run_bass_kernel_spmd(nc, [{f"in_{k}": v for k, v in arrays.items()}], core_ids=[0])
    return r.results[0]["out_0"]
```

```python
from contextlib import ExitStack

import concourse.bass as bass
from concourse import mybir

F32 = mybir.dt.float32
F32R = mybir.dt.float32r
ACT = mybir.ActivationFunctionType
ALU = mybir.AluOpType
AX = mybir.AxisListType

P = 128
D = 1024
KD = D // P
SEQ = 256
META = 16
TOK = SEQ + META
NT = SEQ // P
S5W, S5G, S5H, S5P = 512, 32, 16, 64
NS5 = S5G * S5P // P
CH = S5W // P
HEADS, DK, DV = 4, 128, 256
DFF = 4 * D
KF = DFF // P
DFF2 = 2816
KF2 = DFF2 // P
QT = 4
AH = 8
HD = 64
NMOD = 6
ALPHA = 2.0 ** 0.25
LN_EPS = 1e-5
RMS_EPS = 1e-6
TWO_PI = 6.283185307179586
HALF_TURN = 3.1415925
ROUND = 12582912.0
PI_A, PI_B, PI_C = 6.28125, 0.0019353071693331003, 1.0253131677018246e-11

RING = 4
AHEAD = 3
B_U, B_Q, B_K, B_V = 0, 4, 8, 12
B_GS, B_O, B_GM = 20, 28, 36
B_GLU, B_MOUT, B_WO = 44, 52, 60
B_F1 = 68
B_IN2 = B_F1 + 2 * KF
B_OUT2 = B_IN2 + 14
B_F2 = B_OUT2 + KD
NBLK = B_F2 + 3 * KF2
N_POOL = B_MOUT
LOOP1_PAIR = 8
ADA_RING = 4
ADA_SHARE = (1, 1, 1, 1, 2, 2, 0, 0)
ADA_LOOP = 3
SP_LOOP = B_F1 + 20
OUT_BANK = (0, 1, 2, 3)
GROUPS = ((0, 1), (1, 2), (2, 4), (4, 6), (6, 8))
GROUP_OF = (0, 1, 2, 2, 3, 3, 4, 4)
MIX_BANK = (2, 6, 7, 2)
POOL2 = (B_IN2 + AHEAD, B_F2)
LOOP2_TRIPLE = 6
M_SH1, M_SC1, M_GT1, M_SH2, M_SC2, M_GT2 = (n * KD for n in range(NMOD))

COLS = {}


def _layout_cols():
    at = 0
    for name, n in (("b_in", 44), ("conv_w", 32), ("conv_b", 8), ("s5_d", 4), ("ln0_g", 8), ("ln0_b", 8),
                    ("ln1_g", 8), ("ln1_b", 8), ("b_up", 32), ("ln2_g", 8), ("ln2_b", 8), ("m_norm_g", 8),
                    ("lam_re", 16), ("lam_im", 16), ("log_dt", 16), ("b_ada", 48), ("g_norm1", 8), ("g_q", 1),
                    ("g_k", 1), ("g_tok_v", 1), ("g_attn", 4), ("g_tok", 4), ("g_norm2", 8), ("conv2_w", 132),
                    ("conv2_b", 44), ("g_final", 8), ("c", 8)):
        COLS[name] = (at, n)
        at += n
    return at


NCOL = _layout_cols()
C_ID, C_ONE, C_BLK, C_ROT, C_SWAP, C_MASK, C_T = 0, 128, 256, 384, 512, 640, 768
C_ONE_ = C_T + TOK
NCONST = C_ONE_ + 1


def ada_rows(slot):
    at = (ADA_LOOP + 1) * KD
    if slot in (0, 1):
        return range(at + 2 * slot, at + 2 * slot + 2)
    if 8 <= slot < 12:
        return range(at + slot - 4, at + slot - 3)
    return range(0)


S5_AT = (4, 6, 8, 11, 13, 16, 18, 20, 22, 24, 26, 28, 30, 32, 34, 36)
CONV_AT = (2, 3, 4, 5, 6, 7, 9, 11)
SILU_AT = (12, 15, 17, 20, 22, 25, 29, 33)


class Steps:

    def __init__(self, eng, sem):
        self.eng, self.sem, self.n, self.at = eng, sem, 0, None

    def __call__(self, ins):
        ins.then_inc(self.sem, 1)
        self.n += 1
        self.eng.wait_ge(self.sem, self.n if self.at is None else self.at + self.n)

    def enter(self, i, per):
        self.base, self.per, self.at, self.n = self.n, per, i * per + self.n, 0

    def leave(self, turns):
        assert self.n == self.per, (self.n, self.per)
        self.n, self.at = self.base + turns * self.per, None


def two_blocks(nc: bass.Bass, A: dict, out: bass.AP):
    with ExitStack() as ctx:
        def sb(name, shape, dt=F32, scope=None):
            return (scope or ctx).enter_context(nc.sbuf_tensor(name, shape, dt))

        def sem(name):
            return ctx.enter_context(nc.semaphore(name))

        raw = sb("raw", [P, RING, 1024])
        wh = sb("wh", [P, RING, 1024], F32R)
        wl = sb("wl", [P, RING, 1024], F32R)
        xh = sb("xh", [P, KD, TOK], F32R)
        xl = sb("xl", [P, KD, TOK], F32R)
        res = sb("res", [P, KD, TOK])
        cols = sb("cols", [P, NCOL])
        cst = sb("cst", [P, NCONST])
        hb = sb("hb", [P, 52])
        mod = sb("mod", [P, NMOD * KD])
        eps = sb("eps", [P, 3])
        sc = sb("silu_c", [P, KD])
        std = sb("std", [P, SEQ])
        rstd2 = sb("rstd2", [P, SEQ])
        rstd = sb("rstd", [P, SEQ])

        tabs = ExitStack()
        tab = sb("tab", [P, NS5, 2, TOK], F32, tabs)
        tabs.close()
        att = ExitStack()
        prob = sb("prob", [P, 2, NT, SEQ], F32, att)
        probt = sb("probt", [P, 2, NT, SEQ], F32, att)
        att.close()
        gh = sb("gh", [P, 4, SEQ], F32R)
        gl = sb("gl", [P, 4, SEQ], F32R)
        tg_m = sb("tg_m", [P, KD, SEQ])
        mh = sb("mh", [P, KD, SEQ], F32R)
        ml = sb("ml", [P, KD, SEQ], F32R)
        rest_of_tab = sb("rest_of_tab", [P, NS5 * 2 * TOK - 2 * 4 * SEQ - 3 * KD * SEQ])

        ph1 = ExitStack()
        tg_s = sb("tg_s", [P, KD, SEQ], F32, ph1)
        tg_o = sb("tg_o", [P, KD, SEQ], F32, ph1)
        vtk = sb("vtk", [P, 3, HEADS, DV + 1], F32, ph1)
        qkT = sb("qkT", [P, 8, TOK + 3], F32, ph1)
        uT = sb("uT", [P, CH, TOK], F32, ph1)
        hraw = sb("hraw", [P, NT, HEADS, DV + 1], F32, ph1)
        swork = sb("swork", [P, 4, TOK], F32, ph1)
        sA, sB = swork[:, 0:2, :], swork[:, 2:4, :]
        zz = sb("zz", [P, 2, TOK], F32, ph1)
        xst = sb("xst", [P, 4, 2, SEQ], F32, ph1)
        cv = sb("cv", [P, 2, TOK], F32, ph1)
        vr = sb("vr", [P, 2, TOK], F32, ph1)
        ee = sb("ee", [P, 640], F32, ph1)
        pp = sb("pp", [P, 640], F32, ph1)
        rows = sb("rows", [HEADS, 4, TOK], F32, ph1)
        wg = sb("wg", [P, KD, 8], F32, ph1)
        bg = sb("bg", [HEADS, 2], F32, ph1)
        sel = sb("sel", [HEADS, HEADS, P], F32, ph1)
        aT = sb("aT", [P, 3, HEADS], F32, ph1)
        floor = sb("floor", [P, NT, HEADS], F32, ph1)
        hst = sb("hst", [P, 6], F32, ph1)
        hmv = sb("hmv", [P, NT, HEADS, 2], F32, ph1)
        hsm = sb("hsm", [P, 4, NT, HEADS], F32, ph1)
        early = hraw[:, :, :, :].rearrange("p t h e -> p (t h e)")
        s5m = early[:, 0:1024].rearrange("p (n s h) -> p n s h", n=4, s=NS5)
        zre = early[:, 1024:1536].rearrange("p (s h) -> p s h", s=NS5)
        zim = early[:, 1536:2048].rearrange("p (s h) -> p s h", s=NS5)
        btr = sb("btr", [P, CH, P], F32, ph1)
        bti = sb("bti", [P, CH, P], F32, ph1)
        cbr = sb("cbr", [P, NS5, 2 * S5H], F32, ph1)
        cbi = sb("cbi", [P, NS5, 2 * S5H], F32, ph1)
        sv = sb("sv", [P, 20, NS5], F32, ph1)
        xt = [vtk[:, :, :, :].rearrange("p a b c -> p (a b c)")[:, n * D:(n + 1) * D] for n in range(3)]
        lnst = sb("lnst", [P, 3, 2, 6], F32, ph1)
        lnmv = sb("lnmv", [P, 3, 2], F32, ph1)
        lnr = sb("lnr", [P, 3, 2], F32, ph1)
        swork_flat = swork[:, :, :].rearrange("p a t -> p (a t)")
        tz = swork_flat[:, 0:2 * SEQ].rearrange("p (a t) -> p a t", a=2)
        tw = swork_flat[:, 2 * SEQ:4 * SEQ].rearrange("p (a t) -> p a t", a=2)

        ph1.close()

        mods = ExitStack()
        ada_w = sb("ada_w", [P, ADA_RING, D], F32, mods)
        mods.close()
        ob = sb("ob", [P, NT, D])
        rest_of_ada = sb("rest_of_ada", [P, (ADA_RING - NT) * D])
        ada_acc = sb("ada_acc", [P, 3, D])
        ffn = ExitStack()
        relu = sb("relu", [P, 2, SEQ], F32, ffn)
        relu2 = sb("relu2", [P, 2, SEQ], F32, ffn)
        ffn.close()
        qs = sb("qs", [P, 3, SEQ])
        qg = sb("qg", [P, 3, SEQ])
        sq = sb("sq", [P, KD, SEQ])
        gain = sb("gain", [P, 2, KD])
        rope = sb("rope", [P, 2, SEQ])
        zv = sb("zv", [P, QT, SEQ])
        zu = sb("zu", [P, QT, SEQ])
        zms = sb("zms", [P, NT, AH])
        zvt = sb("zvt", [P, NT, QT * P])
        ws = sb("ws", [P, AH, P])
        wst = sb("wst", [P, AH, P])
        bs = sb("bs", [P, QT, P])
        qstd = sb("qstd", [P, 2, SEQ])
        qrot = sb("qrot", [P, SEQ])
        qf = sb("qf", [P, QT, SEQ])
        kf = sb("kf", [P, 2, SEQ])
        vv = sb("vv", [P, SEQ])
        vtok = sb("vtok", [P, NT, P])
        smax = sb("smax", [P, AH, 2, NT])
        ssum = sb("ssum", [P, AH, NT])
        ao = sb("ao", [P, QT, SEQ])
        ca = sb("ca", [P, 2, SEQ])
        cb = sb("cb", [P, 2, SEQ])
        cg = sb("cg", [P, 2, SEQ])

        ps = ctx.enter_context(nc.psum_tensor("ps", [P, 8, 512], F32))

        landed = [sem(f"block_landed_{r}") for r in range(RING)]
        hi_done, lo_pool, lo_dve, blk_done = sem("hi_done"), sem("lo_by_pool"), sem("lo_by_dve"), sem("block_done")
        act_step, dve_step, pool_step = sem("act_step"), sem("dve_step"), sem("pool_step")
        S = {n: sem(n) for n in (
            "x_landed", "x2_landed", "meta_landed", "cols_landed", "consts_landed", "gates_landed", "s5m_landed",
            "stored",
            "cleared", "ln0_var", "ln0_std", "ln0_norm", "ln0_turned", "ln0_h", "ln0_hi", "ln0_lo",
            "dt_done", "half_done", "phase_done", "tables_done", "z_done", "z_turned", "bt_done",
            "c_done", "gate_mm", "gate_ev", "abs_f", "ln_done", "rows_done", "a_turned", "a_copied", "floor_done",
            "u_ev", "qk_ev", "conv_done", "silu_done", "v_ev", "v_turned", "v_copied", "gs_ev", "o_ev", "gm_ev",
            "s5_in", "s5_free", "s5_x", "s5_y", "y_sum", "y_hi", "y_act", "y_lo",
            "cs_done", "e_done", "p_done", "num_done", "num_copied", "hvar", "hstd", "hnorm",
            "h_turned", "h_gated", "hm_f", "hm_hi", "hm_lo",
            "glu_t", "glu_ev", "mout_ev", "mix_hi", "mix_lo", "wo_ev",
            "ada_used", "mod_mm", "mod_done", "silu_c", "f_relu", "f_hi", "f_lo", "f1_res", "n1_pair",
            "mixing_landed", "ws_turned", "ws_copied",
            "zv_ev", "zv_act", "zv_turned", "zv_sq", "zv_copied", "zv_ms", "zv_std", "zv_n", "zu_ev", "zu_act", "mixed", "tok_pre", "tok_done",
            "q_ev", "q_stat", "q_std", "b3_full", "b3_free", "v2_ev", "qk_ready",
            "s_done", "max_done", "exp_done", "prob_done", "pt_done", "pt_copied", "o_done", "ao_done",
            "tok_sq", "att_sq", "branch_ms", "branch_std", "branch_f", "branch_hi", "branch_lo",
            "out2_ev", "ff2_a", "ff2_b", "ff2_ca", "ff2_cb", "ff2_silu", "ff2_g", "ff2_hi", "ff2_lo", "f2_res",
            "fin_sq", "fin_ms", "fin_std", "fin_rstd", "fin_f", "fin_turned", "fin_by_act", "fin_by_dve",
        )}

        NORM_BASE = {"mean": (0, 1), "d": (0, 4), "sq": (0, 4, 8, 12), "var": (0, 1, 2, 3), "std": (0, 1, 2, 3),
                     "h": (0, 8, 16, 24), "hi": (0, 5, 5, 10), "lo": (0, 5, 5, 10)}
        NORM = {what: sem(f"norm_{what}") for what in NORM_BASE}

        def norm(tag, what, n=1):
            return NORM[what], NORM_BASE[what][("n1", "n2", "r1", "r2").index(tag)] + n

        ada_landed = [sem(f"ada_landed_{r}") for r in range(ADA_RING)]

        def col(name, n=0, rows_=P):
            return cols[0:rows_, COLS[name][0] + n:COLS[name][0] + n + 1]

        def span(name):
            return cols[:, COLS[name][0]:COLS[name][0] + COLS[name][1]]

        ident = cst[:, C_ID:C_ID + P]
        ones = cst[:, C_ONE:C_ONE + P]

        J = ((0, META), (META, META + P), (META + P, TOK))

        def y_s(c):
            return uT[:, c, META:TOK]

        def lo_made(b, t=0):
            if b < N_POOL:
                return lo_pool, t + (b + 1)
            if POOL2[0] <= b < POOL2[1]:
                return lo_pool, t + (b - POOL2[0] + N_POOL + 1)
            by_pool = N_POOL + (POOL2[1] - POOL2[0] if b >= POOL2[1] else 0)
            return lo_dve, t + (b + 1 - by_pool)

        block = ctx.enter_context(nc.Block())

        @block.sync
        def _(sp):
            sp.dma_start(xt[1], A["x"][0, 0:P, :]).then_inc(S["x_landed"], 16)
            sp.dma_start(xt[2], A["x"][0, P:2 * P, :]).then_inc(S["x2_landed"], 16)
            for b in range(RING):
                sp.dma_start(raw[:, b], A["w_stream"][b]).then_inc(landed[b], 16)
            with sp.Fori(0, N_POOL // RING) as i:
                for r in range(RING):
                    sp.wait_ge(lo_pool, i * RING + (r + 1))
                    sp.dma_start(raw[:, r], A["w_stream"][i * RING + (RING + r)]).then_inc(landed[r], 16)

            def block_in(b, t=0):
                sp.wait_ge(*lo_made(b - RING, t))
                sp.dma_start(raw[:, b % RING], A["w_stream"][t + b]).then_inc(landed[b % RING], 16)

            def ada_in(n, t=0):
                if n >= ADA_RING:
                    sp.wait_ge(S["ada_used"], t + (n - ADA_RING + 1))
                sp.dma_start(ada_w[:, n % ADA_RING], A["w_ada"][t + n]).then_inc(ada_landed[n % ADA_RING], 16)

            FIRST, EARLY = N_POOL + RING, B_F1 + RING
            with sp.Fori(0, (EARLY - FIRST) // RING) as i:
                for r in range(RING):
                    block_in(FIRST + r, i * RING)
            sp.wait_ge(S["mix_lo"], KD)
            for n in range(ADA_RING):
                ada_in(n)
            for b in range(EARLY, SP_LOOP):
                block_in(b)
                if b > EARLY + 4 and (b - EARLY) % 2:
                    ada_in(ADA_RING + (b - EARLY - 5) // 2)
            for n in range(KD + 2, KD + ADA_RING):
                ada_in(n)
            with sp.Fori(0, ADA_LOOP) as i:
                n = KD + ADA_RING
                for q in range(8):
                    block_in(SP_LOOP + 2 * q, i * 16)
                    block_in(SP_LOOP + 2 * q + 1, i * 16)
                    for _ in range(ADA_SHARE[q]):
                        ada_in(n, i * 8)
                        n += 1
            AFTER = SP_LOOP + ADA_LOOP * 16
            for b in range(AFTER, B_F2 + 18):
                block_in(b)
                if b in (B_F2 + 12, B_F2 + 15):
                    for n in range(2):
                        ada_in((NMOD - 1) * KD + ADA_RING + 2 * ((b - B_F2 - 12) // 3) + n)
                for n in ada_rows(b - AFTER - AHEAD):
                    if n + ADA_RING < NMOD * KD:
                        ada_in(n + ADA_RING)
            with sp.Fori(0, (NBLK - B_F2 - 18) // RING) as i:
                for r in range(RING):
                    block_in(B_F2 + 18 + r, i * RING)
            for n in range(4):
                t, half = n % 2, n // 2
                sp.wait_ge(S["fin_by_dve" if half else "fin_by_act"], t + 1)
                sp.dma_start(out[0, t * P:(t + 1) * P, half * 512:(half + 1) * 512], ob[:, t, half * 512:(half + 1) * 512])\
                    .then_inc(S["stored"], 16)
            sp.wait_ge(S["stored"], 64)

        @block.tensor
        def _(pe):
            def evacuated(b):
                if b < 2:
                    return
                c = b - 2
                for first, n, name in ((B_WO, 8, "wo_ev"), (B_MOUT, 8, "mout_ev"), (B_GLU, 8, "glu_ev"),
                                       (B_GM, 8, "gm_ev"), (B_O, 8, "o_ev"), (B_GS, 8, "gs_ev"),
                                       (B_V, 8, "v_ev"), (B_Q, 8, "qk_ev"), (B_U, 4, "u_ev")):
                    if c >= first:
                        pe.wait_ge(S[name], c - first + 1)
                        return

            def split_ready(b):
                pe.wait_ge(*lo_made(b))

            def product(bank, n, slot, pieces, ready=None):
                k = 0
                for tile, ah, al in pieces:
                    if ready:
                        pe.wait_ge(S[ready], k // 3 + 1)
                    w_hi, w_lo = (w[:, slot, tile * P:(tile + 1) * P] for w in (wh, wl))
                    for w, a in ((w_hi, ah), (w_hi, al), (w_lo, ah)):
                        mm = nc.tensor.matmul(bank[:, 0:n], w, a, start=(k == 0), stop=(k == 3 * len(pieces) - 1))
                        k += 1
                return mm

            def stream(b, first_token, h=xh, l=xl, n=KD):
                evacuated(b)
                split_ready(b)
                product(ps[:, b % 2], TOK - first_token, b % RING,
                        [(k, h[:, k, first_token:TOK], l[:, k, first_token:TOK]) for k in range(n)],
                        ready={B_U: "ln0_lo", B_MOUT: "hm_lo"}.get(b)).then_inc(blk_done, 1)

            pe.wait_ge(S["consts_landed"], 16)
            pe.wait_ge(S["ln0_norm"], 3)
            for k in range(KD):
                if k >= 2:
                    pe.wait_ge(S["ln0_hi"], k - 1)
                for n, (a, z) in enumerate(J):
                    mm = nc.tensor.transpose(ps[:, 2 + k % 2, a:z], xt[n][0:z - a, k * P:(k + 1) * P], ident[0:z - a, 0:z - a])
                mm.then_inc(S["ln0_turned"], 1)
            for b in range(B_U, B_Q):
                stream(b, 0)
            pe.wait_ge(S["gates_landed"], 48)
            for k in range(KD):
                for g in range(2):
                    mm = nc.tensor.matmul(ps[32 * g:32 * g + HEADS, 6 + g, 0:TOK], wg[:, k, 4 * g:4 * g + 4], res[:, k, :],
                                          start=(k == 0), stop=(k == KD - 1))
                    if k == KD - 1:
                        mm.then_inc(S["gate_mm"], 1)
            pe.wait_ge(S["z_done"], 1)
            for n, z in enumerate((zre, zim)):
                for c in range(CH):
                    mm = nc.tensor.transpose(ps[:, 2 + n, c * P:(c + 1) * P],
                                             z[:, 4 * c:4 * c + 4, :].rearrange("p s h -> p (s h)"), ident)
                mm.then_inc(S["z_turned"], 1)

            def s5_in(s):
                if s == 0:
                    pe.wait_ge(S["bt_done"], 2)
                    pe.wait_ge(S["u_ev"], CH)
                else:
                    pe.wait_ge(S["s5_free"], s)
                r, c = 32 * (s % 4), s // 4
                for n, bt in enumerate((btr, bti)):
                    mm = nc.tensor.matmul(ps[:, 2 + n, 0:TOK], bt[r:r + 32, c, :], uT[r:r + 32, c, :], start=True, stop=True,
                                          tile_position=(r, 0))
                mm.then_inc(S["s5_in"], 1)

            def s5_out(c):
                if c == 0:
                    pe.wait_ge(S["c_done"], 1)
                else:
                    pe.wait_ge(S["y_sum"], c)
                pe.wait_ge(S["s5_x"], 4 * c + 4)
                for part, w in enumerate((cbr, cbi)):
                    for q in range(4):
                        mm = nc.tensor.matmul(ps[32 * q:32 * q + 32, 4, 0:SEQ], w[:, 4 * c + q, :], xst[:, q, part, :],
                                              start=(part == 0), stop=(part == 1))
                mm.then_inc(S["s5_y"], 1)

            def turn_gates():
                pe.wait_ge(S["rows_done"], 1)
                for n, (a, z) in enumerate(J):
                    nc.tensor.transpose(ps[0:z - a, 6, 4 * n:4 * n + 4], rows[:, 0, a:z], ident[0:HEADS, 0:HEADS])
                for n in range(NT):
                    a, z = J[1 + n]
                    mm = nc.tensor.transpose(ps[:, 6, 12 + 4 * n:16 + 4 * n], rows[:, 3, a:z], ident[0:HEADS, 0:HEADS])
                mm.then_inc(S["a_turned"], 1)

            def turn_v(e):
                pe.wait_ge(S["v_ev"], e + 1)
                if e == 0:
                    pe.wait_ge(S["gate_ev"], 2)
                else:
                    pe.wait_ge(S["v_copied"], e)
                for n, (a, z) in enumerate(J):
                    mm = nc.tensor.transpose(ps[0:z - a, 7, n * P:(n + 1) * P], vr[:, e % 2, a:z], ident)
                mm.then_inc(S["v_turned"], 1)

            def scores(h):
                if h == 0:
                    pe.wait_ge(S["a_copied"], 1)
                    pe.wait_ge(S["v_copied"], 8)
                else:
                    pe.wait_ge(S["e_done"], h)
                    pe.wait_ge(S["num_copied"], NT * h)
                pe.wait_ge(S["silu_done"], 5 + h)
                for n, (tile, masked) in enumerate(((1, True), (2, False), (1, False), (2, True))):
                    a, z = J[tile]
                    o = ps[:, 5, n * P:(n + 1) * P]
                    nc.tensor.matmul(o, sel[:, h, :], rows[:, 2, a:z], start=True, stop=not masked)
                    if masked:
                        nc.tensor.matmul(o, ident, cst[:, C_MASK:C_MASK + P], start=False, stop=True)
                q, k = qkT[:, h], qkT[:, HEADS + h]
                nc.tensor.matmul(ps[:, 6, 0:SEQ], k[:, META:META + P], q[:, META:TOK], start=True, stop=True)
                nc.tensor.matmul(ps[:, 6, SEQ:SEQ + P], k[:, META + P:TOK], q[:, META + P:TOK], start=True, stop=True)
                nc.tensor.matmul(ps[0:META, 7, 0:SEQ], k[:, 0:META], q[:, META:TOK], start=True, stop=True)\
                    .then_inc(S["cs_done"], 1)

            def numerators(h, t):
                pe.wait_ge(S["p_done"], h + 1)
                if h == 0:
                    pe.wait_ge(pool_step, 1)
                if h or t:
                    pe.wait_ge(S["num_copied"], NT * h + t)
                o = ps[:, 7, 0:DV + 1]
                nc.tensor.matmul(o, pp[0:META, 384 + t * P:384 + (t + 1) * P], vtk[0:META, 0, h, :], start=True, stop=False)
                mm = nc.tensor.matmul(o, pp[:, t * P:(t + 1) * P], vtk[:, 1, h, :], start=False, stop=(t == 0))
                if t:
                    mm = nc.tensor.matmul(o, pp[:, 256:384], vtk[:, 2, h, :], start=False, stop=True)
                mm.then_inc(S["num_done"], 1)

            for b in range(B_Q, B_GLU):
                stream(b, 0 if b < B_GS else META)
                if b in S5_AT:
                    s5_in(S5_AT.index(b))
                if b - 4 in S5_AT[3::4]:
                    s5_out(S5_AT[3::4].index(b - 4))
                if b == 8:
                    turn_gates()
                if 13 <= b < 21:
                    turn_v(b - 13)
                if b in (23, 27, 31, 35):
                    scores((b - 23) // 4)
                if b in (25, 29, 33, 37):
                    numerators((b - 25) // 4, 0)
                if b in (26, 30, 34, 38):
                    numerators((b - 26) // 4, 1)

            def turn_heads(m):
                h, half = m // 2, m % 2
                if m == 0:
                    pe.wait_ge(S["hnorm"], NT * HEADS)
                if m >= 2:
                    pe.wait_ge(S["h_gated"], m - 1)
                for t in range(NT):
                    mm = nc.tensor.transpose(ps[:, 5 + m % 2, t * P:(t + 1) * P], hraw[:, t, h, half * P:(half + 1) * P], ident)
                mm.then_inc(S["h_turned"], 1)

            pe.wait_ge(S["y_lo"], CH)
            for b in range(B_GLU, B_MOUT):
                evacuated(b)
                split_ready(b)
                for half in range(2):
                    mm = product(ps[:, b % 2, half * SEQ:(half + 1) * SEQ], SEQ, b % RING,
                                 [(4 * half + k, gh[:, k, :], gl[:, k, :]) for k in range(CH)])
                mm.then_inc(blk_done, 1)
                turn_heads(b - B_GLU)
            for b in range(B_MOUT, B_WO):
                stream(b, META)

            def mean_of(m):
                pe.wait_ge(S["wo_ev"], m + 1)
                mm = nc.tensor.matmul(ps[:, 6, 0:SEQ], ones, res[:, m, META:TOK], start=(m == 0), stop=(m == KD - 1))
                if m == KD - 1:
                    mm.then_inc(NORM["mean"], 1)

            for b in range(B_WO, B_F1):
                evacuated(b)
                split_ready(b)
                product(ps[:, b % 2], SEQ, b % RING, [(k, mh[:, k, :], ml[:, k, :]) for k in range(KD)],
                        ready="mix_lo" if b == B_WO else None).then_inc(blk_done, 1)
                if b > B_WO:
                    mean_of(b - B_WO - 1)
            mean_of(KD - 1)

            def sum_squares(tag, bank, n=KD, per=1):
                for m in range(n):
                    pe.wait_ge(*norm(tag, "sq", m // per + 1))
                    mm = nc.tensor.matmul(ps[:, bank, 0:SEQ], ones, sq[:, m, :], start=(m == 0), stop=(m == n - 1))
                mm.then_inc(NORM["var"], 1)

            def block(b, bank, name, value, t=0, h=xh, l=xl, first=META, order=range(KD), ready=None):
                if name:
                    pe.wait_ge(S[name], value)
                pe.wait_ge(*lo_made(b, t))
                k = 0
                for n in order:
                    if ready:
                        pe.wait_ge(*ready(n))
                    a, z = h[:, n, first:first + SEQ], l[:, n, first:first + SEQ]
                    w_hi, w_lo = (w[:, b % RING, n * P:(n + 1) * P] for w in (wh, wl))
                    for w, x in ((w_hi, a), (w_hi, z), (w_lo, a)):
                        mm = nc.tensor.matmul(ps[:, bank, 0:SEQ], w, x, start=(k == 0), stop=(k == 3 * KD - 1))
                        k += 1
                mm.then_inc(blk_done, 1)

            def down(b, j, name, value, t=0, first=False, last=False):
                pe.wait_ge(*lo_made(b, t))
                pe.wait_ge(S[name], value)
                for m in range(KD):
                    o = ps[:, 2 + m // 2, (m % 2) * SEQ:(m % 2 + 1) * SEQ]
                    w_hi, w_lo = (w[:, b % RING, m * P:(m + 1) * P] for w in (wh, wl))
                    for n, (w, x) in enumerate(((w_hi, gh), (w_hi, gl), (w_lo, gh))):
                        mm = nc.tensor.matmul(o, w, x[:, j % 4, :], start=(first and m % 2 == 0 and n == 0),
                                              stop=(last and n == 2), skip_group_check=True)
                mm.then_inc(blk_done, 1)

            def modulation(acc, used, done, at=0, bank=7):
                pe.wait_ge(S["ada_used"], used)
                if done is not None:
                    pe.wait_ge(S["mod_done"], done)
                for m in range(KD):
                    mm = nc.tensor.matmul(ps[:, bank, at + m:at + m + 1], ada_acc[:, acc, m * P:(m + 1) * P],
                                          cst[:, C_ONE_:C_ONE_ + 1], start=True, stop=True)
                mm.then_inc(S["mod_mm"], 1)

            for g in range(4):
                pe.wait_ge(S["n1_pair"], g + 1)
                mm = nc.tensor.matmul(ps[:, 7, 0:SEQ], ones, sq[:, 2 * g, :], start=(g == 0), stop=(g == 3))
            mm.then_inc(NORM["var"], 1)
            pe.wait_ge(S["wo_ev"], KD)
            block(B_F1, 0, None, 0, ready=lambda n: norm("n1", "lo", GROUP_OF[n] + 1))

            def pair(j, i=0):
                if j >= 2:
                    block(B_F1 - 1 + 2 * j, j % 2, "f_relu", i * 8 + (j - 1), i * 16)
                else:
                    block(B_F1 - 1 + 2 * j, j % 2, None, 0, i * 16)
                down(B_F1 + 2 * j, j - 1, "f_lo", i * 8 + j, i * 16, first=(j == 1))

            for j in range(1, LOOP1_PAIR):
                pair(j)
            with pe.Fori(0, 3) as i:
                for q in range(8):
                    pair(LOOP1_PAIR + q, i)
                    if q == 6:
                        modulation(0, i * 8 + 16, None)
            modulation(1, KD, None, bank=6)
            down(B_F1 + 2 * KF - 1, KF - 1, "f_lo", KF, last=True)

            for g in range(4):
                pe.wait_ge(S["f1_res"], g + 1)
                for m in (2 * g, 2 * g + 1):
                    mm = nc.tensor.matmul(ps[:, 6, 0:SEQ], ones, res[:, m, META:TOK], start=(m == 0), stop=(m == KD - 1))
            mm.then_inc(NORM["mean"], 1)
            sum_squares("n2", 7, per=2)
            pe.wait_ge(S["mixing_landed"], 64)
            for n in range(2):
                for q in range(4):
                    mm = nc.tensor.transpose(ps[:, 2 + n, q * P:(q + 1) * P], ws[:, 4 * n + q, :], ident)
                mm.then_inc(S["ws_turned"], 1)
            sum_squares("r1", 6, per=2)

            def q_stat(t):
                pe.wait_ge(S["q_ev"], t + 1)
                if t:
                    pe.wait_ge(S["q_std"], t)
                else:
                    pe.wait_ge(S["ws_copied"], 2)
                nc.tensor.matmul(ps[:, 2, 0:SEQ], cst[:, C_BLK:C_BLK + P], qs[:, t % 3, :], start=True, stop=True)\
                    .then_inc(S["q_stat"], 1)
                bank3(lambda: nc.tensor.matmul(ps[:, 3, 0:SEQ], cst[:, C_ROT:C_ROT + P], qg[:, t % 3, :], start=True, stop=True))

            uses = [0]

            def bank3(make):
                if uses[0]:
                    pe.wait_ge(S["b3_free"], uses[0])
                make().then_inc(S["b3_full"], 1)
                uses[0] += 1

            def turn_zv(c):
                pe.wait_ge(S["zv_act"], 1)
                if c == 0:
                    pe.wait_ge(S["q_std"], 5)
                else:
                    pe.wait_ge(S["zv_copied"], c)
                for m in range(QT):
                    mm = nc.tensor.transpose(ps[:, 2, m * P:(m + 1) * P], zv[:, m, c * P:(c + 1) * P], ident)
                mm.then_inc(S["zv_turned"], 1)

            def turn_v2():
                pe.wait_ge(S["v2_ev"], 1)

                def make():
                    for c in range(NT):
                        mm = nc.tensor.transpose(ps[:, 3, c * P:(c + 1) * P], vv[:, c * P:(c + 1) * P], ident)
                    return mm
                bank3(make)

            def swap_k():
                pe.wait_ge(S["qk_ready"], 1)
                bank3(lambda: nc.tensor.matmul(ps[:, 3, 0:SEQ], cst[:, C_SWAP:C_SWAP + P], kf[:, 0, :], start=True, stop=True))

            def mix_tokens(m):
                pe.wait_ge(S["zv_n"], NT)
                if m == 1:
                    pe.wait_ge(S["exp_done"], AH)
                if m == 3:
                    pe.wait_ge(S["tok_pre"], 1)
                for c in range(NT):
                    for g in range(2):
                        o = ps[64 * g:64 * g + 64, MIX_BANK[m], c * P:(c + 1) * P]
                        mm = nc.tensor.matmul(o, zvt[:, c, m * P + 64 * g:m * P + 64 * g + 64], wst[:, 2 * m + g, :],
                                              start=True, stop=True)
                mm.then_inc(S["mixed"], 1)

            def scores2(h):
                r, qt = 64 * (h % 2), h // 2
                pe.wait_ge(S["qk_ready"], 2 + qt)
                if h == 1:
                    pe.wait_ge(S["b3_free"], 5)
                if h >= 2:
                    pe.wait_ge(S["exp_done"], h - 1)
                k = kf[r:r + 64, 0 if h // 4 == h % 2 else 1, :]
                for t in range(NT):
                    mm = nc.tensor.matmul(ps[:, 6 + h % 2, t * SEQ:(t + 1) * SEQ], qf[r:r + 64, qt, t * P:(t + 1) * P], k,
                                          start=True, stop=True)
                mm.then_inc(S["s_done"], 1)

            def turn_probs(h):
                pe.wait_ge(S["prob_done"], h + 1)
                if h >= 2:
                    pe.wait_ge(S["pt_copied"], h - 1)
                for s in range(NT):
                    for t in range(NT):
                        mm = nc.tensor.transpose(ps[:, 4 + h % 2, s * SEQ + t * P:s * SEQ + (t + 1) * P],
                                                 prob[:, h % 2, t, s * P:(s + 1) * P], ident)
                mm.then_inc(S["pt_done"], 1)

            def weigh_v(h):
                pe.wait_ge(S["pt_copied"], h + 1)
                r, qt, kv = 64 * (h % 2), h // 2, h // 4
                if h == 0:
                    pe.wait_ge(S["b3_free"], 7)
                elif h % 2 == 0:
                    pe.wait_ge(S["ao_done"], qt)
                for s in range(NT):
                    mm = nc.tensor.matmul(ps[r:r + 64, 3, 0:SEQ], vtok[:, s, 64 * kv:64 * kv + 64],
                                          probt[:, h % 2, s, :], start=(s == 0), stop=(s == NT - 1))
                mm.then_inc(S["o_done"], 1)

            for b in range(B_IN2, B_OUT2):
                n = b - B_IN2
                if n == 2:
                    free = ("v2_ev", 1)
                elif 3 <= n < 8:
                    free = ("q_ev", n - 2)
                elif 8 <= n < 12:
                    free = ("zv_ev", n - 7)
                else:
                    free = ("zu_ev", n - 11) if n >= 12 else (None, 0)
                block(b, b % 2, *free, ready=(lambda q: norm("r1", "lo", GROUP_OF[q] + 1)) if n == 0 else None)
                if n == 1:
                    turn_v2()
                if n == 5:
                    swap_k()
                if n >= 7:
                    turn_probs(n - 7)
                if 5 <= n < 13:
                    scores2(n - 5)
                if 2 <= n < 7:
                    q_stat(n - 2)
                if n >= 8:
                    weigh_v(n - 8)
                if n in (10, 11):
                    turn_zv(n - 10)
            turn_probs(AH - 1)
            weigh_v(AH - 2)
            mix_tokens(0)
            mix_tokens(1)
            mix_tokens(2)
            weigh_v(AH - 1)
            mix_tokens(3)

            def branch_ms(name, bank, at, read):
                pe.wait_ge(S[read], QT)
                for m in range(QT):
                    pe.wait_ge(S[name], m + 1)
                    mm = nc.tensor.matmul(ps[:, bank, 0:SEQ], ones, sq[:, at + m, :], start=(m == 0), stop=(m == QT - 1))
                mm.then_inc(S["branch_ms"], 1)

            branch_ms("tok_sq", 2, QT, "tok_pre")
            modulation(1, (NMOD - 1) * KD, None, 0, 5)

            for b in range(B_OUT2, B_F2):
                pe.wait_ge(*lo_made(b))
                half, pair_ = divmod(b - B_OUT2, 4)
                if half == 0:
                    pe.wait_ge(*((S["zu_ev"], 3), (S["zu_ev"], 4), (S["tok_pre"], QT), (S["exp_done"], AH))[pair_])
                at = QT * (1 - half)
                for k in range(QT):
                    if pair_ == 0:
                        pe.wait_ge(S["branch_lo"], QT * half + k + 1)
                    for m in range(2):
                        o = ps[:, (0, 1, 6, 7)[pair_], m * SEQ:(m + 1) * SEQ]
                        w_hi, w_lo = (w[:, b % RING, (QT * m + k) * P:(QT * m + k + 1) * P] for w in (wh, wl))
                        for n, (w, x) in enumerate(((w_hi, mh), (w_hi, ml), (w_lo, mh))):
                            mm = nc.tensor.matmul(o, w, x[:, at + k, :], start=(half == 0 and k == 0 and m == 0 and n == 0),
                                                  stop=(half == 1 and k == QT - 1 and n == 2), skip_group_check=True)
                mm.then_inc(blk_done, 1)
                if b == B_OUT2:
                    branch_ms("att_sq", 3, 0, "ao_done")
            sum_squares("r2", 4)

            def up2(j, i=0, ready=None):
                t = i * 12
                b = B_F2 + (0 if j == 0 else 3 * j - 1)
                block(b, 0, *(("ff2_ca", i * 4 + j) if j else ("out2_ev", KD)), t, ready=ready)
                block(b + 1, 1, *(("ff2_cb", i * 4 + j) if j else ("out2_ev", KD)), t)

            def triple(j, i=0):
                up2(j, i)
                down(B_F2 + 3 * j + 1, j - 1, "ff2_lo", i * 4 + j, i * 12, first=(j == 1))

            up2(0, ready=lambda q: norm("r2", "lo", GROUP_OF[q] + 1))
            for j in range(1, LOOP2_TRIPLE):
                triple(j)
            with pe.Fori(0, (KF2 - LOOP2_TRIPLE) // 4) as i:
                for q in range(4):
                    triple(LOOP2_TRIPLE + q, i)
            modulation(2, NMOD * KD, None)
            down(NBLK - 1, KF2 - 1, "ff2_lo", KF2, last=True)

            def turn_out(half):
                for t in range(NT):
                    if half == 1:
                        pe.wait_ge(S["f2_res"], 2 * t + 2)
                    for m in range(4 * half, 4 * half + 4):
                        pe.wait_ge(S["fin_f"], m + 1)
                        mm = nc.tensor.transpose(ps[:, OUT_BANK[2 * half + t], (m % 4) * P:(m % 4 + 1) * P],
                                                 tg_m[:, m, t * P:(t + 1) * P], ident)
                    mm.then_inc(S["fin_turned"], 1)

            for m in range(KD):
                pe.wait_ge(S["fin_sq"], m + 1)
                for t in range(NT):
                    mm = nc.tensor.matmul(ps[:, 6 + t, t:t + 1], sq[:, m, t * P:(t + 1) * P], cst[:, C_ONE:C_ONE + 1],
                                          start=(m == 0), stop=(m == KD - 1))
            mm.then_inc(S["fin_ms"], 1)
            turn_out(0)
            turn_out(1)

        @block.scalar
        def _(act):
            step = Steps(act, act_step)
            act.dma_start(cols[:, :], A["cols"]).then_inc(S["cols_landed"], 16)
            act.dma_start(xt[0][0:META, :], A["meta_tokens"]).then_inc(S["meta_landed"], 16)
            act.dma_start(cst[:, :], A["consts"]).then_inc(S["consts_landed"], 16)
            act.dma_start(s5m[:, :, :, :], A["s5_mats"]).then_inc(S["s5m_landed"], 16)
            act.dma_start(wg[:, :, :], A["w_gates"]).then_inc(S["gates_landed"], 16)
            act.dma_start(bg[:, :], A["b_gates"]).then_inc(S["gates_landed"], 16)
            act.dma_start(sel[:, :, :], A["sel"]).then_inc(S["gates_landed"], 16)

            def hi(b, t=0):
                if isinstance(b, int) and isinstance(t, int) and b + t >= NBLK:
                    return
                act.wait_ge(landed[b % RING], t * (16 // RING) + 16 * (b // RING + 1))
                if b >= RING:
                    act.wait_ge(blk_done, t + (b - RING + 1))
                nc.scalar.activation(wh[:, b % RING], raw[:, b % RING], ACT.Identity).then_inc(hi_done, 1)

            act.wait_ge(S["ln0_var"], 1)
            nc.scalar.activation(lnr[:, :, 0], lnr[:, :, 1], ACT.Sqrt).then_inc(S["ln0_std"], 1)
            hi(0)
            hi(1)
            act.wait_ge(S["cols_landed"], 16)
            nc.scalar.activation(sv[:, 0], span("log_dt"), ACT.Exp).then_inc(S["dt_done"], 1)
            for k in range(KD):
                act.wait_ge(S["ln0_turned"], k + 1)
                for dst, s_ in ((res, "ln0_h"), (xh, "ln0_hi")):
                    nc.scalar.activation(dst[:, k, :], ps[:, 2 + k % 2, 0:TOK], ACT.Identity, bias=col("ln0_b", k),
                                         scale=col("ln0_g", k)).then_inc(S[s_], 1)

            hi(2)
            half_pi = hb[:, 51:52]
            act.wait_ge(S["phase_done"], 2)
            nc.scalar.activation(sv[:, 3], sv[:, 1], ACT.Tanh, scale=0.5).then_inc(S["half_done"], 1)
            for dst, src, scale, bias in ((6, 5, HALF_TURN, None), (19, 5, 2 * HALF_TURN, None), (18, 17, -2 * HALF_TURN, half_pi)):
                nc.scalar.activation(sv[:, dst], sv[:, src], ACT.Sin, scale=scale, **({"bias": bias} if bias is not None else {}))\
                    .then_inc(S["half_done"], 1)

            def tables(q):
                act.wait_ge(S["phase_done"], 3 + q)
                s = slice(4 * q, 4 * q + 4)
                nc.scalar.activation(tab[:, s, 1, :], tab[:, s, 1, :], ACT.Sin, scale=2 * HALF_TURN).then_inc(S["tables_done"], 1)
                nc.scalar.activation(tab[:, s, 0, :], tab[:, s, 0, :], ACT.Sin, bias=half_pi, scale=-2 * HALF_TURN)\
                    .then_inc(S["tables_done"], 1)

            def gate_rows():
                act.wait_ge(S["gates_landed"], 48)
                for g in range(2):
                    act.wait_ge(S["gate_mm"], g + 1)
                    nc.scalar.activation(rows[:, g, :], ps[32 * g:32 * g + HEADS, 6 + g, 0:TOK], ACT.Identity, bias=bg[:, g:g + 1])\
                        .then_inc(S["gate_ev"], 1)

            def softplus_rows():
                act.wait_ge(S["abs_f"], 1)
                step(nc.scalar.activation(rows[:, 2, :], rows[:, 2, :], ACT.Exp, scale=-1.0))
                nc.scalar.activation(rows[:, 2, :], rows[:, 2, :], ACT.Ln, bias=1.0).then_inc(S["ln_done"], 1)

            def evac(b):
                if b >= B_GLU:
                    return
                act.wait_ge(blk_done, b + 1)
                p_ = ps[:, b % 2, 0:TOK]
                if b < B_Q:
                    nc.scalar.activation(uT[:, b, :], p_, ACT.Identity, bias=col("b_in", b)).then_inc(S["u_ev"], 1)
                elif b < B_V:
                    t = b - B_Q
                    if t == 0:
                        act.wait_ge(S["cleared"], 2)
                    nc.scalar.activation(qkT[:, t, 3:], p_, ACT.Identity, bias=col("b_in", b)).then_inc(S["qk_ev"], 1)
                elif b < B_GS:
                    e = b - B_V
                    if e >= 2:
                        act.wait_ge(S["v_turned"], e - 1)
                    nc.scalar.activation(vr[:, e % 2, :], p_, ACT.Identity, bias=col("b_in", b)).then_inc(S["v_ev"], 1)
                else:
                    first, dst, name = ((B_GS, tg_s, "gs_ev"), (B_O, tg_o, "o_ev"), (B_GM, tg_m, "gm_ev"))[(b - B_GS) // 8]
                    if b == B_GM:
                        act.wait_ge(S["s5_x"], -(-(2 * 4 * SEQ + KD * SEQ) // (2 * TOK)))
                    nc.scalar.activation(dst[:, b - first, :], ps[:, b % 2, 0:SEQ], ACT.Tanh, bias=hb[:, b - B_GS:b - B_GS + 1],
                                         scale=0.5).then_inc(S[name], 1)

            def silu(t):
                act.wait_ge(S["conv_done"], t + 1)
                nc.scalar.activation(qkT[:, t, 0:TOK], cv[:, t % 2, :], ACT.Silu).then_inc(S["silu_done"], 1)

            def v_copy(e):
                h, half = e // 2, e % 2
                act.wait_ge(S["v_turned"], e + 1)
                step(nc.scalar.copy(vtk[0:META, 0, h, half * P:(half + 1) * P], ps[0:META, 7, 0:P]))
                nc.scalar.copy(vtk[:, 1:3, h, half * P:(half + 1) * P],
                               ps[:, 7, P:3 * P].rearrange("p (j e) -> p j e", j=2)).then_inc(S["v_copied"], 1)

            def decay(h):
                act.wait_ge(S["cs_done"], h + 1)
                if h == 0:
                    act.wait_ge(S["a_copied"], 1)
                else:
                    act.wait_ge(S["p_done"], h)
                nc.scalar.activation(ee[:, 0:256], ps[:, 5, 0:256], ACT.Exp, bias=aT[:, 1, h:h + 1])
                nc.scalar.activation(ee[:, 256:384], ps[:, 5, 384:512], ACT.Exp, bias=aT[:, 2, h:h + 1])
                for t, a in ((0, 256), (1, 128)):
                    ins = nc.scalar.activation(ee[0:META, 384 + t * P:384 + (t + 1) * P], ps[0:META, 5, a:a + P], ACT.Exp,
                                               bias=aT[0:META, 0, h:h + 1])
                ins.then_inc(S["e_done"], 1)

            def num_copy(h, t):
                act.wait_ge(S["num_done"], NT * h + t + 1)
                nc.scalar.copy(hraw[:, t, h, :], ps[:, 7, 0:DV + 1]).then_inc(S["num_copied"], 1)

            for b in range(B_U, B_GLU):
                if b in (24, 28, 32, 36):
                    decay((b - 24) // 4)
                if b in (26, 30, 34, 38):
                    num_copy((b - 26) // 4, 0)
                if b in (27, 31, 35, 39):
                    num_copy((b - 27) // 4, 1)
                hi(b + AHEAD)
                evac(b)
                if b == 4:
                    softplus_rows()
                if b in (1, 4, 5, 6):
                    tables(max(0, b - 3))
                if b == 3:
                    gate_rows()
                    for n, bt in enumerate((btr, bti)):
                        act.wait_ge(S["z_turned"], n + 1)
                        nc.scalar.copy(bt[:, :, :].rearrange("p c q -> p (c q)"), ps[:, 2 + n, :]).then_inc(S["bt_done"], 1)
                if b == 9:
                    act.wait_ge(S["a_turned"], 1)
                    nc.scalar.activation(floor[:, :, :].rearrange("p t h -> p (t h)"), ps[:, 6, 12:20], ACT.Exp)\
                        .then_inc(S["floor_done"], 1)
                if b in SILU_AT:
                    silu(SILU_AT.index(b))
                if b == SILU_AT[-1]:
                    nc.scalar.activation(sc[:, :], span("c"), ACT.Silu).then_inc(S["silu_c"], 1)
                if 14 <= b < 22:
                    v_copy(b - 14)
                if b == 41:
                    act.wait_ge(S["hvar"], 1)
                    nc.scalar.activation(hsm[:, 1], hsm[:, 1], ACT.Sqrt).then_inc(S["hstd"], 1)
                if b in (38, 41):
                    for c in (range(CH - 1) if b == 38 else range(CH - 1, CH)):
                        act.wait_ge(S["y_sum"], c + 1)
                        nc.scalar.activation(gh[:, c, :], y_s(c), ACT.Gelu_apprx_tanh).then_inc(S["y_hi"], 1)
                        act.wait_ge(S["y_hi"], c + 1)
                        nc.scalar.activation(y_s(c), y_s(c), ACT.Gelu_apprx_tanh).then_inc(S["y_act"], 1)


            def gate_heads(m):
                act.wait_ge(S["h_gated"], m + 1)
                if m == 0:
                    act.wait_ge(blk_done, B_GLU)
                nc.scalar.activation(xh[:, m, META:TOK], tg_o[:, m, :], ACT.Identity, scale=col("m_norm_g", m)).then_inc(S["hm_hi"], 1)
                act.wait_ge(S["hm_hi"], m + 1)
                nc.scalar.activation(tg_o[:, m, :], tg_o[:, m, :], ACT.Identity, scale=col("m_norm_g", m)).then_inc(S["hm_f"], 1)

            for b in range(B_GLU, B_MOUT):
                hi(b + AHEAD)
                j = b - B_GLU
                if j:
                    gate_heads(j - 1)
                act.wait_ge(blk_done, b + 1)
                if j >= 2:
                    act.wait_ge(S["glu_ev"], j - 1)
                nc.scalar.activation(tz[:, j % 2, :], ps[:, b % 2, SEQ:2 * SEQ], ACT.Tanh, scale=0.5).then_inc(S["glu_t"], 1)
            gate_heads(KD - 1)

            def mix_hi(m):
                act.wait_ge(S["mout_ev"], m + 1)
                nc.scalar.activation(mh[:, m, :], tg_s[:, m, :], ACT.Identity).then_inc(S["mix_hi"], 1)

            for b in range(B_MOUT, B_WO):
                hi(b + AHEAD)
                if b > B_MOUT:
                    mix_hi(b - B_MOUT - 1)
            mix_hi(KD - 1)
            for b in range(B_WO, B_F1):
                hi(b + AHEAD)

            def squares(tag, src, what):
                for g in range(4):
                    act.wait_ge(*norm(tag, what, g + 1))
                    nc.scalar.activation(sq[:, 2 * g:2 * (g + 1), :], src[:, 2 * g:2 * (g + 1), :], ACT.Square)\
                        .then_inc(NORM["sq"], 1)

            def deviation(tag, bank, eps_col, scale=1.0):
                act.wait_ge(*norm(tag, "var"))
                nc.scalar.activation(std[:, :], ps[:, bank, 0:SEQ], ACT.Sqrt, bias=eps_col, scale=scale)\
                    .then_inc(NORM["std"], 1)

            def high_parts(tag, src):
                for a, z in GROUPS:
                    act.wait_ge(*norm(tag, "h", z))
                    nc.scalar.activation(xh[:, a:z, META:TOK], src[:, a:z, :], ACT.Identity)\
                        .then_inc(NORM["hi"], 1)

            y = res[:, :, META:TOK]
            squares("n1", y, "d")
            deviation("n1", 7, eps[:, 0:1])
            high_parts("n1", y)
            act.wait_ge(blk_done, B_F1)
            act.wait_ge(S["wo_ev"], KD)
            act.wait_ge(S["mix_lo"], KD)
            act.dma_start(rope[:, :, :], A["rope"]).then_inc(S["mixing_landed"], 16)
            act.dma_start(ws[:, :, :], A["w_s"]).then_inc(S["mixing_landed"], 16)
            for g in range(2):
                act.dma_start(bs[64 * g:64 * g + 64, :, :],
                              A["b_s"][None, g::2, :].to_broadcast([64, QT, P])).then_inc(S["mixing_landed"], 16)

            def relu_block(b, j, t=0, i=0):
                act.wait_ge(blk_done, t + (b + 1))
                if j >= 2:
                    act.wait_ge(S["f_lo"], i * 8 + (j - 1))
                bias = cols[:, bass.ds(i * 8 + (COLS["b_up"][0] + j), 1)]
                nc.scalar.activation(relu[:, j % 2, :], ps[:, j % 2, 0:SEQ], ACT.Relu, bias=bias).then_inc(S["f_relu"], 1)
                act.wait_ge(S["f_relu"], i * 8 + (j + 1))
                nc.scalar.activation(gh[:, j % 4, :], relu[:, j % 2, :], ACT.Square).then_inc(S["f_hi"], 1)

            hi(B_F1 + AHEAD)
            relu_block(B_F1, 0)

            def pair(j, i=0):
                b, t = B_F1 - 1 + 2 * j, i * 16
                hi(b + AHEAD, t)
                relu_block(b, j, t, i)
                hi(b + 1 + AHEAD, t)

            for j in range(1, LOOP1_PAIR):
                pair(j)
            with act.Fori(0, 3) as i:
                for q in range(8):
                    pair(LOOP1_PAIR + q, i)
            hi(B_F1 + 2 * KF - 1 + AHEAD)

            squares("n2", y, "d")
            deviation("n2", 7, eps[:, 1:2])
            for g in range(4):
                act.wait_ge(*norm("n2", "h", 2 * g + 2))
                if g == 0:
                    act.wait_ge(*norm("n2", "var"))
                nc.scalar.activation(sq[:, 2 * g:2 * g + 2, :], y[:, 2 * g:2 * g + 2, :], ACT.Square).then_inc(NORM["sq"], 1)
            for n in range(2):
                act.wait_ge(S["ws_turned"], n + 1)
                nc.scalar.copy(wst[:, 4 * n:4 * n + 4, :].rearrange("p h q -> p (h q)"), ps[:, 2 + n, :]).then_inc(S["ws_copied"], 1)
            deviation("r1", 6, eps[:, 2:3])
            high_parts("r1", tg_m)

            def q_post(t):
                act.wait_ge(S["q_stat"], t + 1)
                if t >= 2:
                    act.wait_ge(S["qk_ready"], t - 1)
                nc.scalar.activation(qstd[:, t % 2, :], ps[:, 2, 0:SEQ], ACT.Sqrt, bias=eps[:, 2:3]).then_inc(S["q_std"], 1)

            def exps(h):
                act.wait_ge(S["max_done"], h + 1)
                if h >= 2:
                    act.wait_ge(S["pt_done"], h - 1)
                for t in range(NT):
                    nc.scalar.activation(prob[:, h % 2, t, :], ps[:, 6 + h % 2, t * SEQ:(t + 1) * SEQ], ACT.Exp,
                                         bias=smax[:, h, 1, t:t + 1], scale=HD ** -0.5,
                                         accum_out=ssum[:, h, t:t + 1]).then_inc(act_step, 1)
                    step.n += 1
                act.wait_ge(act_step, step.n)
                act.sem_inc(S["exp_done"], 1)

            def probt_copy(h):
                act.wait_ge(S["pt_done"], h + 1)
                if h >= 2:
                    act.wait_ge(S["o_done"], h - 1)
                nc.scalar.copy(probt[:, h % 2, :, :].rearrange("p s t -> p (s t)"), ps[:, 4 + h % 2, :]).then_inc(S["pt_copied"], 1)

            ROTATED = (2, 3, 4, 6, 7)
            for b in range(B_IN2, B_OUT2):
                n = b - B_IN2
                hi(b + AHEAD)
                if 3 <= n < 6:
                    q_post(n - 3)
                if n in (11, 12):
                    c = n - 11
                    act.wait_ge(S["zv_turned"], c + 1)
                    if c == 0:
                        act.wait_ge(*norm("r1", "var"))
                    nc.scalar.activation(sq[:, 2 * c:2 * c + 2, :].rearrange("p a t -> p (a t)"), ps[:, 2, :], ACT.Square)\
                        .then_inc(S["zv_sq"], 1)
                    nc.scalar.copy(zvt[:, c, :], ps[:, 2, :]).then_inc(S["zv_copied"], 1)
                if n == 13:
                    act.wait_ge(S["zv_ms"], NT)
                    nc.scalar.activation(zms[:, :, :], zms[:, :, :], ACT.Sqrt, bias=eps[:, 2:3], scale=1.0 / HD)\
                        .then_inc(S["zv_std"], 1)
                act.wait_ge(blk_done, b + 1)
                p_ = ps[:, b % 2, 0:SEQ]
                if n == 0:
                    nc.scalar.copy(vv[:, :], p_).then_inc(S["v2_ev"], 1)
                elif n < 6:
                    t = n - 1
                    if t >= 3:
                        act.wait_ge(S["qk_ready"], t - 2)
                        act.wait_ge(S["b3_full"], ROTATED[t - 3])
                    nc.scalar.activation(qs[:, t % 3, :], p_, ACT.Square)
                    nc.scalar.activation(qg[:, t % 3, :], p_, ACT.Identity, scale=col("g_q" if t else "g_k"))\
                        .then_inc(S["q_ev"], 1)
                elif n < 10:
                    nc.scalar.copy(zv[:, n - 6, :], p_).then_inc(S["zv_ev"], 1)
                else:
                    nc.scalar.copy(zu[:, n - 10, :], p_).then_inc(S["zu_ev"], 1)
                if n == 6:
                    q_post(3)
                    q_post(4)
                if 5 <= n < 13:
                    exps(n - 5)
                if n >= 7:
                    probt_copy(n - 7)
                if n == 9:
                    act.wait_ge(S["zv_ev"], QT)
                    nc.scalar.activation(zv[:, :, :], zv[:, :, :], ACT.Gelu_apprx_tanh).then_inc(S["zv_act"], 1)
            probt_copy(AH - 1)
            act.wait_ge(S["zu_ev"], QT)
            nc.scalar.activation(zu[:, :, :], zu[:, :, :], ACT.Gelu_apprx_tanh).then_inc(S["zu_act"], 1)
            for m in range(QT):
                act.wait_ge(S["tok_done"], m + 1)
                nc.scalar.activation(sq[:, QT + m, :], zu[:, m, :], ACT.Square).then_inc(S["tok_sq"], 1)

            def branch_hi(n, src, base):
                for m in range(QT):
                    act.wait_ge(S["branch_f"], n * QT + m + 1)
                    nc.scalar.activation(mh[:, base + m, :], src[:, m, :], ACT.Identity).then_inc(S["branch_hi"], 1)

            act.wait_ge(S["branch_ms"], 1)
            nc.scalar.activation(rstd2[:, :], ps[:, 2, 0:SEQ], ACT.Sqrt, bias=eps[:, 2:3], scale=2.0).then_inc(S["branch_std"], 1)
            for m in range(QT):
                act.wait_ge(S["ao_done"], m + 1)
                nc.scalar.activation(sq[:, m, :], ao[:, m, :], ACT.Square).then_inc(S["att_sq"], 1)
            branch_hi(0, zu, QT)
            hi(B_OUT2 + AHEAD)
            act.wait_ge(S["branch_ms"], 2)
            nc.scalar.activation(std[:, :], ps[:, 3, 0:SEQ], ACT.Sqrt, bias=eps[:, 2:3], scale=2.0).then_inc(S["branch_std"], 1)
            branch_hi(1, ao, 0)
            for b in range(B_OUT2, B_F2):
                if b > B_OUT2:
                    hi(b + AHEAD)
                if b >= B_OUT2 + 4:
                    for m in range(2 * (b - B_OUT2 - 4), 2 * (b - B_OUT2 - 4) + 2):
                        act.wait_ge(S["out2_ev"], m + 1)
                        nc.scalar.activation(sq[:, m, :], y[:, m, :], ACT.Square).then_inc(NORM["sq"], 1)
            deviation("r2", 4, eps[:, 2:3])
            high_parts("r2", tg_m)

            def taps(j, i, which):
                dst, bank, off = ((ca, 0, 0), (cb, 1, KF2))[which]
                b = B_F2 + (0 if j == 0 else 3 * j - 1) + which
                act.wait_ge(blk_done, i * 12 + (b + 1))
                if j >= 2:
                    act.wait_ge(S["ff2_g"], i * 4 + (j - 1))
                w, bias = (cols[:, bass.ds(i * 4 + (COLS[n][0] + o + off + j), 1)] for n, o in (("conv2_w", 2 * KF2), ("conv2_b", 0)))
                nc.scalar.activation(dst[:, j % 2, :], ps[:, bank, 0:SEQ], ACT.Identity, bias=bias, scale=w)\
                    .then_inc(S["ff2_b" if which else "ff2_a"], 1)

            def silu2(j, i):
                act.wait_ge(S["ff2_ca"], i * 4 + (j + 1))
                nc.scalar.activation(ca[:, j % 2, :], ca[:, j % 2, :], ACT.Silu).then_inc(S["ff2_silu"], 1)

            def high2(j, i):
                act.wait_ge(S["ff2_g"], i * 4 + (j + 1))
                nc.scalar.activation(gh[:, j % 4, :], cg[:, j % 2, :], ACT.Identity).then_inc(S["ff2_hi"], 1)

            def triple(j, i=0):
                b, t = B_F2 + 3 * j - 1, i * 12
                hi(b + AHEAD, t)
                high2(j - 1, i)
                taps(j, i, 0)
                hi(b + 1 + AHEAD, t)
                taps(j, i, 1)
                silu2(j, i)
                hi(b + 2 + AHEAD, t)

            hi(B_F2 + AHEAD)
            taps(0, 0, 0)
            hi(B_F2 + 1 + AHEAD)
            taps(0, 0, 1)
            silu2(0, 0)
            for j in range(1, LOOP2_TRIPLE):
                triple(j)
            with act.Fori(0, (KF2 - LOOP2_TRIPLE) // 4 - 1) as i:
                for q in range(4):
                    triple(LOOP2_TRIPLE + q, i)
            for q in range(KF2 - 4, KF2):
                triple(q)
            high2(KF2 - 1, 0)

            for m in range(KD):
                act.wait_ge(S["f2_res"], m + 1)
                nc.scalar.activation(sq[:, m, :], y[:, m, :], ACT.Square).then_inc(S["fin_sq"], 1)
            act.wait_ge(S["fin_ms"], 1)
            for t in range(NT):
                nc.scalar.activation(std[:, t:t + 1], ps[:, 6 + t, t:t + 1], ACT.Sqrt, bias=eps[:, 2:3]).then_inc(S["fin_std"], 1)
            act.wait_ge(S["fin_rstd"], 1)
            for t in range(NT):
                act.wait_ge(S["fin_turned"], t + 1)
                nc.scalar.activation(ob[:, t, 0:512], ps[:, OUT_BANK[t], :], ACT.Identity, scale=std[:, t:t + 1])\
                    .then_inc(S["fin_by_act"], 1)

        @block.vector
        def _(dve):
            step = Steps(dve, dve_step)
            V = nc.vector

            def lo(b, t=0):
                if isinstance(t, int) and b + t >= NBLK:
                    return
                dve.wait_ge(hi_done, t + (b + 1))
                V.tensor_tensor(wl[:, b % RING], raw[:, b % RING], wh[:, b % RING].bitcast(F32), ALU.subtract).then_inc(lo_dve, 1)

            V.memset(hb[:, 51:52], TWO_PI / 4)
            V.memset(eps[:, 0:1], 16 * LN_EPS)
            V.memset(eps[:, 1:2], LN_EPS)
            V.memset(eps[:, 2:3], RMS_EPS)
            step(V.memset(lnr[:, :, :], 1.0))

            for n, name in ((1, "x_landed"), (2, "x2_landed"), (0, "meta_landed")):
                r = META if n == 0 else P
                dve.wait_ge(S[name], 16)
                for q in range(2):
                    V.bn_stats(lnst[0:r, n, q, :], xt[n][0:r, q * 512:(q + 1) * 512]).then_inc(dve_step, 1)
                step.n += 2
                dve.wait_ge(dve_step, step.n)
                step(V.bn_aggr(lnmv[0:r, n, :], lnst[0:r, n, :, :].rearrange("p a b -> p (a b)")))
                ins = V.tensor_scalar(lnr[0:r, n, 1:2], lnmv[0:r, n, 1:2], LN_EPS, None, ALU.add)
            ins.then_inc(S["ln0_var"], 1)
            dve.wait_ge(S["ln0_std"], 1)
            step(V.reciprocal(lnr[:, :, 0], lnr[:, :, 0]))
            for n in (1, 2, 0):
                r = META if n == 0 else P
                V.tensor_scalar(xt[n][0:r, :], xt[n][0:r, :], lnmv[0:r, n, 0:1], lnr[0:r, n, 0:1], ALU.subtract, ALU.mult)\
                    .then_inc(S["ln0_norm"], 1)

            dve.wait_ge(S["cols_landed"], 16)
            dve.wait_ge(S["dt_done"], 1)
            step(V.tensor_tensor(sv[:, 2], span("lam_im"), sv[:, 0], ALU.mult))
            V.tensor_tensor(sv[:, 1], span("lam_re"), sv[:, 0], ALU.mult).then_inc(S["phase_done"], 1)
            step(V.tensor_scalar(sv[:, 4], sv[:, 2], 1.0 / TWO_PI, ROUND, ALU.mult, ALU.add))
            step(V.tensor_scalar(sv[:, 4], sv[:, 4], ROUND, None, ALU.subtract))
            for part in (PI_A, PI_B, PI_C):
                step(V.scalar_tensor_tensor(sv[:, 2], sv[:, 4], -part, sv[:, 2], ALU.mult, ALU.add))
            step(V.tensor_scalar(sv[:, 5], sv[:, 2], 1.0 / TWO_PI, None, ALU.mult))
            V.scalar_tensor_tensor(sv[:, 17], sv[:, 5], -1.0, sv[:, 5], ALU.mult, ALU.max).then_inc(S["phase_done"], 1)
            V.tensor_scalar(hb[:, 0:24], cols[:, 20:44], 0.5, None, ALU.mult)
            def table_phases(q):
                s = slice(4 * q, 4 * q + 4)
                u, f = tab[:, s, 0, :], tab[:, s, 1, :]
                tmp = swork[:, :, :]
                step(V.tensor_tensor(u, cst[:, None, C_T:C_T + TOK].to_broadcast([P, 4, TOK]),
                                     sv[:, 5, s, None].to_broadcast([P, 4, TOK]), ALU.mult))
                step(V.tensor_scalar(tmp, u, ROUND, ROUND, ALU.add, ALU.subtract))
                step(V.tensor_tensor(f, u, tmp, ALU.subtract))
                V.scalar_tensor_tensor(u, f, -1.0, f, ALU.mult, ALU.max).then_inc(S["phase_done"], 1)
                dve.wait_ge(S["phase_done"], q + 3)

            dve.wait_ge(S["consts_landed"], 16)
            table_phases(0)

            dve.wait_ge(S["half_done"], 1)
            step(V.tensor_scalar(sv[:, 7], sv[:, 3], -1.0, 1.0, ALU.mult, ALU.add))
            step(V.reciprocal(sv[:, 7], sv[:, 7]))
            step(V.scalar_tensor_tensor(sv[:, 8], sv[:, 3], 2.0, sv[:, 7], ALU.mult, ALU.mult))
            step(V.tensor_scalar(sv[:, 9], sv[:, 8], 1.0, None, ALU.add))
            dve.wait_ge(S["half_done"], 4)
            step(V.tensor_tensor(sv[:, 10], sv[:, 6], sv[:, 6], ALU.mult))
            step(V.tensor_tensor(sv[:, 11], sv[:, 8], sv[:, 18], ALU.mult))
            step(V.scalar_tensor_tensor(sv[:, 11], sv[:, 10], -2.0, sv[:, 11], ALU.mult, ALU.add))
            step(V.tensor_tensor(sv[:, 12], sv[:, 9], sv[:, 19], ALU.mult))
            lr, li = span("lam_re"), span("lam_im")
            step(V.tensor_tensor(sv[:, 13], lr, lr, ALU.mult))
            step(V.tensor_tensor(sv[:, 14], li, li, ALU.mult))
            step(V.tensor_tensor(sv[:, 13], sv[:, 13], sv[:, 14], ALU.add))
            step(V.reciprocal(sv[:, 13], sv[:, 13]))
            step(V.tensor_tensor(sv[:, 14], sv[:, 11], lr, ALU.mult))
            step(V.tensor_tensor(sv[:, 15], sv[:, 12], li, ALU.mult))
            step(V.tensor_tensor(sv[:, 14], sv[:, 14], sv[:, 15], ALU.add))
            step(V.tensor_tensor(sv[:, 14], sv[:, 14], sv[:, 13], ALU.mult))
            step(V.tensor_tensor(sv[:, 15], sv[:, 12], lr, ALU.mult))
            step(V.tensor_tensor(sv[:, 16], sv[:, 11], li, ALU.mult))
            step(V.tensor_tensor(sv[:, 15], sv[:, 15], sv[:, 16], ALU.subtract))
            step(V.tensor_tensor(sv[:, 15], sv[:, 15], sv[:, 13], ALU.mult))
            dve.wait_ge(S["s5m_landed"], 16)
            dve.wait_ge(S["cleared"], 1)
            fr, fi = (sv[:, n, :, None].to_broadcast([P, NS5, S5H]) for n in (14, 15))
            w = [sA.rearrange("p a t -> p (a t)")[:, 0:256].rearrange("p (s h) -> p s h", s=NS5),
                 sB.rearrange("p a t -> p (a t)")[:, 0:256].rearrange("p (s h) -> p s h", s=NS5)]
            for z, (x0, x1), op in ((zre, (fr, fi), ALU.subtract), (zim, (fi, fr), ALU.add)):
                step(V.tensor_tensor(w[0], s5m[:, 0], x0, ALU.mult))
                step(V.tensor_tensor(w[1], s5m[:, 1], x1, ALU.mult))
                for g in range(2):
                    ins = V.tensor_tensor(z[64 * g:64 * g + 64, :, S5H * g:S5H * (g + 1)], w[0][64 * g:64 * g + 64],
                                          w[1][64 * g:64 * g + 64], op)
                    if z is zre:
                        step(ins)
                    elif g:
                        ins.then_inc(S["z_done"], 1)
            for c_part, n in ((cbr, 2), (cbi, 3)):
                for g in range(2):
                    ins = V.tensor_copy(c_part[64 * g:64 * g + 64, :, S5H * g:S5H * (g + 1)], s5m[64 * g:64 * g + 64, n])
            ins.then_inc(S["c_done"], 1)
            dve.wait_ge(S["z_done"], 1)
            table_phases(1)
            table_phases(2)
            dve.wait_ge(S["gate_ev"], 2)
            V.scalar_tensor_tensor(rows[:, 2, :], rows[:, 1, :], -1.0, rows[:, 1, :], ALU.mult, ALU.max).then_inc(S["abs_f"], 1)
            step(V.tensor_scalar(rows[:, 1, :], rows[:, 1, :], 0.0, None, ALU.min))
            table_phases(3)

            def gate_rows():
                dve.wait_ge(S["ln_done"], 1)
                step(V.tensor_tensor(rows[:, 1, :], rows[:, 1, :], rows[:, 2, :], ALU.subtract))
                one = cst[0:HEADS, C_ONE_:C_ONE_ + 1].to_broadcast([HEADS, TOK])
                step(V.tensor_tensor_scan(rows[:, 3, :], one, rows[:, 1, :], 0.0, ALU.mult, ALU.add))
                step(V.tensor_tensor(rows[:, 0, :], rows[:, 0, :], rows[:, 3, :], ALU.subtract))
                step(V.tensor_tensor_scan(rows[:, 2, :], rows[:, 0, :], rows[:, 0, :], 0.0, ALU.max, ALU.max))
                step(V.scalar_tensor_tensor(rows[:, 3, :], rows[:, 3, :], -1.0, rows[:, 2, :], ALU.mult, ALU.subtract))
                V.tensor_scalar(rows[:, 2, :], rows[:, 2, :], -1.0, None, ALU.mult).then_inc(S["rows_done"], 1)

            def scan(s):
                dve.wait_ge(S["s5_in"], s + 1)
                dve.wait_ge(S["tables_done"], 2 * (s // 4) + 2)
                bu, cs, sc = ps[:, 2:4, 0:TOK], tab[:, s, 0:2, :], tab[:, s, ::-1, :]
                V.tensor_tensor(sA, bu, cs, ALU.mult).then_inc(dve_step, 1)
                V.tensor_tensor(sB, bu, sc, ALU.mult).then_inc(S["s5_free"], 1)
                step.n += 1
                dve.wait_ge(dve_step, step.n)
                dve.wait_ge(S["s5_free"], s + 1)
                V.tensor_tensor(sA[:, 0, :], sA[:, 0, :], sA[:, 1, :], ALU.add).then_inc(dve_step, 1)
                V.tensor_tensor(sB[:, 0, :], sB[:, 1, :], sB[:, 0, :], ALU.subtract).then_inc(dve_step, 1)
                step.n += 2
                dve.wait_ge(dve_step, step.n)
                r = sv[:, 9, s:s + 1].to_broadcast([P, TOK])
                V.tensor_tensor_scan(zz[:, 0, :], r, sA[:, 0, :], 0.0, ALU.mult, ALU.add).then_inc(dve_step, 1)
                V.tensor_tensor_scan(zz[:, 1, :], r, sB[:, 0, :], 0.0, ALU.mult, ALU.add).then_inc(dve_step, 1)
                step.n += 2
                dve.wait_ge(dve_step, step.n)
                z = zz[:, :, META:TOK]
                sP, sQ = sA[:, :, 0:SEQ], sB[:, :, 0:SEQ]
                V.tensor_tensor(sP, z, cs[:, :, META:TOK], ALU.mult).then_inc(dve_step, 1)
                V.tensor_tensor(sQ, z, sc[:, :, META:TOK], ALU.mult).then_inc(dve_step, 1)
                step.n += 2
                dve.wait_ge(dve_step, step.n)
                if s >= 4:
                    dve.wait_ge(S["s5_y"], s // 4)
                V.tensor_tensor(xst[:, s % 4, 0, :], sP[:, 0, :], sP[:, 1, :], ALU.subtract)
                V.scalar_tensor_tensor(xst[:, s % 4, 1, :], sQ[:, 0, :], -1.0, sQ[:, 1, :], ALU.mult, ALU.subtract)\
                    .then_inc(S["s5_x"], 1)
                dve.wait_ge(S["s5_x"], s + 1)

            def y_sum(c):
                dve.wait_ge(S["s5_y"], c + 1)
                V.scalar_tensor_tensor(y_s(c), y_s(c), col("s5_d", c), ps[:, 4, 0:SEQ], ALU.mult, ALU.add).then_inc(S["y_sum"], 1)

            def conv(t):
                dve.wait_ge(S["qk_ev"], t + 1)
                if t >= 2:
                    dve.wait_ge(S["silu_done"], t - 1)
                a = cv[:, t % 2, :]
                step(V.tensor_scalar(a, qkT[:, t, 3:3 + TOK], col("conv_w", 8 * 3 + t), col("conv_b", t), ALU.mult, ALU.add))
                for w_ in range(2, -1, -1):
                    ins = V.scalar_tensor_tensor(a, qkT[:, t, w_:w_ + TOK], col("conv_w", 8 * w_ + t), a, ALU.mult, ALU.add)
                    if w_:
                        step(ins)
                ins.then_inc(S["conv_done"], 1)

            def weigh(h):
                dve.wait_ge(S["e_done"], h + 1)
                if h:
                    dve.wait_ge(S["num_done"], NT * h)
                sc = DK ** -0.5
                V.scalar_tensor_tensor(pp[:, 0:384], ps[:, 6, 0:384], sc, ee[:, 0:384], ALU.mult, ALU.mult)
                V.scalar_tensor_tensor(pp[0:META, 384:640], ps[0:META, 7, 0:SEQ], sc, ee[0:META, 384:640], ALU.mult, ALU.mult)\
                    .then_inc(S["p_done"], 1)

            def head_stat(h):
                for t in range(NT):
                    dve.wait_ge(S["num_copied"], NT * h + t + 1)
                    step(V.bn_stats(hst[:, :], hraw[:, t, h, 0:DV]))
                    step(V.bn_aggr(hmv[:, t, h, :], hst[:, :]))

            for s in range(NS5):
                scan(s)
                if s == 0:
                    gate_rows()
                if s % 4 == 0 and s:
                    y_sum(s // 4 - 1)
                if s == 3:
                    dve.wait_ge(S["floor_done"], 1)
                    V.tensor_copy(aT[0:META, 0, :], ps[0:META, 6, 0:4])
                    V.tensor_copy(aT[:, 1:3, :].rearrange("p j h -> p (j h)"), ps[:, 6, 4:12]).then_inc(S["a_copied"], 1)
                if s in CONV_AT:
                    conv(CONV_AT.index(s))
                if s in (8, 10, 12, 14):
                    weigh((s - 8) // 2)
                if s in (11, 13, 15):
                    head_stat((s - 11) // 2)

            y_sum(CH - 1)
            head_stat(HEADS - 1)
            dve.wait_ge(S["num_copied"], NT * HEADS)
            den, var = hraw[:, :, :, DV], hmv[:, :, :, 1]
            step(V.scalar_tensor_tensor(hsm[:, 0], den, -1.0, den, ALU.mult, ALU.max))
            dve.wait_ge(S["floor_done"], 1)
            step(V.tensor_tensor(hsm[:, 0], hsm[:, 0], floor[:, :, :], ALU.max))
            step(V.reciprocal(hsm[:, 0], hsm[:, 0]))
            step(V.tensor_tensor(hsm[:, 1], var, hsm[:, 0], ALU.mult))
            step(V.tensor_tensor(hsm[:, 1], hsm[:, 1], hsm[:, 0], ALU.mult))
            V.tensor_scalar(hsm[:, 1], hsm[:, 1], LN_EPS, None, ALU.add).then_inc(S["hvar"], 1)
            dve.wait_ge(S["hstd"], 1)
            step(V.reciprocal(hsm[:, 1], hsm[:, 1]))
            step(V.tensor_tensor(hsm[:, 1], hsm[:, 1], hsm[:, 0], ALU.mult))
            for h in range(HEADS):
                for t in range(NT):
                    V.tensor_scalar(hraw[:, t, h, 0:DV], hraw[:, t, h, 0:DV], hmv[:, t, h, 0:1], hsm[:, 1, t, h:h + 1],
                                    ALU.subtract, ALU.mult).then_inc(S["hnorm"], 1)
            for b in range(B_GLU, B_MOUT):
                if b + AHEAD >= N_POOL:
                    lo(b + AHEAD)
                j = b - B_GLU
                dve.wait_ge(S["glu_t"], j + 1)
                if j == 0:
                    dve.wait_ge(S["gs_ev"], KD)
                V.scalar_tensor_tensor(tw[:, j % 2, :], tz[:, j % 2, :], 1.0, ps[:, b % 2, 0:SEQ], ALU.add, ALU.mult)\
                    .then_inc(S["glu_ev"], 1)
                dve.wait_ge(S["glu_ev"], j + 1)
                step(V.scalar_tensor_tensor(tg_s[:, j, :], tg_s[:, j, :], 1.0, tw[:, j % 2, :], ALU.add, ALU.mult))
                dve.wait_ge(S["h_turned"], j + 1)
                dve.wait_ge(S["o_ev"], j + 1)
                V.scalar_tensor_tensor(tg_o[:, j, :], tg_o[:, j, :], 1.0, ps[:, 5 + j % 2, 0:SEQ], ALU.add, ALU.mult)\
                    .then_inc(S["h_gated"], 1)
            for b in range(B_MOUT, B_WO):
                lo(b + AHEAD)
                m = b - B_MOUT
                dve.wait_ge(blk_done, b + 1)
                if m == 0:
                    dve.wait_ge(S["gm_ev"], KD)
                step(V.scalar_tensor_tensor(tw[:, m % 2, :], tg_m[:, m, :], 1.0, ps[:, b % 2, 0:SEQ], ALU.add, ALU.mult))
                V.tensor_tensor(tg_s[:, m, :], tg_s[:, m, :], tw[:, m % 2, :], ALU.add).then_inc(S["mout_ev"], 1)
            for b in range(B_WO, B_F1):
                lo(b + AHEAD)
                m = b - B_WO
                dve.wait_ge(blk_done, b + 1)
                V.scalar_tensor_tensor(res[:, m, META:TOK], res[:, m, META:TOK], 4 * ALPHA, ps[:, b % 2, 0:SEQ],
                                       ALU.mult, ALU.add).then_inc(S["wo_ev"], 1)

            y = res[:, :, META:TOK]

            def centre(tag):
                dve.wait_ge(*norm(tag, "mean"))
                for g in range(4):
                    V.tensor_tensor(y[:, 2 * g:2 * g + 2, :], y[:, 2 * g:2 * g + 2, :],
                                    ps[:, 6:7, 0:SEQ].to_broadcast([P, 2, SEQ]), ALU.subtract).then_inc(NORM["d"], 1)

            def scaled(tag, dst, g_of, b_of):
                dve.wait_ge(*norm(tag, "std"))
                step(V.reciprocal(rstd[:, :], std[:, :]))
                for m in range(0, KD, 2):
                    step(V.tensor_tensor(dst[:, m:m + 2, :], y[:, m:m + 2, :], rstd[:, None, :].to_broadcast([P, 2, SEQ]), ALU.mult))
                    for n in (m, m + 1):
                        V.tensor_scalar(dst[:, n, :], dst[:, n, :], g_of(n), b_of(n), ALU.mult, ALU.add).then_inc(NORM["h"], 1)

            centre("n1")
            for g in range(4):
                dve.wait_ge(*norm("n1", "sq", g + 1))
                V.tensor_tensor(sq[:, 2 * g, :], sq[:, 2 * g, :], sq[:, 2 * g + 1, :], ALU.add).then_inc(S["n1_pair"], 1)
            scaled("n1", y, lambda m: col("ln1_g", m), lambda m: col("ln1_b", m))

            def ada(n, acc_, t=0):
                k, acc = n % KD, ada_acc[:, acc_, :]
                dve.wait_ge(ada_landed[n % ADA_RING], t * (16 // ADA_RING) + 16 * (n // ADA_RING + 1))
                if k:
                    dve.wait_ge(S["ada_used"], t + n)
                w = ada_w[:, n % ADA_RING]
                if k == 0:
                    ins = V.tensor_scalar(acc, w, sc[:, 0:1], None, ALU.mult)
                else:
                    ins = V.scalar_tensor_tensor(acc, w, sc[:, k:k + 1], acc, ALU.mult, ALU.add)
                ins.then_inc(S["ada_used"], 1)

            def mod_out(p_, nth, i=0, bank=7):
                dve.wait_ge(S["mod_mm"], i + nth)
                V.tensor_tensor(mod[:, bass.ds(i * KD + p_ * KD, KD)], ps[:, bank, 0:KD],
                                cols[:, bass.ds(i * KD + (COLS["b_ada"][0] + p_ * KD), KD)], ALU.add).then_inc(S["mod_done"], 1)

            lo(B_F1 + AHEAD)
            dve.wait_ge(S["silu_c"], 1)
            for j in range(1, LOOP1_PAIR):
                lo(B_F1 - 1 + 2 * j + AHEAD)
                lo(B_F1 + 2 * j + AHEAD)
                ada(j - 1, 1)
            ada(KD - 1, 1)
            with dve.Fori(0, ADA_LOOP) as i:
                n = KD
                for q in range(8):
                    b = B_F1 - 1 + 2 * (LOOP1_PAIR + q)
                    lo(b + AHEAD, i * 16)
                    lo(b + 1 + AHEAD, i * 16)
                    for _ in range(ADA_SHARE[q]):
                        ada(n, 0, i * 8)
                        n += 1
                mod_out(1, 1, i)
            lo(B_F1 + 2 * KF - 1 + AHEAD)
            mod_out(0, ADA_LOOP + 1, bank=6)
            dve.wait_ge(S["mod_done"], ADA_LOOP + 1)
            step(V.scalar_tensor_tensor(gain[:, 0, :], mod[:, M_SC1:M_SC1 + KD], 1.0, span("g_norm1"), ALU.add, ALU.mult))

            dve.wait_ge(blk_done, B_IN2)
            for g in range(4):
                V.scalar_tensor_tensor(y[:, 2 * g:2 * g + 2, :], y[:, 2 * g:2 * g + 2, :], ALPHA,
                                       ps[:, 2 + g, :].rearrange("p (a t) -> p a t", a=2), ALU.mult, ALU.add)\
                    .then_inc(S["f1_res"], 1)
            dve.wait_ge(S["f1_res"], 4)
            centre("n2")
            scaled("n2", y, lambda m: col("ln2_g", m), lambda m: col("ln2_b", m))
            dve.wait_ge(*norm("n2", "h", KD))
            scaled("r1", tg_m, lambda m: gain[:, 0, m:m + 1], lambda m: mod[:, M_SH1 + m:M_SH1 + m + 1])

            reads = [0]

            def bank3_read(last):
                last.then_inc(S["b3_free"], 1)
                reads[0] += 1

            def q_finish(t):
                dst = qf[:, t - 1, :] if t else kf[:, 0, :]
                dve.wait_ge(S["b3_full"], reads[0] + 1)
                if t == 0:
                    dve.wait_ge(S["mixing_landed"], 64)
                bank3_read(V.tensor_tensor(qrot[:, :], ps[:, 3, 0:SEQ], rope[:, 1, :], ALU.mult))
                step(V.tensor_tensor(dst, qg[:, t % 3, :], rope[:, 0, :], ALU.mult))
                dve.wait_ge(S["b3_free"], reads[0])
                step(V.tensor_tensor(dst, dst, qrot[:, :], ALU.add))
                dve.wait_ge(S["q_std"], t + 1)
                step(V.reciprocal(qstd[:, t % 2, :], qstd[:, t % 2, :]))
                V.tensor_tensor(dst, dst, qstd[:, t % 2, :], ALU.mult).then_inc(S["qk_ready"], 1)

            def maxima(h):
                dve.wait_ge(S["s_done"], h + 1)
                step(V.tensor_reduce(smax[:, h, 0, :], ps[:, 6 + h % 2, :].rearrange("p (t s) -> p t s", t=NT), AX.X, ALU.max))
                V.tensor_scalar(smax[:, h, 1, :], smax[:, h, 0, :], -HD ** -0.5, None, ALU.mult).then_inc(S["max_done"], 1)

            def normed(h):
                dve.wait_ge(S["exp_done"], h + 1)
                step(V.reciprocal(ssum[:, h, :], ssum[:, h, :]))
                for t in range(NT):
                    ins = V.tensor_scalar(prob[:, h % 2, t, :], prob[:, h % 2, t, :], ssum[:, h, t:t + 1], None, ALU.mult)
                ins.then_inc(S["prob_done"], 1)

            def attended(m):
                dve.wait_ge(S["o_done"], 2 * m + 2)
                V.tensor_copy(ao[:, m, :], ps[:, 3, 0:SEQ]).then_inc(S["ao_done"], 1)

            def other_rows(slot):
                for n in ada_rows(slot):
                    ada(n, 1)

            for n in range(B_OUT2 - B_IN2):
                if n == 2:
                    dve.wait_ge(S["b3_full"], reads[0] + 1)
                    bank3_read(V.tensor_copy(vtok[:, :, :].rearrange("p s e -> p (s e)"), ps[:, 3, 0:SEQ]))
                if n == 6:
                    dve.wait_ge(S["b3_full"], reads[0] + 1)
                    bank3_read(V.tensor_copy(kf[:, 1, :], ps[:, 3, 0:SEQ]))
                if n >= 7:
                    normed(n - 7)
                if n >= 6:
                    maxima(n - 6)
                if 3 <= n < 8:
                    q_finish(n - 3)
                if n in (10, 12):
                    attended((n - 10) // 2)
                if n in (11, 12):
                    c = n - 11
                    dve.wait_ge(S["zv_sq"], c + 1)
                    V.tensor_reduce(zms[:, c, :], sq[:, 2 * c:2 * c + 2, :].rearrange("p a (h e) -> p (a h) e", e=HD), AX.X, ALU.add)\
                        .then_inc(S["zv_ms"], 1)
                other_rows(n)
            normed(AH - 1)
            attended(2)
            dve.wait_ge(S["zv_std"], 1)
            step(V.reciprocal(zms[:, :, :], zms[:, :, :]))
            for c in range(NT):
                dve.wait_ge(S["zv_copied"], c + 1)
                z = zvt[:, c, :].rearrange("p (h e) -> p h e", e=HD)
                V.tensor_tensor(z, z, zms[:, c, :, None].to_broadcast([P, AH, HD]), ALU.mult).then_inc(S["zv_n"], 1)
            dve.wait_ge(S["mixing_landed"], 64)
            for m in range(QT):
                dve.wait_ge(S["mixed"], m + 1)
                V.scalar_tensor_tensor(zv[:, m, :].rearrange("p (c t) -> p c t", c=NT),
                                       ps[:, MIX_BANK[m], 0:SEQ].rearrange("p (c t) -> p c t", c=NT), col("g_tok_v"),
                                       bs[:, m:m + 1, :].to_broadcast([P, NT, P]), ALU.mult, ALU.add).then_inc(S["tok_pre"], 1)
                dve.wait_ge(S["tok_pre"], m + 1)
                dve.wait_ge(S["zu_act"], 1)
                V.tensor_tensor(zu[:, m, :], zu[:, m, :], zv[:, m, :], ALU.mult).then_inc(S["tok_done"], 1)
            attended(3)
            for n, (src, g_name, dev) in enumerate(((zu, "g_tok", rstd2), (ao, "g_attn", std))):
                dve.wait_ge(S["branch_std"], n + 1)
                step(V.reciprocal(dev[:, :], dev[:, :]))
                for m in range(QT):
                    V.scalar_tensor_tensor(src[:, m, :], src[:, m, :], col(g_name, m), dev[:, :], ALU.mult, ALU.mult)\
                        .then_inc(S["branch_f"], 1)

            for b in range(B_OUT2, B_F2):
                if B_F2 <= b + AHEAD and b < B_OUT2 + 4:
                    lo(b + AHEAD)
                other_rows(b - B_IN2)
                if b >= B_OUT2 + 4:
                    pair_ = b - B_OUT2 - 4
                    dve.wait_ge(blk_done, b + 1)
                    for m in (2 * pair_, 2 * pair_ + 1):
                        V.scalar_tensor_tensor(y[:, m, :], ps[:, (0, 1, 6, 7)[pair_], (m % 2) * SEQ:(m % 2 + 1) * SEQ],
                                               mod[:, M_GT1 + m:M_GT1 + m + 1], y[:, m, :], ALU.mult, ALU.add)\
                            .then_inc(S["out2_ev"], 1)
                    if b + AHEAD >= B_F2:
                        lo(b + AHEAD)
            mod_out(NMOD - 2, NMOD - 1, bank=5)
            dve.wait_ge(S["mod_done"], NMOD - 1)
            step(V.scalar_tensor_tensor(gain[:, 1, :], mod[:, M_SC2:M_SC2 + KD], 1.0, span("g_norm2"), ALU.add, ALU.mult))
            dve.wait_ge(S["out2_ev"], KD)
            scaled("r2", tg_m, lambda m: gain[:, 1, m:m + 1], lambda m: mod[:, M_SH2 + m:M_SH2 + m + 1])

            def outer_taps(j, i, which):
                dst, bank, off = ((ca, 0, 0), (cb, 1, KF2))[which]
                done = S["ff2_cb" if which else "ff2_ca"]
                dve.wait_ge(S["ff2_b" if which else "ff2_a"], i * 4 + (j + 1))
                w0, w2 = (cols[:, bass.ds(i * 4 + (COLS["conv2_w"][0] + o * 2 * KF2 + off + j), 1)] for o in (0, 2))
                step(V.scalar_tensor_tensor(dst[:, j % 2, 1:SEQ], ps[:, bank, 0:SEQ - 1], w0, dst[:, j % 2, 1:SEQ], ALU.mult, ALU.add))
                V.scalar_tensor_tensor(dst[:, j % 2, 0:SEQ - 1], ps[:, bank, 1:SEQ], w2, dst[:, j % 2, 0:SEQ - 1], ALU.mult, ALU.add)\
                    .then_inc(done, 1)

            def triple(j, i=0):
                b, t = B_F2 + 3 * j - 1, i * 12
                lo(b + AHEAD, t)
                outer_taps(j, i, 0)
                lo(b + 1 + AHEAD, t)
                outer_taps(j, i, 1)
                lo(b + 2 + AHEAD, t)

            lo(B_F2 + AHEAD)
            outer_taps(0, 0, 0)
            lo(B_F2 + 1 + AHEAD)
            outer_taps(0, 0, 1)
            for j in range(1, LOOP2_TRIPLE):
                triple(j)
                if j >= 2:
                    for n in range(2):
                        ada((NMOD - 1) * KD + 2 * (j - 2) + n, 2)
            with dve.Fori(0, (KF2 - LOOP2_TRIPLE) // 4 - 1) as i:
                step.enter(i, 8)
                for q in range(4):
                    triple(LOOP2_TRIPLE + q, i)
            step.leave((KF2 - LOOP2_TRIPLE) // 4 - 1)
            for j in range(KF2 - 4, KF2):
                triple(j)
            mod_out(NMOD - 1, NMOD)

            dve.wait_ge(blk_done, NBLK)
            dve.wait_ge(S["mod_done"], NMOD)
            for m in range(KD):
                V.scalar_tensor_tensor(y[:, m, :], ps[:, 2 + m // 2, (m % 2) * SEQ:(m % 2 + 1) * SEQ],
                                       mod[:, M_GT2 + m:M_GT2 + m + 1], y[:, m, :], ALU.mult, ALU.add).then_inc(S["f2_res"], 1)
            for m in range(KD):
                dve.wait_ge(S["f2_res"], m + 1)
                V.tensor_scalar(tg_m[:, m, :], y[:, m, :], col("g_final", m), None, ALU.mult).then_inc(S["fin_f"], 1)
            dve.wait_ge(S["fin_std"], NT)
            V.reciprocal(std[:, 0:NT], std[:, 0:NT]).then_inc(S["fin_rstd"], 1)
            dve.wait_ge(S["fin_rstd"], 1)
            for t in range(NT):
                dve.wait_ge(S["fin_turned"], NT + t + 1)
                V.tensor_scalar(ob[:, t, 512:D], ps[:, OUT_BANK[NT + t], :], std[:, t:t + 1], None, ALU.mult)\
                    .then_inc(S["fin_by_dve"], 1)

        @block.gpsimd
        def _(pool):
            G = nc.gpsimd
            for n, z in enumerate((zre, zim, cbr, cbi)):
                ins = G.memset(z[:, :, :], 0.0)
            ins.then_inc(S["cleared"], 1)
            G.memset(qkT[:, :, 0:3], 0.0).then_inc(S["cleared"], 1)

            def lo(b):
                pool.wait_ge(hi_done, b + 1)
                G.tensor_tensor(wl[:, b % RING], raw[:, b % RING], wh[:, b % RING].bitcast(F32), ALU.subtract).then_inc(lo_pool, 1)

            def hm_lo(m):
                pool.wait_ge(S["hm_f"], m + 1)
                G.tensor_tensor(xl[:, m, META:TOK], tg_o[:, m, :], xh[:, m, META:TOK].bitcast(F32), ALU.subtract)\
                    .then_inc(S["hm_lo"], 1)

            lo(0)
            lo(1)
            for k in range(KD):
                pool.wait_ge(S["ln0_h"], k + 1)
                pool.wait_ge(S["ln0_hi"], k + 1)
                G.tensor_tensor(xl[:, k, :], res[:, k, :], xh[:, k, :].bitcast(F32), ALU.subtract).then_inc(S["ln0_lo"], 1)
            for b in range(2, N_POOL):
                lo(b)
                if b == 8:
                    pool.wait_ge(S["ln0_hi"], KD)
                    pool.wait_ge(S["ln0_turned"], KD)
                    G.memset(vtk[:, :, :, DV:DV + 1], 1.0).then_inc(pool_step, 1)
                if b in (41, 44):
                    for c in (range(CH - 1) if b == 41 else range(CH - 1, CH)):
                        pool.wait_ge(S["y_hi"], c + 1)
                        pool.wait_ge(S["y_act"], c + 1)
                        G.tensor_tensor(gl[:, c, :], y_s(c), gh[:, c, :].bitcast(F32), ALU.subtract).then_inc(S["y_lo"], 1)
                if b > 47:
                    hm_lo(b - 48)
            for m in range(N_POOL - 48, KD):
                hm_lo(m)
            for m in range(KD):
                pool.wait_ge(S["mix_hi"], m + 1)
                pool.wait_ge(S["mout_ev"], m + 1)
                G.tensor_tensor(ml[:, m, :], tg_s[:, m, :], mh[:, m, :].bitcast(F32), ALU.subtract).then_inc(S["mix_lo"], 1)

            def low_parts(tag, src):
                for g, (a, z) in enumerate(GROUPS):
                    s = slice(a, z)
                    pool.wait_ge(*norm(tag, "hi", g + 1))
                    G.tensor_tensor(xl[:, s, META:TOK], src[:, s, :], xh[:, s, META:TOK].bitcast(F32), ALU.subtract)\
                        .then_inc(NORM["lo"], 1)

            y = res[:, :, META:TOK]
            low_parts("n1", y)

            def square_low(j, i=0):
                pool.wait_ge(S["f_relu"], i * 8 + (j + 1))
                G.tensor_tensor(relu2[:, j % 2, :], relu[:, j % 2, :], relu[:, j % 2, :], ALU.mult).then_inc(pool_step, 1)
                pool.wait_ge(pool_step, i * 8 + (j + 2))
                pool.wait_ge(S["f_hi"], i * 8 + (j + 1))
                G.tensor_tensor(gl[:, j % 4, :], relu2[:, j % 2, :], gh[:, j % 4, :].bitcast(F32), ALU.subtract).then_inc(S["f_lo"], 1)

            for j in range(LOOP1_PAIR):
                square_low(j)
            with pool.Fori(0, 3) as i:
                for q in range(8):
                    square_low(LOOP1_PAIR + q, i)
            low_parts("r1", tg_m)
            for b in range(POOL2[0], B_OUT2 + AHEAD):
                lo(b)

            def branch_lo(n, src, base):
                for m in range(QT):
                    pool.wait_ge(S["branch_hi"], n * QT + m + 1)
                    G.tensor_tensor(ml[:, base + m, :], src[:, m, :], mh[:, base + m, :].bitcast(F32), ALU.subtract)\
                        .then_inc(S["branch_lo"], 1)

            branch_lo(0, zu, QT)
            lo(B_OUT2 + AHEAD)
            branch_lo(1, ao, 0)
            for b in range(B_OUT2 + AHEAD + 1, POOL2[1]):
                lo(b)
            low_parts("r2", tg_m)

            def gated(j, i=0):
                pool.wait_ge(S["ff2_silu"], i * 4 + (j + 1))
                pool.wait_ge(S["ff2_cb"], i * 4 + (j + 1))
                G.tensor_tensor(cg[:, j % 2, :], ca[:, j % 2, :], cb[:, j % 2, :], ALU.mult).then_inc(S["ff2_g"], 1)

            def gated_low(j, i=0):
                pool.wait_ge(S["ff2_hi"], i * 4 + (j + 1))
                G.tensor_tensor(gl[:, j % 4, :], cg[:, j % 2, :], gh[:, j % 4, :].bitcast(F32), ALU.subtract).then_inc(S["ff2_lo"], 1)

            for j in range(LOOP2_TRIPLE):
                gated(j)
                gated_low(j)
            with pool.Fori(0, (KF2 - LOOP2_TRIPLE) // 4) as i:
                for q in range(4):
                    gated(LOOP2_TRIPLE + q, i)
                    gated_low(LOOP2_TRIPLE + q, i)


def _tiles(w):
    k, n = w.shape
    return w.reshape(k // P, P, n // P, P).transpose(2, 1, 0, 3).reshape(n // P, P, k)


def _cols(v):
    return v.reshape(-1, P).T


def kernel(**inputs):
    import numpy as np
    import concourse.bacc as bacc
    from concourse.bass_utils import run_bass_kernel_spmd

    I = {k: np.asarray(v) for k, v in inputs.items()}
    f = np.float32

    w_in = I["w_in"][0]
    gates_at = S5W + 2 * HEADS * DK + 2 * HEADS * DV
    o_at = S5W + 2 * HEADS * DK + HEADS * DV
    w1, w2 = I["w_in_2"][0], I["w_up_2"][0]
    glu = _tiles(I["s5_w_glu"][0])
    up, down = _tiles(I["w_up"][0]), I["w_down"][0].reshape(KF, P, D)
    up2, down2 = _tiles(w2), I["w_down_2"][0].reshape(KF2, P, D)
    t2 = _tiles(w1)
    o2, half = _tiles(I["w_out_2"][0]), D // 2
    ffn1 = np.concatenate([up[:1], np.stack([up[1:], down[:-1]], 1).reshape(-1, P, D), down[-1:]])
    ffn2 = np.concatenate([up2[:1], up2[KF2:KF2 + 1],
                           np.stack([up2[1:KF2], up2[KF2 + 1:], down2[:-1]], 1).reshape(-1, P, D), down2[-1:]])
    stream = np.concatenate([
        _tiles(w_in[:, :o_at]),
        _tiles(w_in[:, gates_at + 8:gates_at + 8 + D]),
        _tiles(w_in[:, o_at:gates_at]),
        _tiles(w_in[:, gates_at + 8 + D:]),
        np.concatenate([glu[:KD], glu[KD:]], 2),
        _tiles(I["m_w_out"][0]), _tiles(I["w_o"][0]), ffn1,
        t2[5:6], t2[4:5], t2[0:4], t2[10:14], t2[6:10],
        np.concatenate([o2[0::2, :, half:], o2[1::2, :, half:]], 2), np.concatenate([o2[0::2, :, :half], o2[1::2, :, :half]], 2),
        ffn2])
    assert stream.shape == (NBLK, P, D)

    b_in = I["b_in"][0]
    b_main = np.concatenate([b_in[:o_at], b_in[gates_at + 8:gates_at + 8 + D], b_in[o_at:gates_at], b_in[gates_at + 8 + D:]])

    def states(v):
        return v.reshape((NS5, P) + v.shape[2:]).swapaxes(0, 1)

    twice = lambda v: np.concatenate([v, v])[:, None]
    vectors = {
        "b_in": _cols(b_main),
        "conv_w": np.concatenate([_cols(I["qk_conv_w"][0, n]) for n in range(4)], 1),
        "conv_b": _cols(I["qk_conv_b"][0]), "s5_d": _cols(I["s5_d"][0]),
        "ln0_g": _cols(I["ln0_g"]), "ln0_b": _cols(I["ln0_b"]),
        "ln1_g": _cols(I["ln1_g"][0]), "ln1_b": _cols(I["ln1_b"][0]), "b_up": _cols(I["b_up"][0]),
        "ln2_g": _cols(I["ln2_g"][0]), "ln2_b": _cols(I["ln2_b"][0]), "m_norm_g": _cols(I["m_norm_g"][0]),
        "lam_re": states(I["s5_lambda_re"][0]), "lam_im": states(I["s5_lambda_im"][0]),
        "log_dt": states(np.repeat(I["s5_log_dt"][0][:, None], S5P, 1)),
        "b_ada": _cols(I["b_ada_2"][0]), "g_norm1": _cols(I["g_norm1_2"][0]),
        "g_q": twice(I["g_q_2"][0]), "g_k": twice(I["g_k_2"][0]), "g_tok_v": twice(I["g_tok_v_2"][0]),
        "g_attn": _cols(I["g_attn_out_2"][0]), "g_tok": _cols(I["g_tok_out_2"][0]), "g_norm2": _cols(I["g_norm2_2"][0]),
        "conv2_w": np.concatenate([_cols(I["w_conv_2"][0, n]) for n in range(3)], 1),
        "conv2_b": _cols(I["b_conv_2"][0]), "g_final": _cols(I["g_final_2"]), "c": _cols(I["c_2"][0]),
    }
    cols = np.concatenate([vectors[n] for n in COLS], 1)
    s5_mats = np.stack([states(I["s5_b_re"][0]), states(I["s5_b_im"][0]),
                        states(I["s5_c_re"][0].transpose(0, 2, 1)), states(I["s5_c_im"][0].transpose(0, 2, 1))], 1)

    consts = np.zeros((P, NCONST), f)
    consts[:, C_ID:C_ID + P] = np.eye(P)
    consts[:, C_ONE:C_ONE + P] = 1.0 / D
    for g in range(2):
        consts[64 * g:64 * g + 64, C_BLK + 64 * g:C_BLK + 64 * g + 64] = 1.0 / HD
    for o in range(P):
        a = o % 32
        src, sign = (o + 16, -1.0) if a < 16 else (o - 16, 1.0)
        consts[src, C_ROT + o] = sign
        consts[(o + 64) % P, C_SWAP + o] = 1.0
    consts[:, C_MASK:C_MASK + P] = np.where(np.arange(P)[:, None] <= np.arange(P)[None, :], 0.0, -1e30)
    consts[:, C_T:C_T + TOK] = np.arange(TOK)
    consts[:, C_ONE_] = 1.0
    sel = np.zeros((HEADS, HEADS, P), f)
    for h in range(HEADS):
        sel[h, h] = 1.0
    n = np.arange(SEQ)
    inv = np.power(f(10000.0), -np.arange(0, 32, 2, dtype=f) / f(32)).astype(f)
    ar, ac = ((n // 64).astype(f)[:, None] * inv, (n % 64).astype(f)[:, None] * inv)
    ang = np.concatenate([ar, ar, ac, ac], 1).T
    rope = np.stack([np.concatenate([np.cos(ang)] * 2), np.concatenate([np.sin(ang)] * 2)], 1).astype(f)

    arrays = {
        "x": I["x"], "meta_tokens": I["meta_tokens"], "w_stream": stream, "cols": cols, "consts": consts,
        "s5_mats": s5_mats, "sel": sel, "rope": rope,
        "w_gates": w_in[:, gates_at:gates_at + 8].reshape(KD, P, 8).transpose(1, 0, 2),
        "b_gates": b_in[gates_at:gates_at + 8].reshape(2, HEADS).T,
        "w_ada": I["w_ada_2"][0].reshape(KD, P, NMOD, D).transpose(2, 0, 1, 3).reshape(NMOD * KD, P, D),
        "w_s": I["w_s_2"][0].transpose(1, 0, 2),
        "b_s": I["b_s_2"][0],
    }
    arrays = {k: np.ascontiguousarray(v) for k, v in arrays.items()}
    nc = bacc.Bacc("TRN2", target_bir_lowering=False, num_devices=1)
    A = {k: nc.dram_tensor(f"in_{k}", v.shape, mybir.dt.from_np(v.dtype), kind="ExternalInput").ap() for k, v in arrays.items()}
    out = nc.dram_tensor("out_0", (1, SEQ, D), F32, kind="ExternalOutput").ap()
    two_blocks(nc, A, out)
    r = run_bass_kernel_spmd(nc, [{f"in_{k}": v for k, v in arrays.items()}], core_ids=[0])
    return r.results[0]["out_0"]
```
